# Optimizing a Trainium2 kernel written in Bass

```python
import jax, jax.numpy as jnp
from jax import lax
import numpy as np
import math

D_MODEL = 1024
BATCH = 1
SEQ = 256
DEPTH = 2

N_EVEN = (DEPTH + 1) // 2
N_ODD = DEPTH // 2
D_FF = 2816
RMS_EPS = 1e-6
ROPE_THETA = 10000.0

GLA_HEADS = 4
GLA_DK = 64
GLA_DV = 128
GLA_GATE_RANK = 16
GLA_GATE_TAU = 16.0
GLA_CHUNK = 64

POOL_WINDOWS = (2, 4, 8, 16)
POOL_GROUPS = 4
POOL_GROUP_DIM = 128
POOL_DIM = POOL_GROUPS * POOL_GROUP_DIM

ATT_HEADS = 8
ATT_KV_HEADS = 2
ATT_HEAD_DIM = 128
IDX_HEADS = 4
IDX_DIM = 64
TOPK_MAX = 256
Q_BLOCK = 128

EVEN_SIZES = (GLA_HEADS * GLA_DK, GLA_HEADS * GLA_DK, GLA_HEADS * GLA_DV, GLA_HEADS * GLA_DV, GLA_GATE_RANK, POOL_DIM)
EVEN_IN = sum(EVEN_SIZES)
EVEN_SPLITS = tuple(int(s) for s in np.cumsum(EVEN_SIZES)[:-1])
EVEN_MIX = GLA_HEADS * GLA_DV + POOL_DIM
ODD_SIZES = (ATT_HEADS * ATT_HEAD_DIM, ATT_KV_HEADS * ATT_HEAD_DIM, ATT_KV_HEADS * ATT_HEAD_DIM, IDX_HEADS * IDX_DIM, IDX_DIM, IDX_HEADS)
ODD_IN = sum(ODD_SIZES)
ODD_SPLITS = tuple(int(s) for s in np.cumsum(ODD_SIZES)[:-1])
ODD_MIX = ATT_HEADS * ATT_HEAD_DIM


def rms_norm(x, g):
    xf = x.astype(jnp.float32)
    y = xf * lax.rsqrt(jnp.mean(xf * xf, axis=-1, keepdims=True) + RMS_EPS)
    return (y * g.astype(jnp.float32)).astype(x.dtype)

def swiglu(x, wi, wo):
    gate, up = jnp.split(x @ wi, 2, axis=-1)
    return (jax.nn.silu(gate) * up) @ wo

def rope(x, positions):
    d = x.shape[-1]
    inv = ROPE_THETA ** (-jnp.arange(0, d, 2, dtype=jnp.float32) / d)
    ang = positions.astype(jnp.float32)[..., None] * inv
    cos = jnp.cos(ang)[:, :, None, :]
    sin = jnp.sin(ang)[:, :, None, :]
    xf = x.astype(jnp.float32)
    x1, x2 = jnp.split(xf, 2, axis=-1)
    out = jnp.concatenate([x1 * cos - x2 * sin, x2 * cos + x1 * sin], axis=-1)
    return out.astype(x.dtype)

def gla_chunked(q, k, v, log_a):
    B, S, H, DK = q.shape
    DV = v.shape[-1]
    C = GLA_CHUNK
    n = S // C

    def to_chunks(t):
        return t.astype(jnp.float32).reshape(B, n, C, H, t.shape[-1]).transpose(1, 0, 3, 2, 4)

    qc = to_chunks(q.astype(jnp.float32) * (DK ** -0.5))
    kc, vc, ac = to_chunks(k), to_chunks(v), to_chunks(log_a)
    causal = jnp.tril(jnp.ones((C, C), dtype=bool))[:, :, None]

    def step(state, inp):
        qb, kb, vb, ab = inp
        b = jnp.cumsum(ab, axis=2)
        inter = jnp.einsum('bhcd,bhde->bhce', qb * jnp.exp(b), state)
        rel = jnp.where(causal, b[:, :, :, None, :] - b[:, :, None, :, :], -jnp.inf)
        scores = jnp.einsum('bhid,bhjd,bhijd->bhij', qb, kb, jnp.exp(rel))
        intra = jnp.einsum('bhij,bhje->bhie', scores, vb)
        b_last = b[:, :, -1, :]
        k_dec = kb * jnp.exp(b_last[:, :, None, :] - b)
        state = jnp.exp(b_last)[..., None] * state + jnp.einsum('bhcd,bhce->bhde', k_dec, vb)
        return state, inter + intra

    s0 = jnp.zeros((B, H, DK, DV), jnp.float32)
    _, out = lax.scan(step, s0, (qc, kc, vc, ac))
    return out.transpose(1, 0, 3, 2, 4).reshape(B, S, H, DV)

def multiscale_pool(u):
    B, S, _ = u.shape
    ug = u.astype(jnp.float32).reshape(B, S, POOL_GROUPS, POOL_GROUP_DIM)
    csum = jnp.cumsum(ug, axis=1)
    t = jnp.arange(1, S + 1, dtype=jnp.float32)
    outs = []
    for g, w in enumerate(POOL_WINDOWS):
        c = csum[:, :, g]
        c_prev = jnp.pad(c, ((0, 0), (w, 0), (0, 0)))[:, :S]
        count = jnp.minimum(t, float(w))[None, :, None]
        outs.append((c - c_prev) / count - ug[:, :, g])
    return jnp.stack(outs, axis=2)

def gla_pool_mixer(hn, w_in, gate_w, gate_b, out_norm, pool_w, pool_scale, w_out):
    B, S, _ = hn.shape
    proj = hn @ w_in
    q, k, v, g, a_lr, u = jnp.split(proj, EVEN_SPLITS, axis=-1)
    log_a = jax.nn.log_sigmoid((a_lr @ gate_w + gate_b).astype(jnp.float32)) / GLA_GATE_TAU
    o = gla_chunked(q.reshape(B, S, GLA_HEADS, GLA_DK), k.reshape(B, S, GLA_HEADS, GLA_DK),
                    v.reshape(B, S, GLA_HEADS, GLA_DV), log_a.reshape(B, S, GLA_HEADS, GLA_DK))
    o = rms_norm(o, out_norm.reshape(GLA_HEADS, GLA_DV)).reshape(B, S, GLA_HEADS * GLA_DV)
    o = (o * jax.nn.silu(g.astype(jnp.float32))).astype(hn.dtype)
    p = multiscale_pool(u)
    p = jnp.einsum('bsgc,gcd->bsgd', p, pool_w.astype(jnp.float32)).reshape(B, S, POOL_DIM)
    p = (p * pool_scale.astype(jnp.float32)).astype(hn.dtype)
    return jnp.concatenate([o, p], axis=-1) @ w_out

def dsa_attention(q, k, v, qi, ki, wi):
    B, S, H, Dh = q.shape
    G = k.shape[2]
    R = H // G
    top_k = min(TOPK_MAX, S // 4)
    n_blocks = S // Q_BLOCK
    idx_scale = (IDX_DIM ** -0.5) * (IDX_HEADS ** -0.5)
    key_pos = jnp.arange(S)
    ki_f = ki.astype(jnp.float32)

    def block(i):
        start = i * Q_BLOCK
        qb = lax.dynamic_slice_in_dim(q, start, Q_BLOCK, axis=1).reshape(B, Q_BLOCK, G, R, Dh)
        qib = lax.dynamic_slice_in_dim(qi, start, Q_BLOCK, axis=1).astype(jnp.float32)
        wib = lax.dynamic_slice_in_dim(wi, start, Q_BLOCK, axis=1).astype(jnp.float32)
        q_pos = start + jnp.arange(Q_BLOCK)
        logits = jax.nn.relu(jnp.einsum('bthd,bsd->bths', qib, ki_f))
        iscore = jnp.einsum('bth,bths->bts', wib, logits) * idx_scale
        admissible = key_pos[None, :] <= q_pos[:, None]
        iscore = jnp.where(admissible[None], iscore, -jnp.inf)
        _, sel = lax.top_k(iscore, top_k)
        valid = sel <= q_pos[None, :, None]
        k_sel = jax.vmap(lambda a, ix: a[ix])(k, sel)
        v_sel = jax.vmap(lambda a, ix: a[ix])(v, sel)
        s = jnp.einsum('btgrd,btkgd->btgrk', qb.astype(jnp.float32), k_sel.astype(jnp.float32)) * (Dh ** -0.5)
        s = jnp.where(valid[:, :, None, None, :], s, -jnp.inf)
        p = jax.nn.softmax(s, axis=-1)
        o = jnp.einsum('btgrk,btkgd->btgrd', p, v_sel.astype(jnp.float32))
        return o.reshape(B, Q_BLOCK, H * Dh).astype(q.dtype)

    out = lax.map(block, jnp.arange(n_blocks))
    return out.transpose(1, 0, 2, 3).reshape(B, S, H * Dh)

def dsa_mixer(hn, positions, w_in, w_out):
    B, S, _ = hn.shape
    proj = hn @ w_in
    q, k, v, qi, ki, wi = jnp.split(proj, ODD_SPLITS, axis=-1)
    q = rope(q.reshape(B, S, ATT_HEADS, ATT_HEAD_DIM), positions)
    k = rope(k.reshape(B, S, ATT_KV_HEADS, ATT_HEAD_DIM), positions)
    v = v.reshape(B, S, ATT_KV_HEADS, ATT_HEAD_DIM)
    qi = rope(qi.reshape(B, S, IDX_HEADS, IDX_DIM), positions)
    ki = rope(ki.reshape(B, S, 1, IDX_DIM), positions)[:, :, 0]
    o = dsa_attention(q, k, v, qi, ki, wi)
    return o @ w_out

def first_inputs(seed: int = 0) -> dict:
    key = jax.random.key(seed)
    ks = jax.random.split(key, 20)
    f32 = jnp.float32

    def nrm(k, shape, scale):
        return jax.random.normal(k, shape, f32) * scale

    def gain(k, shape):
        return 1.0 + 0.02 * jax.random.normal(k, shape, f32)

    x = jax.random.normal(ks[0], (BATCH, SEQ, D_MODEL), f32)
    positions = jnp.broadcast_to(jnp.arange(SEQ, dtype=jnp.int32)[None, :], (BATCH, SEQ)).astype(jnp.int32)
    return {
        "x": x,
        "positions": positions,
        "ffn1_norm": gain(ks[1], (DEPTH, D_MODEL)),
        "ffn1_wi": nrm(ks[2], (DEPTH, D_MODEL, 2 * D_FF), D_MODEL ** -0.5),
        "ffn1_wo": nrm(ks[3], (DEPTH, D_FF, D_MODEL), D_FF ** -0.5),
        "mix_norm": gain(ks[4], (DEPTH, D_MODEL)),
        "ffn2_norm": gain(ks[5], (DEPTH, D_MODEL)),
        "ffn2_wi": nrm(ks[6], (DEPTH, D_MODEL, 2 * D_FF), D_MODEL ** -0.5),
        "ffn2_wo": nrm(ks[7], (DEPTH, D_FF, D_MODEL), D_FF ** -0.5),
        "even_w_in": nrm(ks[8], (N_EVEN, D_MODEL, EVEN_IN), D_MODEL ** -0.5),
        "gla_gate_w": nrm(ks[9], (N_EVEN, GLA_GATE_RANK, GLA_HEADS * GLA_DK), GLA_GATE_RANK ** -0.5),
        "gla_gate_b": nrm(ks[10], (N_EVEN, GLA_HEADS * GLA_DK), 0.1),
        "gla_out_norm": gain(ks[11], (N_EVEN, GLA_HEADS * GLA_DV)),
        "pool_w": nrm(ks[12], (N_EVEN, POOL_GROUPS, POOL_GROUP_DIM, POOL_GROUP_DIM), POOL_GROUP_DIM ** -0.5),
        "pool_scale": gain(ks[13], (N_EVEN, POOL_DIM)),
        "even_w_out": nrm(ks[14], (N_EVEN, EVEN_MIX, D_MODEL), EVEN_MIX ** -0.5),
        "odd_w_in": nrm(ks[15], (N_ODD, D_MODEL, ODD_IN), D_MODEL ** -0.5),
        "odd_w_out": nrm(ks[16], (N_ODD, ODD_MIX, D_MODEL), ODD_MIX ** -0.5),
        "final_norm": gain(ks[17], (D_MODEL,)),
    }

def first_block(x, positions, ffn1_norm, ffn1_wi, ffn1_wo, mix_norm, ffn2_norm, ffn2_wi, ffn2_wo,
              even_w_in, gla_gate_w, gla_gate_b, gla_out_norm, pool_w, pool_scale, even_w_out,
              odd_w_in, odd_w_out, final_norm):
    h = x
    for li in range(DEPTH):
        h = h + 0.5 * swiglu(rms_norm(h, ffn1_norm[li]), ffn1_wi[li], ffn1_wo[li])
        hn = rms_norm(h, mix_norm[li])
        if li % 2 == 0:
            j = li // 2
            mix = gla_pool_mixer(hn, even_w_in[j], gla_gate_w[j], gla_gate_b[j], gla_out_norm[j],
                                 pool_w[j], pool_scale[j], even_w_out[j])
        else:
            j = li // 2
            mix = dsa_mixer(hn, positions, odd_w_in[j], odd_w_out[j])
        h = h + mix
        h = h + 0.5 * swiglu(rms_norm(h, ffn2_norm[li]), ffn2_wi[li], ffn2_wo[li])
    return rms_norm(h, final_norm)


N_MIXERS = 2
N_ATTN_LAYERS = (DEPTH + 1) // 2
N_SSM_LAYERS = DEPTH // 2

HEAD_DIM = 64
N_HEADS = D_MODEL // (2 * HEAD_DIM)

REL_BUCKETS = 32
REL_MAX_DIST = 128

GROUP_CH = 16
GROUPS = D_MODEL // GROUP_CH
SSM_STATE = 64
SSM_CHUNK = 128

FFN_RESIDUAL = 0.5

PLE_DIM = 256

N_NORMS = 8
NEG_INF = -1e30


def rmsnorm(x, g):
    xf = x.astype(jnp.float32)
    y = xf * lax.rsqrt(jnp.mean(xf * xf, axis=-1, keepdims=True) + RMS_EPS)
    return (y * g.astype(jnp.float32)).astype(x.dtype)

def swiglu_2(h, w_in, w_out):
    gu = h @ w_in
    return (jax.nn.silu(gu[..., :D_FF]) * gu[..., D_FF:]) @ w_out

def t5_bucket(n):
    n = jnp.maximum(n, 0)
    max_exact = REL_BUCKETS // 2
    nf = jnp.maximum(n, 1).astype(jnp.float32)
    large = max_exact + (jnp.log(nf / max_exact) / math.log(REL_MAX_DIST / max_exact)
                         * (REL_BUCKETS - max_exact)).astype(jnp.int32)
    large = jnp.minimum(large, REL_BUCKETS - 1)
    return jnp.where(n < max_exact, n, large)

def diff_attention(h, w_qkv, w_o, lam_vecs, subln_g, rel_bias, lambda_init):
    Bsz, S, _ = h.shape
    n_blk = S // Q_BLOCK
    qkv = h @ w_qkv
    q, k, v = jnp.split(qkv, 3, axis=-1)
    q = q.reshape(Bsz, S, N_HEADS, 2, HEAD_DIM).transpose(0, 2, 3, 1, 4) * (HEAD_DIM ** -0.5)
    k = k.reshape(Bsz, S, N_HEADS, 2, HEAD_DIM).transpose(0, 2, 3, 1, 4)
    v = v.reshape(Bsz, S, N_HEADS, 2 * HEAD_DIM).transpose(0, 2, 1, 3)

    lv = lam_vecs.astype(jnp.float32)
    lam = jnp.exp(jnp.sum(lv[0] * lv[1])) - jnp.exp(jnp.sum(lv[2] * lv[3])) + lambda_init

    q_blocks = jnp.moveaxis(q.reshape(Bsz, N_HEADS, 2, n_blk, Q_BLOCK, HEAD_DIM), 3, 0)
    k_pos = jnp.arange(S, dtype=jnp.int32)

    def block(args):
        q_blk, blk = args
        q_pos = blk * Q_BLOCK + jnp.arange(Q_BLOCK, dtype=jnp.int32)
        dist = q_pos[:, None] - k_pos[None, :]
        bias = rel_bias.astype(jnp.float32)[t5_bucket(dist)]
        bias = bias.reshape(Q_BLOCK, S, N_HEADS, 2).transpose(2, 3, 0, 1)
        s = jnp.einsum('bhmqd,bhmkd->bhmqk', q_blk, k).astype(jnp.float32) + bias
        s = jnp.where(dist >= 0, s, NEG_INF)
        prob = jax.nn.softmax(s, axis=-1)
        attn = prob[:, :, 0] - lam * prob[:, :, 1]
        return jnp.einsum('bhqk,bhkv->bhqv', attn.astype(v.dtype), v)

    o = lax.map(block, (q_blocks, jnp.arange(n_blk, dtype=jnp.int32)))
    o = jnp.moveaxis(o, 0, 2).reshape(Bsz, N_HEADS, S, 2 * HEAD_DIM)
    o = rmsnorm(o, subln_g) * (1.0 - lambda_init)
    o = o.transpose(0, 2, 1, 3).reshape(Bsz, S, D_MODEL)
    return o @ w_o

def s5_glu(h, lam_re, lam_im, log_dt, b_re, b_im, c_re, c_im, d_skip, w_glu, b_glu):
    Bsz, S, _ = h.shape
    n_chunks = S // SSM_CHUNK
    lam = lax.complex(lam_re.astype(jnp.float32), lam_im.astype(jnp.float32))
    dt = jnp.exp(log_dt.astype(jnp.float32))[:, None]
    lam_dt = lam * dt
    a_bar = jnp.exp(lam_dt)
    b = lax.complex(b_re.astype(jnp.float32), b_im.astype(jnp.float32))
    b_bar = ((a_bar - 1.0) / lam)[:, :, None] * b
    c = lax.complex(c_re.astype(jnp.float32), c_im.astype(jnp.float32))
    d_g = d_skip.astype(jnp.float32).reshape(GROUPS, GROUP_CH)
    steps = jnp.arange(1, SSM_CHUNK + 1, dtype=jnp.float32)
    a_pow = jnp.exp(steps[:, None, None] * lam_dt[None])

    u = h.astype(jnp.float32).reshape(Bsz, n_chunks, SSM_CHUNK, GROUPS, GROUP_CH)
    u = jnp.moveaxis(u, 1, 0)

    def combine(e1, e2):
        a1, x1 = e1
        a2, x2 = e2
        return a1 * a2, a2 * x1 + x2

    def chunk_step(state, u_c):
        bu = jnp.einsum('gph,bcgh->bcgp', b_bar, u_c.astype(jnp.complex64))
        a = jnp.broadcast_to(a_bar, bu.shape)
        _, xs = lax.associative_scan(combine, (a, bu), axis=1)
        xs = xs + a_pow[None] * state[:, None]
        y = jnp.einsum('ghp,bcgp->bcgh', c, xs).real + d_g * u_c
        return xs[:, -1], y

    state0 = jnp.zeros((Bsz, GROUPS, SSM_STATE), jnp.complex64)
    _, ys = lax.scan(chunk_step, state0, u)
    y = jnp.moveaxis(ys, 0, 1).reshape(Bsz, S, D_MODEL).astype(h.dtype)
    z = jax.nn.gelu(y) @ w_glu + b_glu
    return z[..., :D_MODEL] * jax.nn.sigmoid(z[..., D_MODEL:])

def second_inputs(seed: int = 0) -> dict:
    key = jax.random.key(seed)
    ks = jax.random.split(key, 24)
    f32 = jnp.float32
    nrm = lambda k, shape, scale: jax.random.normal(k, shape, f32) * scale

    x = nrm(ks[0], (BATCH, SEQ, D_MODEL), 1.0)
    p = nrm(ks[1], (DEPTH, BATCH, SEQ, PLE_DIM), 1.0)
    norm_g = 1.0 + nrm(ks[2], (DEPTH, N_NORMS, D_MODEL), 0.05)
    ffn_w_in = nrm(ks[3], (DEPTH, 2, D_MODEL, 2 * D_FF), D_MODEL ** -0.5)
    ffn_w_out = nrm(ks[4], (DEPTH, 2, D_FF, D_MODEL), D_FF ** -0.5)

    attn_w_qkv = nrm(ks[5], (N_ATTN_LAYERS, D_MODEL, 3 * D_MODEL), D_MODEL ** -0.5)
    attn_w_o = nrm(ks[6], (N_ATTN_LAYERS, D_MODEL, D_MODEL), D_MODEL ** -0.5)
    attn_lam = nrm(ks[7], (N_ATTN_LAYERS, 4, HEAD_DIM), 0.1)
    attn_subln_g = 1.0 + nrm(ks[8], (N_ATTN_LAYERS, 2 * HEAD_DIM), 0.05)
    rel_bias = nrm(ks[9], (REL_BUCKETS, 2 * N_HEADS), 0.5)

    n_idx = jnp.arange(SSM_STATE, dtype=f32)
    ssm_lam_re = jnp.full((N_SSM_LAYERS, GROUPS, SSM_STATE), -0.5, f32) + nrm(ks[10], (N_SSM_LAYERS, GROUPS, SSM_STATE), 1e-3)
    ssm_lam_im = jnp.broadcast_to(math.pi * n_idx, (N_SSM_LAYERS, GROUPS, SSM_STATE)) + nrm(ks[11], (N_SSM_LAYERS, GROUPS, SSM_STATE), 1e-3)
    ssm_log_dt = jax.random.uniform(ks[12], (N_SSM_LAYERS, GROUPS), f32, math.log(1e-3), math.log(1e-1))
    b_scale = (2.0 * GROUP_CH) ** -0.5
    c_scale = (2.0 * SSM_STATE) ** -0.5
    ssm_b_re = nrm(ks[13], (N_SSM_LAYERS, GROUPS, SSM_STATE, GROUP_CH), b_scale)
    ssm_b_im = nrm(ks[14], (N_SSM_LAYERS, GROUPS, SSM_STATE, GROUP_CH), b_scale)
    ssm_c_re = nrm(ks[15], (N_SSM_LAYERS, GROUPS, GROUP_CH, SSM_STATE), c_scale)
    ssm_c_im = nrm(ks[16], (N_SSM_LAYERS, GROUPS, GROUP_CH, SSM_STATE), c_scale)
    ssm_d = nrm(ks[17], (N_SSM_LAYERS, D_MODEL), 1.0)
    ssm_w_glu = nrm(ks[18], (N_SSM_LAYERS, D_MODEL, 2 * D_MODEL), D_MODEL ** -0.5)
    ssm_b_glu = nrm(ks[19], (N_SSM_LAYERS, 2 * D_MODEL), 0.01)

    ple_w_proj = nrm(ks[20], (DEPTH, PLE_DIM, D_MODEL), PLE_DIM ** -0.5)
    ple_w_gate = nrm(ks[21], (DEPTH, D_MODEL, D_MODEL), D_MODEL ** -0.5)

    return {"x": x, "p": p, "norm_g": norm_g, "ffn_w_in": ffn_w_in, "ffn_w_out": ffn_w_out,
            "attn_w_qkv": attn_w_qkv, "attn_w_o": attn_w_o, "attn_lam": attn_lam,
            "attn_subln_g": attn_subln_g, "rel_bias": rel_bias,
            "ssm_lam_re": ssm_lam_re, "ssm_lam_im": ssm_lam_im, "ssm_log_dt": ssm_log_dt,
            "ssm_b_re": ssm_b_re, "ssm_b_im": ssm_b_im, "ssm_c_re": ssm_c_re, "ssm_c_im": ssm_c_im,
            "ssm_d": ssm_d, "ssm_w_glu": ssm_w_glu, "ssm_b_glu": ssm_b_glu,
            "ple_w_proj": ple_w_proj, "ple_w_gate": ple_w_gate}

def second_block(x, p, norm_g, ffn_w_in, ffn_w_out, attn_w_qkv, attn_w_o, attn_lam, attn_subln_g,
              rel_bias, ssm_lam_re, ssm_lam_im, ssm_log_dt, ssm_b_re, ssm_b_im, ssm_c_re, ssm_c_im,
              ssm_d, ssm_w_glu, ssm_b_glu, ple_w_proj, ple_w_gate):
    for i in range(DEPTH):
        g = norm_g[i]
        x = x + FFN_RESIDUAL * rmsnorm(swiglu_2(rmsnorm(x, g[0]), ffn_w_in[i, 0], ffn_w_out[i, 0]), g[1])
        h = rmsnorm(x, g[2])
        j = i // N_MIXERS
        if i % N_MIXERS == 0:
            lambda_init = 0.8 - 0.6 * math.exp(-0.3 * i)
            m = diff_attention(h, attn_w_qkv[j], attn_w_o[j], attn_lam[j], attn_subln_g[j],
                               rel_bias, lambda_init)
        else:
            m = s5_glu(h, ssm_lam_re[j], ssm_lam_im[j], ssm_log_dt[j], ssm_b_re[j], ssm_b_im[j],
                       ssm_c_re[j], ssm_c_im[j], ssm_d[j], ssm_w_glu[j], ssm_b_glu[j])
        x = x + rmsnorm(m, g[3])
        x = x + FFN_RESIDUAL * rmsnorm(swiglu_2(rmsnorm(x, g[4]), ffn_w_in[i, 1], ffn_w_out[i, 1]), g[5])
        gate = jax.nn.sigmoid(rmsnorm(x, g[6]) @ ple_w_gate[i])
        x = x + rmsnorm(gate * (p[i] @ ple_w_proj[i]), g[7])
    return x


def setup_inputs(seed=0):
    out = dict(first_inputs(seed))
    for name, value in second_inputs(seed + 1).items():
        if name != "x":
            out[name + "_2"] = value
    return out


def reference(
    x, positions, ffn1_norm, ffn1_wi, ffn1_wo, mix_norm, ffn2_norm, ffn2_wi, ffn2_wo, even_w_in,
    gla_gate_w, gla_gate_b, gla_out_norm, pool_w, pool_scale, even_w_out, odd_w_in, odd_w_out,
    final_norm, p_2, norm_g_2, ffn_w_in_2, ffn_w_out_2, attn_w_qkv_2, attn_w_o_2, attn_lam_2,
    attn_subln_g_2, rel_bias_2, ssm_lam_re_2, ssm_lam_im_2, ssm_log_dt_2, ssm_b_re_2,
    ssm_b_im_2, ssm_c_re_2, ssm_c_im_2, ssm_d_2, ssm_w_glu_2, ssm_b_glu_2, ple_w_proj_2,
    ple_w_gate_2,
):
    x = first_block(
        x, positions, ffn1_norm, ffn1_wi, ffn1_wo, mix_norm, ffn2_norm, ffn2_wi, ffn2_wo,
        even_w_in, gla_gate_w, gla_gate_b, gla_out_norm, pool_w, pool_scale, even_w_out,
        odd_w_in, odd_w_out, final_norm,
    )
    return second_block(
        x, p_2, norm_g_2, ffn_w_in_2, ffn_w_out_2, attn_w_qkv_2, attn_w_o_2, attn_lam_2,
        attn_subln_g_2, rel_bias_2, ssm_lam_re_2, ssm_lam_im_2, ssm_log_dt_2, ssm_b_re_2,
        ssm_b_im_2, ssm_c_re_2, ssm_c_im_2, ssm_d_2, ssm_w_glu_2, ssm_b_glu_2, ple_w_proj_2,
        ple_w_gate_2,
    )


_drawn_inputs = setup_inputs


def setup_inputs(seed=0):
    import zlib

    import numpy as np

    out = dict(_drawn_inputs(seed))
    spreads = {}
    factors = {'ffn2_norm': 3.093,
     'gla_out_norm': 3.409,
     'ssm_lam_re_2': 8.0,
     'ssm_b_re_2': 2.773,
     'ssm_b_im_2': 2.67,
     'ssm_c_re_2': 2.762,
     'ssm_b_glu_2': 8.0}
    for name, (base, spread) in spreads.items():
        noise = np.random.default_rng([zlib.crc32(name.encode()), seed]).standard_normal(out[name].shape)
        drawn = base * np.exp(spread * noise) if base else spread * noise
        out[name] = __import__('jax').numpy.asarray(drawn.astype(out[name].dtype))
    for name, factor in factors.items():
        out[name] = (out[name] * factor).astype(out[name].dtype)
    return out
```

```python
import math
from contextlib import ExitStack

import concourse.bass as bass
import numpy as np
from concourse import mybir

F32 = mybir.dt.float32
F32R = mybir.dt.float32r
I32 = mybir.dt.int32
ALU = mybir.AluOpType
ACT = mybir.ActivationFunctionType
AX = mybir.AxisListType

P = 128
SEQ = 256
MT = SEQ // P
D = 1024
DK = D // P
D_FF = 2816
FK = D_FF // P
CB = 512
FB = CB // 2
NFB = D_FF // FB
DB = D // CB
RING = 4
SLOT = 3 * CB
EPS = 1e-6
NEG = -1e30

GLA_HEADS, GLA_DK, GLA_DV, GLA_CHUNK, GLA_TAU, GATE_RANK = 4, 64, 128, 64, 16.0, 16
GLA_QK = GLA_HEADS * GLA_DK
GLA_V = GLA_HEADS * GLA_DV
POOL_WINDOWS = (2, 4, 8, 16)
POOL_DIM = 512
EVEN_IN = 2 * GLA_QK + 2 * GLA_V + GATE_RANK + POOL_DIM
V_AT, G_AT, LR_AT, U_AT = 2 * GLA_QK, 2 * GLA_QK + GLA_V, 2 * GLA_QK + 2 * GLA_V, EVEN_IN - POOL_DIM

ATT_HEADS, KV_HEADS, HD, IDX_HEADS, IDX_DIM = 8, 2, 128, 4, 64
TOPK = min(256, SEQ // 4)
ATT_K, ATT_V, ATT_QI = ATT_HEADS * HD, (ATT_HEADS + KV_HEADS) * HD, (ATT_HEADS + 2 * KV_HEADS) * HD
ATT_WI = ATT_QI + (IDX_HEADS + 1) * IDX_DIM
ODD_IN = ATT_WI + IDX_HEADS
PICKED, BARRED = -3.3e38, -3.0e38

DIFF_HEADS, DIFF_DIM, LAMBDA_INIT = 8, 64, 0.8 - 0.6 * math.exp(-0.3 * 0)
BUCKETS, MAX_DIST = 32, 128
RELN = 384

GROUPS, GCH, STATES = 64, 16, 64
NJ = GROUPS * STATES // P
TC = 128
PLE = 256

ROUND = 1.5 * 2.0 ** 23
TWO_PI = (6.28125, 0.001935243606567383, 6.357301884918343e-08)
SAFE_PI, SAFE_TURN = 3.1415925, 6.283185

LINEAR = {
    "even_in": (DK, EVEN_IN, 1, 1),
    "even_out": (DK, D, 0, MT),
    "odd_in": (DK, ODD_IN, 1, 1),
    "odd_out": (DK, D, 0, MT),
    "qkv": (DK, 3 * D, 1, 1),
    "w_o": (DK, D, MT, MT),
    "glu": (DK, 2 * D, 0, MT),
    "gate0": (DK, D, MT, 0),
    "ple0": (PLE // P, D, 0, MT),
    "gate1": (DK, D, MT, 0),
    "ple1": (PLE // P, D, 0, MT),
}

STAGE_KINDS = {
    "ffna": (["{}"], 4 + NFB, True, False),
    "even": (["even_in", "even_out"], 8, True, False),
    "odd": (["odd_in", "odd_out"], 8, True, False),
    "final": ([], 0, True, False),
    "ffnb": (["{}"], 4 + NFB, True, True),
    "diff": (["qkv", "w_o"], 8, True, True),
    "ssm": (["glu"], 4, True, True),
    "ple": (["gate", "ple"], 5, True, True),
}
STAGES = ["ffna0", "even", "ffna1", "ffna2", "odd", "ffna3", "final",
          "ffnb0", "diff", "ffnb1", "ple0", "ffnb2", "ssm", "ffnb3", "ple1"]

GAIN_AT = {"ffn1_norm": 0, "mix_norm": 16, "ffn2_norm": 32, "norm_g_2": 48, "pool_scale": 176,
           "attn_subln_g_2": 180, "ssm_d_2": 181}
GAIN_ROWS = 189


def gain_row(stage):
    return {"ffna0": 0, "even": 16, "ffna1": 32, "ffna2": 8, "odd": 24, "ffna3": 40,
            "ffnb0": 48 + 0, "diff": 48 + 16, "ffnb1": 48 + 32, "ple0": 48 + 48,
            "ffnb2": 48 + 64, "ssm": 48 + 80, "ffnb3": 48 + 96, "ple1": 48 + 112}[stage]


ROW_GAINS = {"even": ("gla_out_norm", (0,), GLA_V), "final": ("final_norm", (), D),
             "ffnb0": ("norm_g_2", (0, 1), D), "diff": ("norm_g_2", (0, 3), D),
             "ffnb1": ("norm_g_2", (0, 5), D), "ple0": ("norm_g_2", (0, 7), D),
             "ffnb2": ("norm_g_2", (1, 1), D), "ssm": ("norm_g_2", (1, 3), D),
             "ffnb3": ("norm_g_2", (1, 5), D), "ple1": ("norm_g_2", (1, 7), D)}

FFN_W = {"ffna0": ("ffn1_wi", "ffn1_wo", (0,)), "ffna1": ("ffn2_wi", "ffn2_wo", (0,)),
         "ffna2": ("ffn1_wi", "ffn1_wo", (1,)), "ffna3": ("ffn2_wi", "ffn2_wo", (1,)),
         "ffnb0": ("ffn_w_in_2", "ffn_w_out_2", (0, 0)), "ffnb1": ("ffn_w_in_2", "ffn_w_out_2", (0, 1)),
         "ffnb2": ("ffn_w_in_2", "ffn_w_out_2", (1, 0)), "ffnb3": ("ffn_w_in_2", "ffn_w_out_2", (1, 1))}
LINEAR_W = {"even_in": ("even_w_in", 0), "even_out": ("even_w_out", 0), "odd_in": ("odd_w_in", 0),
            "odd_out": ("odd_w_out", 0), "qkv": ("attn_w_qkv_2", 0), "w_o": ("attn_w_o_2", 0),
            "glu": ("ssm_w_glu_2", 0), "gate0": ("ple_w_gate_2", 0), "ple0": ("ple_w_proj_2", 0),
            "gate1": ("ple_w_gate_2", 1), "ple1": ("ple_w_proj_2", 1)}


def k_groups(n):
    return [3] * 6 + [2] * 2 if n == FK else [2] * (n // 2)


def plan():
    units, first, acts, dves, stage = [], {}, [0], [0], {}
    tg = nn = pre = npost = xu = gb = nf = 0

    def add_block(name, kn, c0, cn, act_counts, dve_counts):
        k = 0
        for n in k_groups(kn):
            units.append((name, k, n, c0, cn))
            k += n
        acts.append(acts[-1] + act_counts)
        dves.append(dves[-1] + dve_counts)

    for name in STAGES:
        kind = name.rstrip("0123456789")
        weights, pairs, in_front, behind = STAGE_KINDS[kind]
        stage[name] = dict(tg=tg, pre=nn if in_front else None, npre=pre, npost=npost, post=nn + 1 if behind else None,
                           xu=xu, gb=gb, nf=nf)
        tg += pairs
        pre += in_front
        nn += in_front + behind
        xu += MT if behind or kind == "final" else 0
        npost += behind
        gb += name in ROW_GAINS
        nf += kind.startswith("ffn")
        for w in weights:
            w = w.format(name) if "{}" in w else w + (name[3:] if kind == "ple" else "")
            first[w] = (len(units), len(acts) - 1)
            if kind.startswith("ffn"):
                for fb in range(NFB):
                    add_block(w + ".in", DK, fb * FB, CB, MT, MT)
                for cb in range(DB):
                    add_block(w + ".out", FK, cb * CB, CB, MT if behind else 0, MT)
            else:
                kn, cols, a, d = LINEAR[w]
                for c0 in range(0, cols, CB):
                    add_block(w, kn, c0, min(CB, cols - c0), a, d)
    return units, first, acts, dves, stage, nn, xu


def tables():
    t = np.arange(P)
    same = (t[:, None] // GLA_CHUNK) == (t[None, :] // GLA_CHUNK)
    src, dst = t[:, None] % GLA_CHUNK, t[None, :] % GLA_CHUNK
    upto = (same & (src <= dst)).astype(np.float32)
    mid = (same & (src < GLA_CHUNK // 2)).astype(np.float32)
    whole = same.astype(np.float32)
    chunk = (t[:, None] // GLA_CHUNK == np.arange(2)[None, :]).astype(np.float32)
    gla = np.concatenate([(upto - mid), upto, (whole - upto), chunk], 1) / np.float32(GLA_TAU)
    s, q = np.arange(SEQ)[:, None], np.arange(SEQ)[None, :]
    pool = []
    for w in POOL_WINDOWS:
        band = ((s <= q) & (s > q - w)).astype(np.float32) / np.minimum(q + 1, w).astype(np.float32)
        pool.append(band - (s == q).astype(np.float32))
    pool = np.stack(pool).reshape(4, MT, P, SEQ).transpose(2, 0, 1, 3)
    keep = (t[None, :GLA_CHUNK] >= (t[:, None] % GLA_CHUNK)).astype(np.int32)
    qpos = np.arange(MT)[None, :, None] * P + t[:, None, None]
    barred = (np.arange(SEQ)[None, None, :] > qpos)
    inv = np.concatenate([np.float32(10000.0) ** (-np.arange(0, d, 2, dtype=np.float32) / np.float32(d))
                          for d in (HD, IDX_DIM)]).astype(np.float32)
    dist = SEQ - 1 - np.arange(RELN)
    n = np.maximum(dist, 0)
    exact = BUCKETS // 2
    large = exact + (np.log(np.maximum(n, 1).astype(np.float32) / np.float32(exact))
                     / np.float32(math.log(MAX_DIST / exact)) * np.float32(BUCKETS - exact)).astype(np.int32)
    bucket = np.where(n < exact, n, np.minimum(large, BUCKETS - 1))
    hot = np.zeros((BUCKETS + 1, RELN), np.float32)
    hot[bucket, np.arange(RELN)] = 8.0
    hot[:, dist < 0] = 0.0
    hot[BUCKETS, dist < 0] = 8.0 * NEG
    parity = np.stack([t % 32 < 16, t % 32 >= 16, t < 64, t >= 64], 1).astype(np.float32)
    steps = np.broadcast_to(np.arange(1, TC + 1, dtype=np.float32)[None], (P, TC))
    return {
        "c_ident": np.eye(P, dtype=np.float32),
        "c_flip": np.ascontiguousarray(np.eye(P, dtype=np.float32)[::-1]),
        "c_gla": np.ascontiguousarray(gla, np.float32),
        "c_pool": np.ascontiguousarray(pool, np.float32),
        "c_keep": np.ascontiguousarray(keep),
        "c_barred": np.ascontiguousarray(barred.astype(np.int32)),
        "c_inv": np.ascontiguousarray(np.broadcast_to(inv[None], (P, inv.size))),
        "c_hot": hot,
        "c_parity": np.ascontiguousarray(parity),
        "c_steps": np.ascontiguousarray(steps),
    }


def build_program(nc, A, out, rel_scratch):
    units, first, acts, dves, stage, N_NORMS, X_ALL = plan()
    ctx = ExitStack()
    with ctx:
        class Sems(dict):
            def __missing__(self, name):
                self[name] = ctx.enter_context(nc.semaphore(name))
                return self[name]

        S = Sems()

        def sb(name, shape, dt=F32, where=ctx):
            return where.enter_context(nc.sbuf_tensor(name, shape, dt))

        raw = sb("raw", [P, RING, SLOT])
        w_hi = sb("w_hi", [P, RING, SLOT], F32R)
        w_lo = sb("w_lo", [P, RING, SLOT], F32R)
        with ExitStack() as place:
            xT_hi = sb("xT_hi", [P, DK, SEQ], F32R, place)
            xT_lo = sb("xT_lo", [P, DK, SEQ], F32R, place)
        sm_blocks = sb("sm_blocks", [P, 4, 4 * SEQ])
        x = sb("x", [P, MT, D])
        y = sb("y", [P, MT, D])
        ident = sb("ident", [P, P])
        gT = sb("gT", [P, GAIN_ROWS])
        gB = sb("gB", [P, 2, D])
        ss = sb("ss", [P, N_NORMS, MT, DB])
        std = sb("std", [P, N_NORMS, MT])
        rstd = sb("rstd", [P, N_NORMS, MT])
        trig = sb("trig", [P, 2, MT, 96])
        neg_lam = sb("neg_lam", [P, 1])
        sm_par = sb("sm_par", [P, 6, NJ])
        acc = ctx.enter_context(nc.psum_tensor("acc", [P, 2 * MT, CB], F32))
        tp = ctx.enter_context(nc.psum_tensor("tp", [P, 2, CB], F32))
        ms = ctx.enter_context(nc.psum_tensor("ms", [P, 2, CB], F32))

        with ExitStack() as arena:
            hT_hi = sb("hT_hi", [P, FK, SEQ], F32R, arena)
            hT_lo = sb("hT_lo", [P, FK, SEQ], F32R, arena)
            silu = sb("silu", [P, 2, MT, FB], F32, arena)
            h = sb("h", [P, 2, MT, FB], F32, arena)
            with ExitStack() as setup:
                gain_rows = sb("gain_rows", [P, 2, P], F32, setup)
                pos_i = sb("pos_i", [P, MT], I32, setup)
                pos = sb("pos", [P, MT], F32, setup)
                inv = sb("inv", [P, 96], F32, setup)
                ang = sb("ang", [P, MT, 96], F32, setup)
                turns = sb("turns", [P, 2, MT, 96], F32, setup)
                red = sb("red", [P, 2, MT, 96], F32, setup)
                lam_v = sb("lam_v", [P, 2, 2, DIFF_DIM], F32, setup)
                lam_p = sb("lam_p", [P, 2, DIFF_DIM], F32, setup)
                lam_s = sb("lam_s", [P, 4], F32, setup)
                rel_b = sb("rel_b", [BUCKETS + 1, 2 * DIFF_HEADS], F32, setup)
                hot = sb("hot", [BUCKETS + 1, RELN], F32, setup)
                rel_v = sb("rel_v", [2 * DIFF_HEADS, RELN], F32, setup)
                sm_rows = sb("sm_rows", [NJ, 14, P], F32, setup)
                sm_dt = sb("sm_dt", [NJ, 2, 2], F32, setup)
            sm_cos = sb("sm_cos", [P, NJ, TC], F32, arena)
            sm_sin = sb("sm_sin", [P, NJ, TC], F32, arena)
            sm_steps = sb("sm_steps", [P, TC], F32, arena)
            sm_parity = sb("sm_parity", [P, 4], F32, arena)
            sm_t = sb("sm_t", [P, 2, 4, TC], F32, arena)
        with ExitStack() as arena:
            ev = sb("ev", [P, MT, EVEN_IN], F32, arena)
            ev_g = sb("ev_g", [P, MT, GLA_V], F32, arena)
            ev_lrT = sb("ev_lrT", [GATE_RANK + 1, SEQ], F32, arena)
            ev_gw = sb("ev_gw", [GATE_RANK + 1, GLA_QK], F32, arena)
            ev_t = sb("ev_t", [P, MT, GLA_QK], F32, arena)
            ev_la = sb("ev_la", [P, MT, GLA_QK], F32, arena)
            ev_e = sb("ev_e", [P, 4, MT, GLA_QK], F32, arena)
            ev_s = sb("ev_s", [P, 4, MT, GLA_QK], F32, arena)
            ev_T = sb("ev_T", [P, 3, 2, SEQ], F32, arena)
            ev_sc = sb("ev_sc", [P, MT, GLA_HEADS, P], F32, arena)
            ev_dec = sb("ev_dec", [P, 2, 2 * MT], F32, arena)
            ev_st = sb("ev_st", [P, 3, 2, GLA_DV], F32, arena)
            ev_o = sb("ev_o", [P, MT, GLA_V], F32, arena)
            ev_c = sb("ev_c", [P, 3 * P + 2], F32, arena)
            ev_keep = sb("ev_keep", [P, GLA_CHUNK], I32, arena)
            ev_pw = sb("ev_pw", [P, 4, MT, SEQ], F32, arena)
            ev_pT = sb("ev_pT", [P, 4, SEQ], F32, arena)
            ev_pm = sb("ev_pm", [P, 4, P], F32, arena)
            ev_ss = sb("ev_ss", [P, 3, MT * GLA_HEADS], F32, arena)
        with ExitStack() as arena:
            od = sb("od", [P, MT, ODD_IN], F32, arena)
            od_r = sb("od_r", [P, MT, ATT_HEADS + KV_HEADS, HD], F32, arena)
            od_ri = sb("od_ri", [P, MT, IDX_HEADS + 2, IDX_DIM], F32, arena)
            od_t = sb("od_t", [P, 4, ATT_HEADS + KV_HEADS, HD // 2], F32, arena)
            od_qT = sb("od_qT", [P, 4, 2, SEQ], F32, arena)
            od_kT = sb("od_kT", [P, KV_HEADS, SEQ], F32, arena)
            od_qiT = sb("od_qiT", [P, 2, SEQ], F32, arena)
            od_kiT = sb("od_kiT", [P, SEQ], F32, arena)
            od_rl = sb("od_rl", [P, MT, IDX_HEADS, SEQ], F32, arena)
            od_is = sb("od_is", [P, MT, SEQ], F32, arena)
            od_m8 = sb("od_m8", [P, 8], F32, arena)
            od_bar = sb("od_bar", [P, MT, SEQ], I32, arena)
            od_fill = sb("od_fill", [P, SEQ], F32, arena)
            od_neg = sb("od_neg", [P, SEQ], F32, arena)
            od_p = sb("od_p", [P, 2, 2, SEQ], F32, arena)
            od_pT = sb("od_pT", [P, 2, CB], F32, arena)
            od_mx = sb("od_mx", [P, 8, 2, 4], F32, arena)
        with ExitStack() as arena:
            df = sb("df", [P, MT, 3 * D], F32, arena)
            df_qT = sb("df_qT", [P, DIFF_HEADS, SEQ], F32, arena)
            df_kT = sb("df_kT", [P, DIFF_HEADS, SEQ], F32, arena)
            df_flip = sb("df_flip", [P, P], F32, arena)
            df_b = sb("df_b", [P, 2, 2, SEQ], F32, arena)
            df_p = sb("df_p", [P, 2, 2, SEQ], F32, arena)
            df_a = sb("df_a", [P, 2, SEQ], F32, arena)
            df_pT = sb("df_pT", [P, 2, SEQ], F32, arena)
            df_mx = sb("df_mx", [P, 16, 5, 2], F32, arena)
            df_o = sb("df_o", [P, MT, D], F32, arena)
            df_ss = sb("df_ss", [P, 3, MT, DIFF_HEADS], F32, arena)
        with ExitStack() as arena:
            pl_g = sb("pl_g", [P, MT, D], F32, arena)
            pl_p = sb("pl_p", [P, MT, PLE], F32, arena)
            pl_hi = sb("pl_hi", [P, 2, SEQ], F32R, arena)
            pl_lo = sb("pl_lo", [P, 2, SEQ], F32R, arena)
        with ExitStack() as arena:
            sm_BT = sb("sm_BT", [P, 2, DK, P], F32, arena)
            sm_CT = sb("sm_CT", [P, 3, NJ, 2 * GCH], F32, arena)
            sm_a = sb("sm_a", [P, 2, 2, 2, TC], F32, arena)
            sm_z = sb("sm_z", [P, 2, 2, 2, TC], F32, arena)
            sm_x = sb("sm_x", [P, 2, 2, 2, 2, TC], F32, arena)
            sm_carry = sb("sm_carry", [P, NJ, 2], F32, arena)
            sm_y = sb("sm_y", [P, 2, 4, TC], F32, arena)
            sm_bg = sb("sm_bg", [P, 2 * D], F32, arena)
        assert 2 * DK * P + 3 * NJ * 2 * GCH + 4 * 8 * TC + 2 * NJ + 8 * TC + 2 * D <= 2 * FK * SEQ + 4 * MT * FB
        flat4 = "p a b c -> p (a b c)"
        sm_bd = [sm_blocks[:, r, :] for r in range(2)]
        sm_cd = [sm_blocks[:, 2 + r, :] for r in range(2)]
        sm_b = silu[:, :, :, :].rearrange(flat4).rearrange("p (r j c) -> p r j c", r=2, j=NJ)
        sm_c = h[:, :, :, :].rearrange(flat4).rearrange("p (r k s) -> p r k s", r=2, k=DK)
        sm_hT = sm_blocks[:, 2:4, :].rearrange("p a (k t) -> p (a k) t", t=SEQ)


        def rows_of(w, k, kn, c, n):
            return w[k * P:(k + kn) * P, bass.ds(c, n)].rearrange("(k p) c -> p k c", p=P)

        def pieces_of(u, shift=0):
            name, k, kn, c0, cn = units[u]
            layer, _, side = name.partition(".")
            if side == "in":
                w = A[FFN_W[layer][0]]
                for i in FFN_W[layer][2]:
                    w = w[i]
                return [(0, FB, rows_of(w, k, kn, shift + c0, FB)),
                        (FB, FB, rows_of(w, k, kn, shift + c0 + D_FF, FB))]
            if side == "out":
                w = A[FFN_W[layer][1]]
                for i in FFN_W[layer][2]:
                    w = w[i]
            else:
                w = A[LINEAR_W[layer][0]][LINEAR_W[layer][1]]
            return [(0, cn, rows_of(w, k, kn, c0, cn))]

        def slot(ring, u):
            _, _, kn, _, cn = units[u]
            return ring[:, u % RING, 0:kn * cn].rearrange("p (k c) -> p k c", k=kn)

        def flat(ring, u):
            _, _, kn, _, cn = units[u]
            return ring[:, u % RING, 0:kn * cn]

        def pair(tile, k):
            return tile[:, k:k + 2, :].rearrange("p k t -> p (k t)")

        def wait_x(eng, name, cb=DB - 1):
            at = STAGES.index(name) if name else len(STAGES)
            if at == 0:
                eng.wait_ge(S["x_landed"], 16)
                return
            before = STAGES[at - 1]
            if stage[before]["post"] is not None or before == "final":
                eng.wait_ge(S["x_upd"], stage[name]["xu"] if name else X_ALL)
            else:
                last = STAGE_KINDS[before.rstrip("0123456789")][0][-1].format(before)
                b = first[last][1] + (NFB if before.startswith("ffn") else 0)
                eng.wait_ge(S["acc_dve"], dves[b + cb + 1])

        def state_part(hp, c):
            return ms[:, 1, hp * P:(hp + 1) * P] if c == 1 else acc[:, 3, (2 * hp + c // 2) * P:(2 * hp + c // 2 + 1) * P]

        def of_head(m, hd):
            return (2 * m + hd // 2) * P

        def tiles_of(jp):
            per = NJ // DK
            j = 2 * per * (jp // per) + jp % per
            return j, j + per

        def z2(m):
            return sm_y[:, m, :, :].rearrange("p k t -> p (k t)")

        def squared_before(name):
            return 2 * DB * [n for n in STAGES if n in ("ple0", "ssm", "ple1")].index(name)

        with_block = ctx.enter_context(nc.Block())

        @with_block.sync
        def _(sp):
            def load(u, i=0, per=0):
                if u >= RING:
                    sp.wait_ge(S["w_split"], u - RING + 1 + per * i)
                pieces = pieces_of(u, FB * i if per else 0)
                for c, n, src in pieces:
                    sp.dma_start(slot(raw, u)[:, :, c:c + n], src).then_inc(
                        S[f"w_landed{u % RING}"], 32 // len(pieces))

            sp.dma_start(ident[:, :], A["c_ident"]).then_inc(S["ident_landed"], 16)
            sp.dma_start(x[:, :, :], A["x"].rearrange("b (m p) d -> p (b m) d", p=P)).then_inc(S["x_landed"], 16)
            u = 0
            while u < len(units):
                if units[u][0].endswith(".in"):
                    n = DK // 2
                    peel = n if u < RING else 0
                    for v in range(peel):
                        load(u + v)
                    with nc.sync.Fori(0, NFB - peel // n) as i:
                        for v in range(n):
                            load(u + peel + v, i, n)
                    u += n * NFB
                else:
                    load(u)
                    u += 1
            wait_x(sp, None)
            sp.dma_start(out.rearrange("b (m p) d -> p (b m) d", p=P), x[:, :, :]).then_inc(S["stored"], 16)
            sp.wait_ge(S["stored"], 16)

        @with_block.gpsimd
        def _(pool):
            def row_gain(name):
                g = stage[name]["gb"]
                key, index, width = ROW_GAINS[name]
                if g >= 2:
                    before = [n for n in ROW_GAINS if n in stage][g - 2]
                    after = STAGES[STAGES.index(before) + 1]
                    wait_x(pool, after)
                v = A[key]
                for i in index:
                    v = v[i]
                pool.dma_start(gB[:, g % 2, 0:width],
                               v.rearrange("(a n) -> a n", a=1).to_broadcast([P, width])).then_inc(
                    S[f"gain_landed{g % 2}"], 16)

            def spread(v, n):
                return v.rearrange("(a n) -> a n", a=1).to_broadcast([P, n])

            pool.memset(rel_b[:, :], 1.0).then_inc(S["rel_ones"], 1)
            pool.dma_start(gain_rows[0:16, 0, :], A["ffn1_norm"].rearrange("l (k p) -> (l k) p", p=P)).then_inc(
                S["gain0_landed"], 16)
            loads = [
                (gain_rows[16:32, 0, :], A["mix_norm"].rearrange("l (k p) -> (l k) p", p=P)),
                (gain_rows[32:48, 0, :], A["ffn2_norm"].rearrange("l (k p) -> (l k) p", p=P)),
                (gain_rows[48:128, 0, :],
                 A["norm_g_2"].rearrange("i j (k p) -> (i j k) p", p=P)[0:80, :]),
                (gain_rows[0:48, 1, :],
                 A["norm_g_2"].rearrange("i j (k p) -> (i j k) p", p=P)[80:128, :]),
                (gain_rows[48:52, 1, :], A["pool_scale"].rearrange("a (k p) -> (a k) p", p=P)),
                (gain_rows[52:53, 1, :], A["attn_subln_g_2"]),
                (gain_rows[53:61, 1, :], A["ssm_d_2"].rearrange("a (k p) -> (a k) p", p=P)),
            ]
            for dst, src in loads:
                pool.dma_start(dst, src).then_inc(S["gains_landed"], 16)
            pool.wait_ge(S["rel_ones"], 1)
            more = [
                (pos_i[:, :], A["positions"].rearrange("b (m p) -> p (b m)", p=P)),
                (inv[:, :], A["c_inv"]),
                (lam_v[:, :, :, :].rearrange("p a b c -> p (a b c)"),
                 spread(A["attn_lam_2"][0].rearrange("a b -> (a b)"), 4 * DIFF_DIM)),
                (rel_b[0:BUCKETS, :], A["rel_bias_2"]),
                (hot[:, :], A["c_hot"]),
            ]
            for dst, src in [
                (sm_rows[:, 0, :], A["ssm_lam_re_2"][0].rearrange("(j g) s -> j (g s)", g=2)),
                (sm_rows[:, 1, :], A["ssm_lam_im_2"][0].rearrange("(j g) s -> j (g s)", g=2)),
                (sm_dt[:, 0, :], A["ssm_log_dt_2"][0].rearrange("(j g) -> j g", g=2)),
            ]:
                pool.dma_start(dst, src).then_inc(S["sm_landed"], 16)
            for dst, src in more:
                pool.dma_start(dst, src, allow_slow_non_contiguous=True).then_inc(S["setup_landed"], 16)
            pool.wait_ge(S["rel_copied"], 1)
            pool.dma_start(rel_scratch, rel_v[:, :]).then_inc(S["rel_stored"], 16)
            pool.wait_ge(S["rel_stored"], 16)

            steps_done = [0]

            def link(ins):
                steps_done[0] += 1
                ins.then_inc(S["pool_step"], 1)
                pool.wait_ge(S["pool_step"], steps_done[0])

            def prepare_ssm(name):
                u0, b0 = first[name]
                tt, ts = nc.gpsimd.tensor_tensor, nc.gpsimd.tensor_scalar
                wait_x(pool, name)
                pool.dma_start(sm_steps[:, :], A["c_steps"]).then_inc(S["sm_consts"], 16)
                pool.dma_start(sm_parity[:, :], A["c_parity"]).then_inc(S["sm_consts"], 16)
                pool.wait_ge(S["sm_consts"], 32)
                pool.wait_ge(S["sm_par_ready"], 1)
                for g in range(8):
                    js = slice(4 * g, 4 * g + 4)
                    steps = sm_steps[:, :].unsqueeze(1).to_broadcast([P, 4, TC])
                    part = lambda k: sm_par[:, k, js].unsqueeze(2).to_broadcast([P, 4, TC])
                    a, b, c = sm_sin[:, js, :], sm_t[:, 0, :, :], sm_t[:, 1, :, :]
                    tt(c, steps, part(5), ALU.mult)
                    link(tt(a, steps, part(4), ALU.mult))
                    link(ts(b, a, ROUND, ROUND, ALU.add, ALU.subtract))
                    link(tt(a, a, b, ALU.subtract))
                    link(tt(a, a, c, ALU.add))
                    link(ts(b, a, ROUND, ROUND, ALU.add, ALU.subtract))
                    ins = tt(a, a, b, ALU.subtract)
                    ins.then_inc(S["sm_turns"], 1)
                    pool.wait_ge(S["sm_turns"], g + 1)
                pool.wait_ge(S["acc_dve"], dves[b0 + NFB])
                pool.wait_ge(S["tp_full"], stage[name]["tg"] + 4 + NFB)
                for dst, src in [
                    (sm_b[:, 0, :, :], A["ssm_b_re_2"][0].rearrange("(j g) s c -> (g s) j c", g=2)),
                    (sm_b[:, 1, :, :], A["ssm_b_im_2"][0].rearrange("(j g) s c -> (g s) j c", g=2)),
                    (sm_c[:, 0, :, :], A["ssm_c_re_2"][0].rearrange("(k g) c s -> (g c) k s", k=DK)),
                    (sm_c[:, 1, :, :], A["ssm_c_im_2"][0].rearrange("(k g) c s -> (g c) k s", k=DK)),
                ]:
                    pool.dma_start(dst, src).then_inc(S["sm_bc_landed"], 16)
                pool.wait_ge(S["sm_bc_landed"], 64)
                fb = lambda k: sm_par[:, k, :].unsqueeze(2).to_broadcast([P, NJ, GCH])
                br, bi = sm_b[:, 0, :, :], sm_b[:, 1, :, :]
                t1, t2 = [sm_t[:, k, :, :].rearrange("p a t -> p (a t)").rearrange("p (j c) -> p j c", c=GCH)
                          for k in range(2)]
                tt(t1, bi, fb(3), ALU.mult)
                link(tt(t2, br, fb(3), ALU.mult))
                tt(br, br, fb(2), ALU.mult)
                link(tt(bi, bi, fb(2), ALU.mult))
                tt(br, br, t1, ALU.subtract)
                link(tt(bi, bi, t2, ALU.add))
                pool.wait_ge(S["unit_used"], u0 + NFB * (DK // 2))
                for r in range(2):
                    bd = sm_bd[r].rearrange("p (j g c) -> p j g c", j=NJ, g=2)
                    cd = sm_cd[r].rearrange("p (k g s) -> p k g s", k=DK, g=2)
                    for g in range(2):
                        ts(bd[:, :, g, :], sm_b[:, r, :, :], sm_parity[:, 2 + g:3 + g], None, ALU.mult)
                    for g in range(2):
                        ins = ts(cd[:, :, g, :], sm_c[:, r, :, :], sm_parity[:, g:g + 1], None, ALU.mult)
                ins.then_inc(S["sm_blocks"], 1)

            def run_ssm():
                half = NJ // 2
                tt = nc.gpsimd.tensor_tensor

                def carry(s):
                    js = slice(tiles_of(s)[0], tiles_of(s)[1] + 1, NJ // DK)
                    pool.wait_ge(S["sm_states"], s + 1)
                    xa, xb = sm_x[:, s % 2, 0, :, :, TC - 1], sm_x[:, s % 2, 1, :, :, TC - 1]
                    tt(sm_carry[:, js, 0], xa[:, :, 0], xb[:, :, 1], ALU.subtract)
                    tt(sm_carry[:, js, 1], xa[:, :, 1], xb[:, :, 0], ALU.add).then_inc(S["sm_carried"], 1)

                for s in range(MT * half):
                    pool.wait_ge(S["sm_read"], s + 1)
                    a, b = sm_a[:, s % 2, :, :, :], sm_z[:, s % 2, :, :, :]
                    tt(a[:, :, 0, :], a[:, :, 0, :], b[:, :, 1, :], ALU.add)
                    tt(a[:, :, 1, :], a[:, :, 1, :], b[:, :, 0, :], ALU.subtract).then_inc(S["sm_framed"], 1)
                    if 1 <= s <= half:
                        carry(s - 1)

            for name in STAGES:
                st = stage[name]
                if name == "ffnb2":
                    prepare_ssm(name)
                if name == "even":
                    wait_x(pool, name)
                    pool.memset(ev_lrT[:, :], 1.0).then_inc(S["ev_cleared"], 1)
                    pool.memset(ev_sc[:, :, :, :], 0.0).then_inc(S["ev_cleared"], 1)
                    for dst, src in [
                        (ev_gw[0:GATE_RANK, :], A["gla_gate_w"][0]),
                        (ev_gw[GATE_RANK:GATE_RANK + 1, :], A["gla_gate_b"]),
                        (ev_c[:, :], A["c_gla"]),
                        (ev_keep[:, :], A["c_keep"]),
                        (ev_pw[:, :, :, :], A["c_pool"]),
                        (ev_pm[:, :, :], A["pool_w"][0].rearrange("g c d -> c g d")),
                    ]:
                        pool.dma_start(dst, src).then_inc(S["ev_landed"], 16)
                if name == "odd":
                    wait_x(pool, name)
                    pool.memset(od_fill[:, :], BARRED).then_inc(S["od_cleared"], 1)
                    pool.memset(od_neg[:, :], NEG).then_inc(S["od_cleared"], 1)
                    pool.dma_start(od_bar[:, :, :], A["c_barred"]).then_inc(S["od_landed"], 16)
                if name == "diff":
                    wait_x(pool, name)
                    pool.dma_start(df_flip[:, :], A["c_flip"]).then_inc(S["df_landed"], 16)
                    for hd in range(DIFF_HEADS):
                        if hd >= 2:
                            pool.wait_ge(S["df_scores"], MT * (hd - 1))
                        src = bass.AP(rel_scratch.tensor, 2 * hd * RELN, [[1, P], [RELN, 2], [1, SEQ]])
                        pool.dma_start(df_b[:, hd % 2, :, :], src).then_inc(S[f"df_bias{hd % 2}"], 16)
                if name.startswith("ple"):
                    wait_x(pool, name)
                    pool.dma_start(pl_p[:, :, :], A["p_2"][int(name[3])].rearrange("b (m p) c -> p (b m) c", p=P)
                                   ).then_inc(S["pl_landed"], 16)
                if name == "ssm":
                    wait_x(pool, name)
                    pool.wait_ge(S["sm_blocks"], 1)
                    pool.dma_start(sm_bg[:, :], spread(A["ssm_b_glu_2"][0], 2 * D)).then_inc(S["sm_bias"], 16)
                if name in ROW_GAINS:
                    row_gain(name)
                if name == "ssm":
                    run_ssm()

        @with_block.tensor
        def _(pe):
            mm = nc.tensor.matmul

            def unit(u, b, lhs_hi, lhs_lo, i=0, per=0, per_b=0, da=0, dd=0):
                _, k, kn, _, cn = units[u]
                if k == 0 and b >= 2:
                    if acts[b - 1]:
                        pe.wait_ge(S["acc_act"], acts[b - 1] + da * i)
                    if dves[b - 1]:
                        pe.wait_ge(S["acc_dve"], dves[b - 1] + dd * i)
                pe.wait_ge(S["w_split"], u + 1 + per * i)
                first_u = u if k == 0 else u - k_at(u)
                last = u + 1 == len(units) or units[u + 1][1] == 0
                for kk in range(kn):
                    hi, lo = slot(w_hi, u)[:, kk, :], slot(w_lo, u)[:, kk, :]
                    for m in range(MT):
                        o = acc[:, 2 * (b % 2) + m, 0:cn]
                        toks = slice(m * P, (m + 1) * P)
                        end = last and kk == kn - 1
                        mm(o, lhs_hi[:, k + kk, toks], hi, start=(k + kk == 0), stop=False)
                        mm(o, lhs_hi[:, k + kk, toks], lo, start=False, stop=False)
                        ins = mm(o, lhs_lo[:, k + kk, toks], hi, start=False, stop=end)
                ins.then_inc(S["unit_used"], 1)

            def k_at(u):
                n = 0
                while units[u - n][1]:
                    n += 1
                return n

            def linear(name, lhs_hi, lhs_lo, tg_need):
                u, b = first[name]
                kn, cols, a, d = LINEAR[name]
                blocks = [v for v in range(u, u + len(units)) if v < len(units) and units[v][0] == name and units[v][1] == 0]
                n = len(k_groups(kn))

                def one(u, b, need, i=0, per=0, per_b=0, da=0, dd=0):
                    for v in range(n):
                        if need:
                            pe.wait_ge(S["tp_lo"], tg_need[v])
                        unit(u + v, b, lhs_hi, lhs_lo, i, per, per_b, da, dd)

                full = sum(units[v][4] == CB for v in blocks)
                loops = (full - 2) // 2 if full > 2 else 0
                for v in range(2):
                    one(u + v * n, b + v, v == 0)
                if loops:
                    with nc.tensor.Fori(0, loops) as i:
                        for v in range(2):
                            one(u + (2 + v) * n, b + 2 + v, False, i, 2 * n, 2, 2 * a, 2 * d)
                for v in range(2 + 2 * loops, len(blocks)):
                    one(u + v * n, b + v, False)

            def turn(dst, src, n=P):
                return nc.tensor.transpose(dst, src, ident[0:n, 0:n])

            def turn_pair(tg, i, per, src, ready):
                ready()
                if tg >= 2:
                    pe.wait_ge(S["tp_lo"], tg - 1 + per * i)
                for j in range(2):
                    for m in range(MT):
                        ins = turn(tp[:, tg % 2, j * SEQ + m * P:j * SEQ + (m + 1) * P], src(j, m))
                ins.then_inc(S["tp_full"], 1)

            def turn_x(name, src=x, sem="x_upd", count=None):
                st = stage[name]
                for kp in range(DK // 2):
                    def ready():
                        if count is not None:
                            pe.wait_ge(S[sem], count)
                        else:
                            wait_x(pe, name, kp // 2)
                    turn_pair(st["tg"] + kp, 0, 0,
                              lambda j, m: src[:, m, (2 * kp + j) * P:(2 * kp + j + 1) * P], ready)

            def setup_rest():
                pe.wait_ge(S["gain0_copied"], 1)
                pe.wait_ge(S["gains_landed"], 16 * 7)
                turn(ms[:, 0, 0:P], gain_rows[:, 0, :])
                turn(ms[:, 0, P:GAIN_ROWS], gain_rows[0:GAIN_ROWS - P, 1, :], GAIN_ROWS - P).then_inc(S["gains_turned"], 1)
                pe.wait_ge(S["setup_landed"], 16 * 5)
                mm(ms[0:2 * DIFF_HEADS, 1, 0:RELN], rel_b[:, :], hot[:, :], start=True, stop=True)
                pe.wait_ge(S["sm_params"], 1)
                for r in range(4):
                    ins = turn(ms[:, 1, RELN + r * NJ:RELN + (r + 1) * NJ], sm_rows[:, r, :], NJ)
                ins.then_inc(S["rel_done"], 1)

            def ffn(name):
                st = stage[name]
                tg, nf = st["tg"], st["nf"]
                u0, b0 = first[name]
                n = DK // 2
                turn_x(name)

                def turn_h(fb, i=0):
                    count = dves[b0 + fb + 1]
                    turn_pair(tg + 4 + fb, i, 2, lambda j, m: h[:, fb % 2, m, j * P:(j + 1) * P],
                              lambda: pe.wait_ge(S["acc_dve"], count + 2 * MT * i))

                for v in range(n):
                    pe.wait_ge(S["tp_lo"], tg + v + 1)
                    unit(u0 + v, b0, xT_hi, xT_lo)
                if STAGES[0] == name:
                    setup_rest()
                with nc.tensor.Fori(0, (NFB - 1) // 2) as i:
                    for j in range(2):
                        fb = 1 + j
                        for v in range(n):
                            if v == 2:
                                turn_h(fb - 1, i)
                            unit(u0 + fb * n + v, b0 + fb, xT_hi, xT_lo, i, 2 * n, 2, 2 * MT, 2 * MT)
                u1, b1 = u0 + NFB * n, b0 + NFB
                per_cb = len(k_groups(FK))
                for cb in range(DB):
                    for v in range(per_cb):
                        if cb == 0:
                            if v == 1:
                                turn_h(NFB - 1)
                            k_last = units[u1 + v][1] + units[u1 + v][2] - 1
                            pe.wait_ge(S["tp_lo"], tg + 4 + k_last // 2 + 1)
                        unit(u1 + cb * per_cb + v, b1 + cb, hT_hi, hT_lo)

            def emptied(b):
                pe.wait_ge(S["acc_act"], acts[b])
                pe.wait_ge(S["acc_dve"], dves[b])

            def even(name):
                st = stage[name]
                tg = st["tg"]
                turn_x(name)
                linear("even_in", xT_hi, xT_lo, [tg + v + 1 for v in range(4)])
                emptied(first["even_in"][1] + 5)
                pe.wait_ge(S["ev_landed"], 96)
                for g in range(4):
                    for t in range(MT):
                        ins = mm(acc[:, g // 2, (g % 2) * SEQ:(g % 2 + 1) * SEQ],
                                 ev[:, t, U_AT + g * P:U_AT + (g + 1) * P], ev_pw[:, g, t, :],
                                 start=(t == 0), stop=(t == MT - 1))
                    if g % 2:
                        ins.then_inc(S["ev_pooled"], 1)
                for m in range(MT):
                    ins = turn(ms[0:GATE_RANK, 0, m * P:(m + 1) * P], ev[:, m, LR_AT:LR_AT + GATE_RANK])
                ins.then_inc(S["ev_lr_turned"], 1)
                pe.wait_ge(S["ev_lr_copied"], 1)
                for m in range(MT):
                    ins = mm(ms[:, 1, m * GLA_QK:(m + 1) * GLA_QK], ev_lrT[:, m * P:(m + 1) * P], ev_gw[:, :],
                             start=True, stop=True)
                ins.then_inc(S["ev_gated"], 1)
                for gp in range(2):
                    pe.wait_ge(S["ev_pool_copied"], gp + 1)
                    pe.wait_ge(S["tp_lo"], tg + 4 + gp - 1)
                    for j in range(2):
                        g = 2 * gp + j
                        ins = mm(tp[:, (tg + 4 + gp) % 2, j * SEQ:(j + 1) * SEQ], ev_pm[:, g, :], ev_pT[:, g, :],
                                 start=True, stop=True)
                    ins.then_inc(S["tp_full"], 1)
                pe.wait_ge(S["ev_decays"], 1)
                for f in range(3):
                    for m in range(MT):
                        ins = mm(acc[:, f, m * GLA_QK:(m + 1) * GLA_QK], ev_c[:, f * P:(f + 1) * P], ev_la[:, m, :],
                                 start=True, stop=True)
                    ins.then_inc(S["ev_summed"], 1)
                for hp in range(2):
                    for m in range(MT):
                        ins = mm(ms[:, 0, hp * 4 + 2 * m:hp * 4 + 2 * m + 2], ev_la[:, m, hp * P:(hp + 1) * P],
                                 ev_c[:, 3 * P:3 * P + 2], start=True, stop=True)
                ins.then_inc(S["ev_summed"], 1)
                for f in range(3):
                    pe.wait_ge(S["ev_scaled"], f + 1)
                    pe.wait_ge(S["ev_exp"], (2, 3, 4)[f])
                    for hp in range(2):
                        for m in range(MT):
                            ins = turn(acc[:, f, hp * SEQ + m * P:hp * SEQ + (m + 1) * P],
                                       ev_s[:, f, m, hp * P:(hp + 1) * P])
                    ins.then_inc(S["ev_turned"], 1)
                pe.wait_ge(S["ev_scaled"], 4)
                for hd in range(GLA_HEADS):
                    half = slice((hd % 2) * 64, (hd % 2) * 64 + 64)
                    for c in range(3):
                        rows = slice((c % 2) * 64, (c % 2) * 64 + 64)
                        ins = mm(state_part(hd // 2, c)[half, :], ev_s[rows, 3, c // 2, hd * 64:(hd + 1) * 64],
                                 ev[rows, c // 2, V_AT + hd * P:V_AT + (hd + 1) * P], start=True, stop=True,
                                 skip_group_check=True)
                ins.then_inc(S["ev_added"], 1)
                pe.wait_ge(S["ev_T_copied"], 2)
                for m in range(MT):
                    for hd in range(GLA_HEADS):
                        half = slice((hd % 2) * 64, (hd % 2) * 64 + 64)
                        for c in range(2):
                            toks = slice(m * P + c * 64, m * P + c * 64 + 64)
                            at = of_head(m, hd) + c * 64
                            ins = mm(acc[c * 64:c * 64 + 64, hd % 2, at:at + 64],
                                     ev_T[half, 1, hd // 2, toks], ev_T[half, 0, hd // 2, toks],
                                     start=True, stop=True, skip_group_check=True)
                ins.then_inc(S["ev_scores"], 1)
                pe.wait_ge(S["ev_T_copied"], 3)
                pe.wait_ge(S["ev_state"], 6)
                pe.wait_ge(S["ev_masked"], 4)
                for m in range(MT):
                    for hd in range(GLA_HEADS):
                        half = slice((hd % 2) * 64, (hd % 2) * 64 + 64)
                        o = acc[:, 2 + hd % 2, of_head(m, hd):of_head(m, hd) + P]
                        ins = mm(o, ev_sc[:, m, hd, :], ev[:, m, V_AT + hd * P:V_AT + (hd + 1) * P],
                                 start=True, stop=False, skip_group_check=True)
                        for c in range(2):
                            if 2 * m + c:
                                ins = mm(o[c * 64:c * 64 + 64, :],
                                         ev_T[half, 2, hd // 2, m * P + c * 64:m * P + c * 64 + 64],
                                         ev_st[half, 2 * m + c - 1, hd // 2, :],
                                         start=False, stop=True, skip_group_check=True)
                ins.then_inc(S["ev_out"], 1)
                for kp in range(2):
                    turn_pair(tg + 6 + kp, 0, 0, lambda j, m: ev_o[:, m, (2 * kp + j) * P:(2 * kp + j + 1) * P],
                              lambda: pe.wait_ge(S["ev_normed"], MT * GLA_HEADS))
                linear("even_out", xT_hi, xT_lo, [tg + 8] * 4)

            def odd(name):
                st = stage[name]
                tg = st["tg"]
                turn_x(name)
                linear("odd_in", xT_hi, xT_lo, [tg + v + 1 for v in range(4)])
                emptied(first["odd_in"][1] + 4)
                def turned(f):
                    bank = f % 4
                    if f >= 4:
                        pe.wait_ge(S["od_T_copied"], f - 3)
                    for j in range(2):
                        for m in range(MT):
                            dst = acc[:, bank, j * SEQ + m * P:j * SEQ + (m + 1) * P]
                            if f == 0:
                                ins = turn(dst, od_ri[:, m, 2 * j:2 * j + 2, :].rearrange("p a b -> p (a b)"))
                            elif f == 1:
                                if j:
                                    continue
                                ins = turn(dst, od_ri[:, m, 4:6, :].rearrange("p a b -> p (a b)"))
                            elif f == 2:
                                ins = turn(dst, od_r[:, m, ATT_HEADS + j, :])
                            else:
                                ins = turn(dst, od_r[:, m, 2 * (f - 3) + j, :])
                    ins.then_inc(S["od_turned"], 1)

                pe.wait_ge(S["od_roped"], 1)
                turned(0)
                turned(1)
                pe.wait_ge(S["od_T_copied"], 2)
                for m in range(MT):
                    n = (m + 1) * P
                    if m:
                        pe.wait_ge(S["od_relu"], 2)
                    for hd in range(IDX_HEADS):
                        half = slice((hd % 2) * 64, (hd % 2) * 64 + 64)
                        ins = mm(ms[:, hd % 2, (hd // 2) * SEQ:(hd // 2) * SEQ + n],
                                 od_qiT[half, hd // 2, m * P:(m + 1) * P], od_kiT[half, 0:n],
                                 start=True, stop=True, skip_group_check=True)
                    ins.then_inc(S["od_logits"], 1)
                pe.wait_ge(S["od_roped"], 2)
                for f in range(2, 7):
                    turned(f)

                def scores(s):
                    hp, m = s // 2, s % 2
                    n = (m + 1) * P
                    if s >= 2:
                        pe.wait_ge(S["od_scored"], 2 * (s - 1))
                    for j in range(2):
                        ins = mm(acc[:, s % 2, j * SEQ:j * SEQ + n], od_qT[:, hp, j, m * P:(m + 1) * P],
                                 od_kT[:, hp // 2, 0:n], start=True, stop=True, skip_group_check=True)
                    ins.then_inc(S["od_scores"], 1)

                def turn_probs(s):
                    m = s % 2
                    pe.wait_ge(S["od_probs"], s + 1)
                    if s >= 2:
                        pe.wait_ge(S["od_pT_copied"], s - 1)
                    for j in range(2):
                        for t in range(m + 1):
                            ins = turn(acc[:, 2 + s % 2, (j * (m + 1) + t) * P:(j * (m + 1) + t + 1) * P],
                                       od_p[:, s % 2, j, t * P:(t + 1) * P])
                    ins.then_inc(S["od_pT_turned"], 1)

                def values(s):
                    hp, m = s // 2, s % 2
                    g = tg + 4 + hp
                    pe.wait_ge(S["od_pT_copied"], s + 1)
                    if m == 0:
                        pe.wait_ge(S["tp_lo"], g - 1)
                    for j in range(2):
                        for t in range(m + 1):
                            ins = mm(tp[:, g % 2, j * SEQ + m * P:j * SEQ + (m + 1) * P],
                                     od[:, t, ATT_V + (hp // 2) * HD:ATT_V + (hp // 2 + 1) * HD],
                                     od_pT[:, s % 2, (j * (m + 1) + t) * P:(j * (m + 1) + t + 1) * P],
                                     start=(t == 0), stop=(t == m), skip_group_check=True)
                    ins.then_inc(S["tp_full"] if m else S["od_half"], 1)

                steps = 2 * ATT_HEADS // 2
                pe.wait_ge(S["od_T_copied"], 7)
                scores(0)
                for s in range(steps):
                    if s + 1 < steps:
                        scores(s + 1)
                    turn_probs(s)
                    if s:
                        values(s - 1)
                values(steps - 1)
                linear("odd_out", xT_hi, xT_lo, [tg + 4 + v + 1 for v in range(4)])

            def diff(name):
                st = stage[name]
                tg = st["tg"]
                turn_x(name)
                linear("qkv", xT_hi, xT_lo, [tg + v + 1 for v in range(4)])
                emptied(first["qkv"][1] + 6)
                for f in range(8):
                    if f >= 4:
                        pe.wait_ge(S["df_T_copied"], f - 3)
                    for j in range(2):
                        hd = 2 * (f % 4) + j
                        for m in range(MT):
                            ins = turn(acc[:, f % 4, j * SEQ + m * P:j * SEQ + (m + 1) * P],
                                       df[:, m, (f // 4) * D + hd * P:(f // 4) * D + (hd + 1) * P])
                    ins.then_inc(S["df_turned"], 1)

                def scores(s):
                    hd, m = s // 2, s % 2
                    n = (m + 1) * P
                    if s >= 2:
                        pe.wait_ge(S["df_exp"], 2 * (s - 1))
                    for j in range(2):
                        half = slice(j * 64, j * 64 + 64)
                        mm(acc[:, 2 * (s % 2) + j, 0:n], df_qT[half, hd, m * P:(m + 1) * P],
                           df_kT[half, hd, 0:n], start=True, stop=False, skip_group_check=True)
                    if s == 0:
                        pe.wait_ge(S["df_landed"], 16)
                    if m == 0:
                        pe.wait_ge(S[f"df_bias{hd % 2}"], 16 * (hd // 2 + 1))
                    for j in range(2):
                        ins = mm(acc[:, 2 * (s % 2) + j, 0:n], df_flip[:, :], df_b[:, hd % 2, j, SEQ - n:SEQ],
                                 start=False, stop=True, skip_group_check=True)
                    ins.then_inc(S["df_scores"], 1)

                def turn_probs(s):
                    m = s % 2
                    pe.wait_ge(S["df_probs"], s + 1)
                    if s >= 2:
                        pe.wait_ge(S["df_pT_copied"], s - 1)
                    for t in range(m + 1):
                        ins = turn(tp[:, s % 2, t * P:(t + 1) * P], df_a[:, s % 2, t * P:(t + 1) * P])
                    ins.then_inc(S["df_pT_turned"], 1)

                def values(s):
                    hd, m = s // 2, s % 2
                    pe.wait_ge(S["df_pT_copied"], s + 1)
                    if m == 0 and hd >= 2:
                        pe.wait_ge(S["df_o_copied"], hd - 1)
                    for t in range(m + 1):
                        ins = mm(ms[:, hd % 2, m * P:(m + 1) * P], df_pT[:, s % 2, t * P:(t + 1) * P],
                                 df[:, t, 2 * D + hd * P:2 * D + (hd + 1) * P],
                                 start=(t == 0), stop=(t == m), skip_group_check=True)
                    ins.then_inc(S["df_out"], 1)

                steps = 2 * DIFF_HEADS
                pe.wait_ge(S["df_T_copied"], 8)
                scores(0)
                for s in range(steps):
                    if s + 1 < steps:
                        scores(s + 1)
                    turn_probs(s)
                    if s:
                        values(s - 1)
                values(steps - 1)
                for kp in range(4):
                    turn_pair(tg + 4 + kp, 0, 0, lambda j, m: df_o[:, m, (2 * kp + j) * P:(2 * kp + j + 1) * P],
                              lambda: pe.wait_ge(S["df_normed"], 1))
                linear("w_o", xT_hi, xT_lo, [tg + 4 + v + 1 for v in range(4)])

            def ple(name):
                st = stage[name]
                tg = st["tg"]
                n = name[3]
                turn_x(name)
                linear("gate" + n, xT_hi, xT_lo, [tg + v + 1 for v in range(4)])
                turn_pair(tg + 4, 0, 0, lambda j, m: pl_p[:, m, j * P:(j + 1) * P],
                          lambda: pe.wait_ge(S["pl_landed"], 16 * (int(n) + 1)))
                linear("ple" + n, pl_hi, pl_lo, [tg + 5])

            def ssm(name):
                st = stage[name]
                tg = st["tg"]
                pe.wait_ge(S["sm_blocks"], 1)
                emptied(first["glu"][1])
                for r in range(2):
                    for k in range(DK):
                        if r and k == 0:
                            pe.wait_ge(S["sm_BT_copied"], 2)
                        ins = turn(acc[:, k // 4, (k % 4) * P:(k % 4 + 1) * P], sm_bd[r][:, k * P:(k + 1) * P])
                    ins.then_inc(S["sm_b_turned"], 1)
                    for k in range(DK):
                        if r and k == 0:
                            pe.wait_ge(S["sm_CT_copied"], 4)
                        ins = turn(acc[:, 2 + k // 4, (k % 4) * P:(k % 4 + 1) * P], sm_cd[r][:, k * P:(k + 1) * P])
                    ins.then_inc(S["sm_c_turned"], 1)
                turn_x(name, y, "sm_xn", MT)
                pe.wait_ge(S["tp_lo"], tg + 4)
                pe.wait_ge(S["tp_hi"], tg + 4)
                pe.wait_ge(S["sm_BT_copied"], 4)
                pe.wait_ge(S["sm_CT_copied"], 6)

                def inputs(s):
                    c, jp = divmod(s, NJ // 2)
                    if s >= 4:
                        pe.wait_ge(S["sm_read"], s - 3)
                    for jj, j in enumerate(tiles_of(jp)):
                        rows = slice(32 * (j % 4), 32 * (j % 4) + 32)
                        for r in range(2):
                            ins = mm(acc[:, s % 4, (2 * jj + r) * TC:(2 * jj + r + 1) * TC],
                                     sm_BT[rows, r, j // 4, :], sm_hT[rows, j // 4, c * TC:(c + 1) * TC],
                                     start=True, stop=True, skip_group_check=True,
                                     tile_position=(32 * (j % 4), 0))
                    ins.then_inc(S["sm_bu"], 1)

                def outputs(s):
                    c, jp = divmod(s, NJ // 2)
                    pe.wait_ge(S["sm_states"], s + 1)
                    if jp % 8 == 0 and c:
                        pe.wait_ge(S["sm_y_read"], jp // 8 + 1)
                    for jj, j in enumerate(tiles_of(jp)):
                        k = j // 4
                        o = ms[32 * (j % 4):32 * (j % 4) + 32, k // 4, (k % 4) * TC:(k % 4 + 1) * TC]
                        xa, xb = sm_x[:, s % 2, 0, jj, :, :], sm_x[:, s % 2, 1, jj, :, :]
                        for n, (part, v) in enumerate([(0, xa[:, 0, :]), (2, xb[:, 1, :]), (1, xa[:, 1, :]), (1, xb[:, 0, :])]):
                            ins = mm(o, sm_CT[:, part, j, :], v, start=(n == 0), stop=(n == 3),
                                     skip_group_check=True, tile_position=(0, 32 * (j % 4)))
                    ins.then_inc(S["sm_out"], 1)

                steps = MT * NJ // 2
                ahead = 3
                for s in range(ahead):
                    inputs(s)
                for s in range(steps):
                    if s + ahead < steps:
                        inputs(s + ahead)
                    outputs(s)
                pe.wait_ge(S["sm_g_split"], 4)
                linear("glu", xT_hi, xT_lo, [tg + 4] * 4)

            pe.wait_ge(S["ident_landed"], 16)
            pe.wait_ge(S["gain0_landed"], 16)
            turn(ms[:, 0, 0:16], gain_rows[0:16, 0, :], 16).then_inc(S["gain0_turned"], 1)
            for name in STAGES:
                kind = name.rstrip("0123456789")
                if kind in ("ffna", "ffnb"):
                    ffn(name)
                elif kind != "final":
                    {"even": even, "odd": odd, "diff": diff, "ple": ple, "ssm": ssm}[kind](name)

        @with_block.scalar
        def _(act):
            f = nc.scalar.activation

            def split(u, i=0, per=0):
                if u >= len(units):
                    return
                act.wait_ge(S[f"w_landed{u % RING}"], 32 * (u // RING + 1) + 32 * (per // RING) * i)
                if u >= RING:
                    act.wait_ge(S["unit_used"], u - RING + 1 + per * i)
                f(flat(w_hi, u), flat(raw, u), ACT.Copy).then_inc(S["w_rounded"], 1)

            def pair_hi(tg, dst, i=0, per=0, gains=None, base=0):
                act.wait_ge(S["tp_full"], tg + 1 + per * i)
                bank = tp[:, tg % 2, :]
                if gains is None:
                    f(dst, bank, ACT.Copy).then_inc(S["tp_hi"], 1)
                elif gains == "same":
                    f(dst, bank, ACT.Copy, scale=gT[:, base:base + 1]).then_inc(S["tp_hi"], 1)
                else:
                    for j in range(2):
                        ins = f(dst[:, j * SEQ:(j + 1) * SEQ], bank[:, j * SEQ:(j + 1) * SEQ], ACT.Copy,
                                scale=gT[:, base + j:base + j + 1])
                    ins.then_inc(S["tp_hi"], 1)

            def hi_x(name):
                for kp in range(4):
                    pair_hi(stage[name]["tg"] + kp, pair(xT_hi, 2 * kp), gains="each",
                            base=gain_row(name) + 2 * kp)

            def norm_in_front(name):
                st = stage[name]
                n = st["pre"]
                wait_x(act, name)
                for m in range(MT):
                    ins = f(y[:, m, :], x[:, m, :], ACT.Square, scale=D ** -0.5, accum_out=ss[:, n, m, 0:1])
                ins.then_inc(S["ss_ready"], 1)
                act.wait_ge(S["ss_ready"], st["npre"] + 1)
                f(std[:, n, :], ss[:, n, :, 0], ACT.Sqrt, bias=EPS).then_inc(S["std_ready"], 1)

            def norm_behind(name, half):
                st = stage[name]
                act.wait_ge(S["var_ready"], st["npost"] + 1)
                f(std[:, st["post"], :], ss[:, st["post"], :, 0], ACT.Sqrt,
                  scale=4.0 if half else 1.0).then_inc(S["std_ready"], 1)

            def linear(name, evac):
                u, b = first[name]
                kn, cols, _, _ = LINEAR[name]
                n = len(k_groups(kn))
                for blk in range(-(-cols // CB)):
                    for v in range(n):
                        if v == n - 1:
                            evac(blk, b + blk, u + blk * n + n)
                        split(u + blk * n + v + RING)

            def front(dst, nn):
                def evac(blk, b, used):
                    act.wait_ge(S["unit_used"], used)
                    act.wait_ge(S["rstd_ready"], nn + 1)
                    cn = min(CB, dst.shape[2] - blk * CB)
                    f(dst[:, 0, blk * CB:blk * CB + cn], acc[:, 2 * (b % 2), 0:cn], ACT.Copy,
                      scale=rstd[:, nn, 0:1]).then_inc(S["acc_act"], 1)
                return evac

            def squares_behind(nn):
                def evac(blk, b, used):
                    act.wait_ge(S["unit_used"], used)
                    if blk:
                        act.wait_ge(S["acc_act"], acts[b])
                    for m in range(MT):
                        f(ms[:, m, :], acc[:, 2 * (b % 2) + m, :], ACT.Square, scale=D ** -0.5,
                          accum_out=ss[:, nn, m, blk:blk + 1]).then_inc(S["acc_act"], 1)
                return evac

            def setup_rest():
                act.wait_ge(S["sm_landed"], 16 * 3)
                f(sm_dt[:, 1, :], sm_dt[:, 0, :], ACT.Exp).then_inc(S["sm_a1"], 1)
                act.wait_ge(S["lam_summed"], 1)
                f(lam_s[:, 2:4], lam_s[:, 0:2], ACT.Exp).then_inc(S["lam_exp"], 1)
                act.wait_ge(S["sm_v1"], 1)
                f(sm_rows[:, 4, :], sm_rows[:, 2, :], ACT.Exp).then_inc(S["sm_a1"], 1)
                act.wait_ge(S["sm_v1"], 2)
                f(sm_rows[:, 6, :], sm_rows[:, 5, :], ACT.Abs).then_inc(S["sm_a1"], 1)
                act.wait_ge(S["sm_a1"], 3)
                f(sm_rows[:, 8, :], sm_rows[:, 5, :], ACT.Sin).then_inc(S["sm_a1"], 1)
                f(sm_rows[:, 7, :], sm_rows[:, 6, :], ACT.Sin, scale=-1.0, bias=math.pi / 2).then_inc(S["sm_a1"], 1)
                act.wait_ge(S["reduced"], 1)
                f(trig[:, 1, :, :], red[:, 0, :, :], ACT.Sin).then_inc(S["trig_ready"], 1)
                f(red[:, 1, :, :], red[:, 0, :, :], ACT.Abs).then_inc(S["trig_abs"], 1)
                act.wait_ge(S["trig_abs"], 1)
                f(trig[:, 0, :, :], red[:, 1, :, :], ACT.Sin, scale=-1.0, bias=math.pi / 2).then_inc(S["trig_ready"], 1)
                act.wait_ge(S["gains_turned"], 1)
                f(gT[:, :], ms[:, 0, 0:GAIN_ROWS], ACT.Copy).then_inc(S["gains_copied"], 1)
                act.wait_ge(S["gains_copied"], 1)

            def ffn(name):
                st = stage[name]
                tg, nn = st["tg"], st["pre"]
                u0, b0 = first[name]
                behind = st["post"] is not None
                hi_x(name)
                norm_in_front(name)
                act.wait_ge(S["rstd_ready"], nn + 1)

                def silus(fb, i=0):
                    act.wait_ge(S["unit_used"], u0 + 4 * (fb + 1) + 8 * i)
                    if fb:
                        act.wait_ge(S["acc_dve"], dves[b0 + fb] - MT + 2 * MT * i)
                    for m in range(MT):
                        f(silu[:, fb % 2, m, :], acc[:, 2 * ((b0 + fb) % 2) + m, 0:FB], ACT.Silu,
                          scale=rstd[:, nn, m:m + 1]).then_inc(S["acc_act"], 1)

                def turn(fb, i=0, per=0):
                    u = u0 + 4 * fb + RING
                    split(u, i, per)
                    split(u + 1, i, per)
                    if fb:
                        dst = hT_hi[:, bass.ds(2 * (fb - 1) + 4 * i, 2), :] if per else hT_hi[:, 2 * (fb - 1):2 * fb, :]
                        pair_hi(tg + 4 + fb - 1, dst.rearrange("p k t -> p (k t)"), i, 2 if per else 0)
                    split(u + 2, i, per)
                    silus(fb, i)
                    split(u + 3, i, per)

                turn(0)
                if name == STAGES[0]:
                    setup_rest()
                with nc.scalar.Fori(0, (NFB - 3) // 2) as i:
                    for j in range(2):
                        turn(1 + j, i, 8)
                turn(NFB - 2)
                turn(NFB - 1)
                u1, b1 = u0 + 4 * NFB, b0 + NFB
                n = len(k_groups(FK))
                for cb in range(DB):
                    for v in range(n):
                        if cb == 0 and v == 1:
                            pair_hi(tg + 4 + NFB - 1, pair(hT_hi, FK - 2))
                        if v == n - 1 and behind:
                            squares_behind(st["post"])(cb, b1 + cb, u1 + (cb + 1) * n)
                            if cb == DB - 1:
                                norm_behind(name, True)
                        split(u1 + cb * n + v + RING)
                        if name == "ffnb2" and v % 2:
                            ssm_trig((cb * n + v) // 2)

            def ssm_trig(g):
                js = slice(4 * g, 4 * g + 4)
                act.wait_ge(S["sm_turns"], g + 1)
                f(sm_cos[:, js, :], sm_sin[:, js, :], ACT.Abs).then_inc(S["sm_abs"], 1)
                f(sm_sin[:, js, :], sm_sin[:, js, :], ACT.Sin, scale=SAFE_TURN)
                act.wait_ge(S["sm_abs"], g + 1)
                f(sm_cos[:, js, :], sm_cos[:, js, :], ACT.Sin, scale=-SAFE_TURN, bias=math.pi / 2).then_inc(S["sm_trig"], 1)

            def even(name):
                act.wait_ge(S["rel_stored"], 16)
                st = stage[name]
                tg, nn = st["tg"], st["pre"]
                hi_x(name)
                norm_in_front(name)
                linear("even_in", front(ev, nn))
                b = first["even_in"][1]
                act.wait_ge(S["acc_act"], acts[b + 5])
                act.wait_ge(S["acc_dve"], dves[b + 5])
                for gp in range(2):
                    act.wait_ge(S["ev_pooled"], gp + 1)
                    f(pair(ev_pT, 2 * gp), acc[:, gp, :], ACT.Copy).then_inc(S["ev_pool_copied"], 1)
                act.wait_ge(S["ev_gated"], 1)
                t = ev_t[:, :, :].rearrange("p m c -> p (m c)")
                f(t, ms[:, 1, :], ACT.Abs).then_inc(S["ev_soft"], 1)
                act.wait_ge(S["ev_soft"], 1)
                f(t, t, ACT.Exp, scale=-1.0).then_inc(S["ev_soft"], 1)
                act.wait_ge(S["ev_soft"], 2)
                f(t, t, ACT.Ln, bias=1.0).then_inc(S["ev_soft"], 1)
                for e, (bank, sign) in enumerate([(0, 1.0), (0, -1.0), (1, 1.0), (2, 1.0)]):
                    act.wait_ge(S["ev_summed"], bank + 1)
                    f(ev_e[:, e, :, :].rearrange("p m c -> p (m c)"), acc[:, bank, :], ACT.Exp,
                      scale=sign).then_inc(S["ev_exp"], 1)
                act.wait_ge(S["ev_summed"], 4)
                f(ev_dec[:, :, :].rearrange("p a b -> p (a b)"), ms[:, 0, 0:8], ACT.Exp).then_inc(S["ev_exp"], 1)
                for e in range(3):
                    act.wait_ge(S["ev_turned"], e + 1)
                    f(ev_T[:, e, :, :].rearrange("p h t -> p (h t)"), acc[:, e, :], ACT.Copy).then_inc(S["ev_T_copied"], 1)
                for gp in range(2):
                    pair_hi(tg + 4 + gp, pair(xT_hi, 4 + 2 * gp), gains="each", base=GAIN_AT["pool_scale"] + 2 * gp)
                for m in range(MT):
                    f(ev_g[:, m, :], ev[:, m, G_AT:G_AT + GLA_V], ACT.Silu).then_inc(S["ev_silu"], 1)
                act.wait_ge(S["ev_out"], 1)
                for m in range(MT):
                    for hd in range(GLA_HEADS):
                        n = m * GLA_HEADS + hd
                        ins = f(y[:, 0, n * P:(n + 1) * P], acc[:, 2 + hd % 2, of_head(m, hd):of_head(m, hd) + P], ACT.Square, scale=GLA_DV ** -0.5,
                                accum_out=ev_ss[:, 0, n:n + 1])
                    ins.then_inc(S["ev_squared"], 1)
                act.wait_ge(S["ev_squared"], MT)
                f(ev_ss[:, 1, :], ev_ss[:, 0, :], ACT.Sqrt, bias=EPS).then_inc(S["ev_rooted"], 1)
                for kp in range(2):
                    pair_hi(tg + 6 + kp, pair(xT_hi, 2 * kp))
                linear("even_out", lambda *a: None)

            def odd(name):
                st = stage[name]
                tg, nn = st["tg"], st["pre"]
                hi_x(name)
                norm_in_front(name)
                linear("odd_in", front(od, nn))
                dsts = [od_qiT[:, :, :].rearrange("p a b -> p (a b)"), od_kiT[:, :],
                        od_kT[:, :, :].rearrange("p a b -> p (a b)")] + \
                       [od_qT[:, k, :, :].rearrange("p a b -> p (a b)") for k in range(4)]

                def copy(k):
                    act.wait_ge(S["od_turned"], k + 1)
                    n = dsts[k].shape[1]
                    f(dsts[k], acc[:, k % 4, 0:n], ACT.Copy).then_inc(S["od_T_copied"], 1)

                copy(0)
                copy(1)
                for m in range(MT):
                    act.wait_ge(S["od_logits"], m + 1)
                    n = (m + 1) * P
                    for hp in range(2):
                        f(od_rl[:, m, :, :].rearrange("p (a b) s -> p a b s", b=2)[:, :, hp, 0:n],
                          ms[:, hp, :].rearrange("p (h s) -> p h s", h=2)[:, :, 0:n], ACT.Relu,
                          scale=IDX_DIM ** -0.5 * IDX_HEADS ** -0.5).then_inc(S["od_relu"], 1)
                for k in range(2, 7):
                    copy(k)

                def exps(s):
                    m = s % 2
                    n = (m + 1) * P
                    act.wait_ge(S["od_maxed"], s + 1)
                    for j in range(2):
                        f(od_p[:, s % 2, j, 0:n], od_p[:, s % 2, j, 0:n], ACT.Exp,
                          bias=od_mx[:, s, j, 1:2], accum_out=od_mx[:, s, j, 2:3]).then_inc(S["od_exp"], 1)

                def copy_probs(s):
                    n = 2 * (s % 2 + 1) * P
                    act.wait_ge(S["od_pT_turned"], s + 1)
                    f(od_pT[:, s % 2, 0:n], acc[:, 2 + s % 2, 0:n], ACT.Copy).then_inc(S["od_pT_copied"], 1)

                for s in range(8):
                    exps(s)
                    if s:
                        copy_probs(s - 1)
                    if s >= 3 and s % 2:
                        pair_hi(tg + 4 + (s - 3) // 2, pair(xT_hi, s - 3))
                copy_probs(7)
                pair_hi(tg + 7, pair(xT_hi, 6))
                linear("odd_out", lambda *a: None)

            def diff(name):
                st = stage[name]
                tg, nn = st["tg"], st["pre"]
                hi_x(name)
                norm_in_front(name)
                linear("qkv", front(df, nn))
                for k in range(8):
                    act.wait_ge(S["df_turned"], k + 1)
                    f(pair(df_qT if k < 4 else df_kT, 2 * (k % 4)), acc[:, k % 4, :], ACT.Copy).then_inc(S["df_T_copied"], 1)

                def exps(s):
                    m = s % 2
                    n = (m + 1) * P
                    act.wait_ge(S["df_maxed"], s + 1)
                    if s >= 2:
                        act.wait_ge(S["df_probs"], s - 1)
                    for j in range(2):
                        f(df_p[:, s % 2, j, 0:n], acc[:, 2 * (s % 2) + j, 0:n], ACT.Exp, scale=DIFF_DIM ** -0.5,
                          bias=df_mx[:, s, 1, j:j + 1], accum_out=df_mx[:, s, 2, j:j + 1]).then_inc(S["df_exp"], 1)

                def copy_probs(s):
                    n = (s % 2 + 1) * P
                    act.wait_ge(S["df_pT_turned"], s + 1)
                    f(df_pT[:, s % 2, 0:n], tp[:, s % 2, 0:n], ACT.Copy).then_inc(S["df_pT_copied"], 1)

                def squares(hd):
                    act.wait_ge(S["df_out"], 2 * (hd + 1))
                    for m in range(MT):
                        ins = f(y[:, m, hd * P:(hd + 1) * P], ms[:, hd % 2, m * P:(m + 1) * P], ACT.Square, scale=HD ** -0.5,
                                accum_out=df_ss[:, 0, m, hd:hd + 1])
                    ins.then_inc(S["df_squared"], 1)

                for s in range(16):
                    exps(s)
                    if s:
                        copy_probs(s - 1)
                    if s >= 3 and s % 2:
                        squares((s - 3) // 2)
                copy_probs(15)
                squares(7)
                act.wait_ge(S["df_squared"], 8)
                f(df_ss[:, 1, :, :], df_ss[:, 0, :, :], ACT.Sqrt, bias=EPS).then_inc(S["df_rooted"], 1)
                for kp in range(4):
                    pair_hi(tg + 4 + kp, pair(xT_hi, 2 * kp), gains="same", base=GAIN_AT["attn_subln_g_2"])
                linear("w_o", squares_behind(st["post"]))
                norm_behind(name, False)

            def ple(name):
                st = stage[name]
                tg, nn, n = st["tg"], st["pre"], name[3]
                hi_x(name)
                norm_in_front(name)

                def gate(blk, b, used):
                    act.wait_ge(S["unit_used"], used)
                    act.wait_ge(S["rstd_ready"], nn + 1)
                    for m in range(MT):
                        f(pl_g[:, m, blk * CB:(blk + 1) * CB], acc[:, 2 * (b % 2) + m, :], ACT.Sigmoid,
                          scale=rstd[:, nn, m:m + 1]).then_inc(S["acc_act"], 1)

                linear("gate" + n, gate)
                pair_hi(tg + 4, pair(pl_hi, 0))

                def squares(blk, b, used):
                    if blk:
                        act.wait_ge(S["y_squared"], squared_before(name) + MT * blk)
                    for m in range(MT):
                        act.wait_ge(S["acc_dve"], dves[b] + m + 1)
                        f(ms[:, m, :], y[:, m, blk * CB:(blk + 1) * CB], ACT.Square, scale=D ** -0.5,
                          accum_out=ss[:, st["post"], m, blk:blk + 1]).then_inc(S["y_squared"], 1)

                linear("ple" + n, squares)
                norm_behind(name, False)

            def ssm(name):
                st = stage[name]
                tg, nn = st["tg"], st["pre"]
                norm_in_front(name)
                act.wait_ge(S["rstd_ready"], nn + 1)
                f(y[:, 0, :], x[:, 0, :], ACT.Copy, scale=rstd[:, nn, 0:1]).then_inc(S["sm_xn"], 1)
                for r in range(2):
                    act.wait_ge(S["sm_b_turned"], r + 1)
                    for hf in range(2):
                        f(sm_BT[:, r, 4 * hf:4 * hf + 4, :].rearrange("p k s -> p (k s)"), acc[:, hf, :],
                          ACT.Copy).then_inc(S["sm_BT_copied"], 1)
                for kp in range(4):
                    act.wait_ge(S["tp_full"], tg + kp + 1)
                    f(sm_hT[:, 2 * kp, :], tp[:, (tg + kp) % 2, 0:SEQ], ACT.Copy,
                      scale=gT[:, gain_row(name) + 2 * kp:gain_row(name) + 2 * kp + 1]).then_inc(S["tp_hi"], 1)
                for q in range(4):
                    c, hf = q // 2, q % 2
                    act.wait_ge(S["sm_y_read"], q + 1)
                    f(sm_y[:, q % 2, :, :], sm_y[:, q % 2, :, :], ACT.Gelu_apprx_tanh).then_inc(S["sm_gelu"], 1)
                    act.wait_ge(S["sm_gelu"], q + 1)
                    f(xT_hi[:, 4 * hf:4 * hf + 4, c * TC:(c + 1) * TC], sm_y[:, q % 2, :, :],
                      ACT.Copy).then_inc(S["sm_g_hi"], 1)

                def evac(blk, b, used):
                    for m in range(MT):
                        if blk < DB:
                            continue
                        cols = slice((blk - DB) * CB, (blk - DB + 1) * CB)
                        act.wait_ge(S["acc_dve"], dves[b] + m + 1)
                        if blk > DB:
                            act.wait_ge(S["y_squared"], squared_before(name) + MT * (blk - DB))
                        f(z2(m), z2(m), ACT.Sigmoid).then_inc(S["sm_sig"], 1)
                        act.wait_ge(S["sm_prod"], MT * (blk - DB) + m + 1)
                        f(ms[:, m, :], y[:, m, cols], ACT.Square, scale=D ** -0.5,
                          accum_out=ss[:, st["post"], m, blk - DB:blk - DB + 1]).then_inc(S["y_squared"], 1)

                linear("glu", evac)
                norm_behind(name, False)

            def final(name):
                norm_in_front(name)

            for u in range(RING):
                split(u)
            act.wait_ge(S["gain0_turned"], 1)
            f(gT[:, 0:16], ms[:, 0, 0:16], ACT.Copy).then_inc(S["gain0_copied"], 1)
            act.wait_ge(S["gain0_copied"], 1)
            for name in STAGES:
                kind = name.rstrip("0123456789")
                {"ffna": ffn, "ffnb": ffn, "even": even, "odd": odd, "final": final, "diff": diff,
                 "ple": ple, "ssm": ssm}[kind](name)

        @with_block.vector
        def _(dve):
            tt, ts, stt = nc.vector.tensor_tensor, nc.vector.tensor_scalar, nc.vector.scalar_tensor_tensor
            chain = [0]

            def link(ins):
                chain[0] += 1
                ins.then_inc(S["dve_step"], 1)
                dve.wait_ge(S["dve_step"], chain[0])

            def split(u, i=0, per=0):
                if u >= len(units):
                    return
                dve.wait_ge(S["w_rounded"], u + 1 + per * i)
                tt(flat(w_lo, u), flat(raw, u), flat(w_hi, u).bitcast(F32), ALU.subtract).then_inc(S["w_split"], 1)

            def pair_lo(tg, lo, hi, i=0, per=0, gains=None, base=0):
                dve.wait_ge(S["tp_hi"], tg + 1 + per * i)
                bank = tp[:, tg % 2, :]
                hi = hi.bitcast(F32)
                if gains is None:
                    tt(lo, bank, hi, ALU.subtract).then_inc(S["tp_lo"], 1)
                elif gains == "same":
                    stt(lo, bank, gT[:, base:base + 1], hi, ALU.mult, ALU.subtract).then_inc(S["tp_lo"], 1)
                else:
                    for j in range(2):
                        c = slice(j * SEQ, (j + 1) * SEQ)
                        ins = stt(lo[:, c], bank[:, c], gT[:, base + j:base + j + 1], hi[:, c], ALU.mult, ALU.subtract)
                    ins.then_inc(S["tp_lo"], 1)

            def lo_x(name):
                for kp in range(4):
                    pair_lo(stage[name]["tg"] + kp, pair(xT_lo, 2 * kp), pair(xT_hi, 2 * kp), gains="each",
                            base=gain_row(name) + 2 * kp)

            def root(nn):
                dve.wait_ge(S["std_ready"], nn + 1)
                nc.vector.reciprocal(rstd[:, nn, :], std[:, nn, :]).then_inc(S["rstd_ready"], 1)

            def linear(name, evac):
                u, b = first[name]
                kn, cols, _, _ = LINEAR[name]
                n = len(k_groups(kn))
                for blk in range(-(-cols // CB)):
                    for v in range(n):
                        if v == n - 1:
                            evac(blk, b + blk, u + blk * n + n)
                        split(u + blk * n + v + RING)

            def front(dst, nn):
                def evac(blk, b, used):
                    dve.wait_ge(S["unit_used"], used)
                    dve.wait_ge(S["rstd_ready"], nn + 1)
                    cn = min(CB, dst.shape[2] - blk * CB)
                    ts(dst[:, 1, blk * CB:blk * CB + cn], acc[:, 2 * (b % 2) + 1, 0:cn], rstd[:, nn, 1:2], None,
                       ALU.mult).then_inc(S["acc_dve"], 1)
                return evac

            def add_to_x(scale):
                def evac(blk, b, used):
                    dve.wait_ge(S["unit_used"], used)
                    for m in range(MT):
                        xs = x[:, m, blk * CB:(blk + 1) * CB]
                        stt(xs, acc[:, 2 * (b % 2) + m, :], scale, xs, ALU.mult, ALU.add).then_inc(S["acc_dve"], 1)
                return evac

            def gained(name):
                g = stage[name]["gb"]
                def evac(blk, b, used):
                    dve.wait_ge(S[f"gain_landed{g % 2}"], 16 * (g // 2 + 1))
                    cols = slice(blk * CB, (blk + 1) * CB)
                    for m in range(MT):
                        dve.wait_ge(S["acc_act"], acts[b] + m + 1)
                        tt(y[:, m, cols], acc[:, 2 * (b % 2) + m, :], gB[:, g % 2, cols],
                           ALU.mult).then_inc(S["acc_dve"], 1)
                return evac

            def variance(name):
                n = stage[name]["post"]
                stt(ss[:, n, :, 0], ss[:, n, :, 0], EPS, ss[:, n, :, 1], ALU.add, ALU.add).then_inc(S["var_ready"], 1)

            def add_normed(name):
                n = stage[name]["post"]
                root(n)
                dve.wait_ge(S["rstd_ready"], n + 1)
                for m in range(MT):
                    stt(x[:, m, :], y[:, m, :], rstd[:, n, m:m + 1], x[:, m, :], ALU.mult,
                        ALU.add).then_inc(S["x_upd"], 1)

            def gain_y(name):
                g = stage[name]["gb"]
                dve.wait_ge(S[f"gain_landed{g % 2}"], 16 * (g // 2 + 1))
                dve.wait_ge(S["y_squared"], squared_before(name) + 2 * DB)
                variance(name)
                for m in range(MT):
                    ins = tt(y[:, m, :], y[:, m, :], gB[:, g % 2, :], ALU.mult)
                link(ins)

            def setup_rest():
                dve.wait_ge(S["setup_landed"], 16 * 5)
                link(tt(lam_p[:, :, :], lam_v[:, :, 0, :], lam_v[:, :, 1, :], ALU.mult))
                nc.vector.tensor_reduce(lam_s[:, 0:2], lam_p[:, :, :], AX.X, ALU.add).then_inc(S["lam_summed"], 1)
                R = lambda k: sm_rows[:, k, :]
                dve.wait_ge(S["sm_a1"], 1)
                dt = sm_dt[:, 1, :].unsqueeze(2).to_broadcast([NJ, 2, STATES])
                v3 = lambda k: R(k).rearrange("p (g s) -> p g s", g=2)
                tt(v3(2), v3(0), dt, ALU.mult).then_inc(S["sm_v1"], 1)
                link(tt(v3(3), v3(1), dt, ALU.mult))
                link(ts(R(5), R(3), 1 / (2 * math.pi), ROUND, ALU.mult, ALU.add))
                link(ts(R(5), R(5), ROUND, None, ALU.subtract))
                link(stt(R(12), R(5), -TWO_PI[0], R(3), ALU.mult, ALU.add))
                link(stt(R(12), R(5), -TWO_PI[1], R(12), ALU.mult, ALU.add))
                link(stt(R(5), R(5), -TWO_PI[2], R(12), ALU.mult, ALU.add))
                ts(R(5), R(5), -SAFE_PI, SAFE_PI, ALU.max, ALU.min).then_inc(S["sm_v1"], 1)
                dve.wait_ge(S["sm_a1"], 5)
                link(tt(R(9), R(4), R(7), ALU.mult))
                link(ts(R(9), R(9), -1.0, None, ALU.add))
                tt(R(10), R(4), R(8), ALU.mult)
                tt(R(11), R(0), R(0), ALU.mult)
                link(tt(R(12), R(1), R(1), ALU.mult))
                link(tt(R(11), R(11), R(12), ALU.add))
                link(nc.vector.reciprocal(R(11), R(11)))
                tt(R(12), R(9), R(0), ALU.mult)
                link(tt(R(13), R(10), R(1), ALU.mult))
                link(tt(R(12), R(12), R(13), ALU.add))
                tt(R(2), R(12), R(11), ALU.mult)
                link(tt(R(13), R(10), R(0), ALU.mult))
                link(tt(R(12), R(9), R(1), ALU.mult))
                link(tt(R(13), R(13), R(12), ALU.subtract))
                tt(R(3), R(13), R(11), ALU.mult)
                ts(R(1), R(5), 1 / (2 * math.pi), None, ALU.mult)
                nc.vector.tensor_copy(R(0), R(4)).then_inc(S["sm_params"], 1)
                dve.wait_ge(S["lam_exp"], 1)
                link(stt(neg_lam[:, :], lam_s[:, 3:4], -LAMBDA_INIT, lam_s[:, 2:3], ALU.add, ALU.subtract))
                link(nc.vector.tensor_copy(pos[:, :], pos_i[:, :]))
                for m in range(MT):
                    ins = ts(ang[:, m, :], inv[:, :], pos[:, m:m + 1], None, ALU.mult)
                link(ins)
                link(ts(turns[:, 0, :, :], ang[:, :, :], 1 / (2 * math.pi), ROUND, ALU.mult, ALU.add))
                link(ts(turns[:, 1, :, :], turns[:, 0, :, :], ROUND, None, ALU.subtract))
                link(stt(red[:, 0, :, :], turns[:, 1, :, :], -TWO_PI[0], ang[:, :, :], ALU.mult, ALU.add))
                link(stt(red[:, 0, :, :], turns[:, 1, :, :], -TWO_PI[1], red[:, 0, :, :], ALU.mult, ALU.add))
                link(stt(red[:, 0, :, :], turns[:, 1, :, :], -TWO_PI[2], red[:, 0, :, :], ALU.mult, ALU.add))
                ts(red[:, 0, :, :], red[:, 0, :, :], -SAFE_PI, SAFE_PI, ALU.max, ALU.min).then_inc(S["reduced"], 1)
                dve.wait_ge(S["rel_done"], 1)
                nc.vector.tensor_copy(rel_v[:, :], ms[0:2 * DIFF_HEADS, 1, 0:RELN]).then_inc(S["rel_copied"], 1)
                link(nc.vector.tensor_copy(sm_par[:, 0:4, :].rearrange("p a b -> p (a b)"), ms[:, 1, RELN:CB]))
                short = 1.5 * 2.0 ** 10
                link(ts(sm_par[:, 4, :], sm_par[:, 1, :], short, None, ALU.add))
                link(ts(sm_par[:, 4, :], sm_par[:, 4, :], short, None, ALU.subtract))
                tt(sm_par[:, 5, :], sm_par[:, 1, :], sm_par[:, 4, :], ALU.subtract).then_inc(S["sm_par_ready"], 1)
                dve.wait_ge(S["gains_copied"], 1)

            def ffn(name):
                st = stage[name]
                tg, nn = st["tg"], st["pre"]
                u0, b0 = first[name]
                behind = st["post"] is not None
                lo_x(name)
                root(nn)
                dve.wait_ge(S["rstd_ready"], nn + 1)

                def products(fb, i=0):
                    if fb:
                        dve.wait_ge(S["tp_full"], tg + 4 + fb - 1 + 2 * i)
                    for m in range(MT):
                        dve.wait_ge(S["acc_act"], acts[b0 + fb] + m + 1 + 2 * MT * i)
                        stt(h[:, fb % 2, m, :], acc[:, 2 * ((b0 + fb) % 2) + m, FB:CB], rstd[:, nn, m:m + 1],
                            silu[:, fb % 2, m, :], ALU.mult, ALU.mult).then_inc(S["acc_dve"], 1)

                def turn(fb, i=0, per=0):
                    u = u0 + 4 * fb + RING
                    split(u, i, per)
                    split(u + 1, i, per)
                    if fb:
                        def of(t):
                            part = t[:, bass.ds(2 * (fb - 1) + 4 * i, 2), :] if per else t[:, 2 * (fb - 1):2 * fb, :]
                            return part.rearrange("p k t -> p (k t)")
                        pair_lo(tg + 4 + fb - 1, of(hT_lo), of(hT_hi), i, 2 if per else 0)
                    split(u + 2, i, per)
                    products(fb, i)
                    split(u + 3, i, per)

                turn(0)
                if name == STAGES[0]:
                    setup_rest()
                with nc.vector.Fori(0, (NFB - 3) // 2) as i:
                    for j in range(2):
                        turn(1 + j, i, 8)
                turn(NFB - 2)
                turn(NFB - 1)
                u1, b1 = u0 + 4 * NFB, b0 + NFB
                n = len(k_groups(FK))
                for cb in range(DB):
                    for v in range(n):
                        if cb == 0 and v == 1:
                            pair_lo(tg + 4 + NFB - 1, pair(hT_lo, FK - 2), pair(hT_hi, FK - 2))
                        if v == n - 1:
                            (gained(name) if behind else add_to_x(0.5))(cb, b1 + cb, u1 + (cb + 1) * n)
                            if behind and cb == DB - 1:
                                variance(name)
                                add_normed(name)
                        split(u1 + cb * n + v + RING)

            def even(name):
                dve.wait_ge(S["rel_stored"], 16)
                st = stage[name]
                tg, nn = st["tg"], st["pre"]
                lo_x(name)
                root(nn)
                linear("even_in", front(ev, nn))
                b = first["even_in"][1]
                dve.wait_ge(S["acc_act"], acts[b + 5])
                dve.wait_ge(S["acc_dve"], dves[b + 5])
                dve.wait_ge(S["ev_lr_turned"], 1)
                dve.wait_ge(S["ev_cleared"], 2)
                nc.vector.tensor_copy(ev_lrT[0:GATE_RANK, :], ms[0:GATE_RANK, 0, 0:SEQ]).then_inc(S["ev_lr_copied"], 1)
                dve.wait_ge(S["ev_soft"], 3)
                stt(ev_la[:, :, :].rearrange("p m c -> p (m c)"), ms[:, 1, :], 0.0,
                    ev_t[:, :, :].rearrange("p m c -> p (m c)"), ALU.min, ALU.subtract).then_inc(S["ev_decays"], 1)
                for e, (at, scale) in enumerate([(0, GLA_DK ** -0.5), (GLA_QK, 1.0), (0, GLA_DK ** -0.5), (GLA_QK, 1.0)]):
                    dve.wait_ge(S["ev_exp"], e + 1)
                    stt(ev_s[:, e, :, :], ev[:, :, at:at + GLA_QK], scale, ev_e[:, e, :, :], ALU.mult,
                        ALU.mult).then_inc(S["ev_scaled"], 1)
                dve.wait_ge(S["ev_added"], 1)
                dve.wait_ge(S["ev_exp"], 5)
                for c in range(3):
                    if c:
                        dve.wait_ge(S["ev_state"], 2 * c)
                    for hp in range(2):
                        new = state_part(hp, c)
                        if c == 0:
                            ins = nc.vector.tensor_copy(ev_st[:, c, hp, :], new)
                        else:
                            ins = stt(ev_st[:, c, hp, :], ev_st[:, c - 1, hp, :], ev_dec[:, hp, c:c + 1], new,
                                      ALU.mult, ALU.add)
                        ins.then_inc(S["ev_state"], 1)
                dve.wait_ge(S["ev_scores"], 1)
                for odd_heads in range(2):
                    for c in range(2):
                        half = slice(64 * c, 64 * c + 64)
                        nc.vector.copy_predicated(
                            ev_sc[half, :, :, :].rearrange("p m (a b) t -> p (m a) b t", b=2)[:, :, odd_heads, half],
                            ev_keep[half, :].unsqueeze(1).to_broadcast([64, GLA_HEADS, 64]),
                            acc[half, odd_heads, :].rearrange("p (h t) -> p h t", h=GLA_HEADS)[:, :, half],
                        ).then_inc(S["ev_masked"], 1)
                for gp in range(2):
                    pair_lo(tg + 4 + gp, pair(xT_lo, 4 + 2 * gp), pair(xT_hi, 4 + 2 * gp), gains="each",
                            base=GAIN_AT["pool_scale"] + 2 * gp)
                g = st["gb"]
                dve.wait_ge(S[f"gain_landed{g % 2}"], 16 * (g // 2 + 1))
                for m in range(MT):
                    dve.wait_ge(S["ev_silu"], m + 1)
                    ins = tt(ev_g[:, m, :], ev_g[:, m, :], gB[:, g % 2, 0:GLA_V], ALU.mult)
                link(ins)
                dve.wait_ge(S["ev_rooted"], 1)
                link(nc.vector.reciprocal(ev_ss[:, 2, :], ev_ss[:, 1, :]))
                for m in range(MT):
                    for hd in range(GLA_HEADS):
                        c = slice(hd * P, (hd + 1) * P)
                        n = m * GLA_HEADS + hd
                        stt(ev_o[:, m, c], acc[:, 2 + hd % 2, of_head(m, hd):of_head(m, hd) + P], ev_ss[:, 2, n:n + 1], ev_g[:, m, c], ALU.mult,
                            ALU.mult).then_inc(S["ev_normed"], 1)
                for kp in range(2):
                    pair_lo(tg + 6 + kp, pair(xT_lo, 2 * kp), pair(xT_hi, 2 * kp))
                linear("even_out", add_to_x(1.0))

            def rope(dst, src, heads, half, at, t):
                def bc(v):
                    return v.unsqueeze(1).to_broadcast([P, heads, half])
                cos, sin = bc(at[0]), bc(at[1])
                x1, x2 = src[:, :, 0, :], src[:, :, 1, :]
                tt(t[0], x1, cos, ALU.mult)
                tt(t[1], x2, sin, ALU.mult)
                tt(t[2], x2, cos, ALU.mult)
                link(tt(t[3], x1, sin, ALU.mult))
                tt(dst[:, :, 0, :], t[0], t[1], ALU.subtract)
                return tt(dst[:, :, 1, :], t[2], t[3], ALU.add)

            def odd(name):
                st = stage[name]
                tg, nn = st["tg"], st["pre"]
                lo_x(name)
                root(nn)
                linear("odd_in", front(od, nn))
                b = first["odd_in"][1]
                dve.wait_ge(S["acc_act"], acts[b + 4])
                dve.wait_ge(S["acc_dve"], dves[b + 4])
                dve.wait_ge(S["trig_ready"], 2)
                for m in range(MT):
                    half = IDX_DIM // 2
                    ins = rope(od_ri[:, m, 0:5, :].rearrange("p h (a c) -> p h a c", a=2),
                               od[:, m, ATT_QI:ATT_WI].rearrange("p (h a c) -> p h a c", a=2, c=half), IDX_HEADS + 1, half,
                               [trig[:, a, m, HD // 2:96] for a in range(2)],
                               [od_t[:, a, 0:5, 0:half] for a in range(4)])
                    link(ins)
                    ins = nc.vector.tensor_copy(od_ri[:, m, 5, :], od_ri[:, m, 4, :])
                ins.then_inc(S["od_roped"], 1)
                for m in range(MT):
                    half = HD // 2
                    ins = rope(od_r[:, m, :, :].rearrange("p h (a c) -> p h a c", a=2),
                               od[:, m, 0:ATT_V].rearrange("p (h a c) -> p h a c", a=2, c=half), ATT_HEADS + KV_HEADS, half,
                               [trig[:, a, m, 0:half] for a in range(2)], [od_t[:, a, :, :] for a in range(4)])
                    if m == 0:
                        link(ins)
                ins.then_inc(S["od_roped"], 1)
                dve.wait_ge(S["od_landed"], 16)
                dve.wait_ge(S["od_cleared"], 2)
                for m in range(MT):
                    n = (m + 1) * P
                    dve.wait_ge(S["od_relu"], 2 * (m + 1))
                    sc = od_is[:, m, 0:n]
                    for hd in range(IDX_HEADS):
                        wi = od[:, m, ATT_WI + hd:ATT_WI + hd + 1]
                        if hd == 0:
                            link(ts(sc, od_rl[:, m, hd, 0:n], wi, None, ALU.mult))
                        else:
                            link(stt(sc, od_rl[:, m, hd, 0:n], wi, sc, ALU.mult, ALU.add))
                    link(nc.vector.copy_predicated(sc, od_bar[:, m, 0:n], od_fill[:, 0:n]))
                    for r in range(TOPK // 8):
                        link(nc.vector.max(od_m8[:, :], sc))
                        link(nc.vector.match_replace(sc, od_m8[:, :], sc, PICKED))
                    link(ts(sc, sc, (PICKED + BARRED) / 2, NEG, ALU.is_ge, ALU.mult))
                    link(nc.vector.copy_predicated(sc, od_bar[:, m, 0:n], od_neg[:, 0:n]))

                def score(s):
                    m = s % 2
                    n = (m + 1) * P
                    dve.wait_ge(S["od_scores"], s + 1)
                    if s >= 2:
                        dve.wait_ge(S["od_pT_turned"], s - 1)
                    for j in range(2):
                        nc.vector.tensor_tensor_reduce(
                            od_p[:, s % 2, j, 0:n], acc[:, s % 2, j * SEQ:j * SEQ + n], od_is[:, m, 0:n],
                            HD ** -0.5, 2 * NEG, ALU.add, ALU.max, od_mx[:, s, j, 0:1]).then_inc(S["od_scored"], 1)
                    dve.wait_ge(S["od_scored"], 2 * (s + 1))
                    ts(od_mx[:, s, :, 1], od_mx[:, s, :, 0], -1.0, None, ALU.mult).then_inc(S["od_maxed"], 1)

                def normalize(s):
                    n = (s % 2 + 1) * P
                    dve.wait_ge(S["od_exp"], 2 * (s + 1))
                    link(nc.vector.reciprocal(od_mx[:, s, :, 3], od_mx[:, s, :, 2]))
                    for j in range(2):
                        ins = ts(od_p[:, s % 2, j, 0:n], od_p[:, s % 2, j, 0:n], od_mx[:, s, j, 3:4], None, ALU.mult)
                    ins.then_inc(S["od_probs"], 1)

                for s in range(8):
                    score(s)
                    if s:
                        normalize(s - 1)
                    if s >= 3 and s % 2:
                        pair_lo(tg + 4 + (s - 3) // 2, pair(xT_lo, s - 3), pair(xT_hi, s - 3))
                normalize(7)
                pair_lo(tg + 7, pair(xT_lo, 6), pair(xT_hi, 6))
                linear("odd_out", add_to_x(1.0))

            def diff(name):
                st = stage[name]
                tg, nn = st["tg"], st["pre"]
                lo_x(name)
                root(nn)
                linear("qkv", front(df, nn))

                def score(s):
                    hd, m = s // 2, s % 2
                    n = (m + 1) * P
                    dve.wait_ge(S["df_scores"], s + 1)
                    link(nc.vector.tensor_reduce(df_mx[:, s, 0, :], acc[:, 2 * (s % 2):2 * (s % 2) + 2, 0:n], AX.X, ALU.max))
                    ts(df_mx[:, s, 1, :], df_mx[:, s, 0, :], -DIFF_DIM ** -0.5, None, ALU.mult).then_inc(S["df_maxed"], 1)

                def combine(s):
                    n = (s % 2 + 1) * P
                    dve.wait_ge(S["df_exp"], 2 * (s + 1))
                    if s >= 2:
                        dve.wait_ge(S["df_pT_turned"], s - 1)
                    link(nc.vector.reciprocal(df_mx[:, s, 3, :], df_mx[:, s, 2, :]))
                    link(ts(df_mx[:, s, 4, 0:1], df_mx[:, s, 3, 1:2], neg_lam[:, :], None, ALU.mult))
                    link(ts(df_p[:, s % 2, 1, 0:n], df_p[:, s % 2, 1, 0:n], df_mx[:, s, 4, 0:1], None, ALU.mult))
                    stt(df_a[:, s % 2, 0:n], df_p[:, s % 2, 0, 0:n], df_mx[:, s, 3, 0:1], df_p[:, s % 2, 1, 0:n],
                        ALU.mult, ALU.add).then_inc(S["df_probs"], 1)

                def copy_out(hd):
                    dve.wait_ge(S["df_squared"], hd + 1)
                    nc.vector.tensor_copy(df_o[:, :, hd * P:(hd + 1) * P],
                                          ms[:, hd % 2, 0:SEQ].rearrange("p (m c) -> p m c", m=MT)).then_inc(S["df_o_copied"], 1)

                for s in range(16):
                    score(s)
                    if s:
                        combine(s - 1)
                    if s >= 3 and s % 2:
                        copy_out((s - 3) // 2)
                combine(15)
                copy_out(7)
                dve.wait_ge(S["df_rooted"], 1)
                link(nc.vector.reciprocal(df_ss[:, 2, :, :], df_ss[:, 1, :, :]))
                link(ts(df_ss[:, 2, :, :], df_ss[:, 2, :, :], 1.0 - LAMBDA_INIT, None, ALU.mult))
                o = df_o[:, :, :].rearrange("p m (h c) -> p (m h) c", c=HD)
                r = df_ss[:, 2, :, :].rearrange("p m h -> p (m h)").unsqueeze(2).to_broadcast([P, MT * DIFF_HEADS, HD])
                tt(o, o, r, ALU.mult).then_inc(S["df_normed"], 1)
                for kp in range(4):
                    pair_lo(tg + 4 + kp, pair(xT_lo, 2 * kp), pair(xT_hi, 2 * kp), gains="same",
                            base=GAIN_AT["attn_subln_g_2"])
                b = first["w_o"][1]
                linear("w_o", lambda blk, bb, used: (gained(name)(blk, bb, used),
                                                     (variance(name), add_normed(name)) if blk else None))

            def ple(name):
                st = stage[name]
                tg, nn, n = st["tg"], st["pre"], name[3]
                lo_x(name)
                root(nn)
                linear("gate" + n, lambda *a: None)
                pair_lo(tg + 4, pair(pl_lo, 0), pair(pl_hi, 0))
                bg = first["gate" + n][1]

                def evac(blk, b, used):
                    dve.wait_ge(S["unit_used"], used)
                    dve.wait_ge(S["acc_act"], acts[bg + 2])
                    cols = slice(blk * CB, (blk + 1) * CB)
                    for m in range(MT):
                        tt(y[:, m, cols], acc[:, 2 * (b % 2) + m, :], pl_g[:, m, cols], ALU.mult).then_inc(S["acc_dve"], 1)
                    if blk == DB - 1:
                        gain_y(name)
                        add_normed(name)

                linear("ple" + n, evac)

            def ssm(name):
                st = stage[name]
                tg, nn = st["tg"], st["pre"]
                root(nn)
                dve.wait_ge(S["rstd_ready"], nn + 1)
                ts(y[:, 1, :], x[:, 1, :], rstd[:, nn, 1:2], None, ALU.mult).then_inc(S["sm_xn"], 1)
                for r in range(2):
                    dve.wait_ge(S["sm_c_turned"], r + 1)
                    for part, sign in [(1, -1.0)] if r else [(0, 1.0), (2, -1.0)]:
                        for hf in range(2):
                            ts(sm_CT[:, part, 16 * hf:16 * hf + 16, :].rearrange("p k s -> p (k s)"), acc[:, 2 + hf, :],
                               sign, None, ALU.mult).then_inc(S["sm_CT_copied"], 1)
                for kp in range(4):
                    dve.wait_ge(S["tp_hi"], tg + kp + 1)
                    k = 2 * kp + 1
                    ts(sm_hT[:, k, :], tp[:, (tg + kp) % 2, SEQ:CB], gT[:, gain_row(name) + k:gain_row(name) + k + 1],
                       None, ALU.mult).then_inc(S["tp_lo"], 1)
                dve.wait_ge(S["sm_trig"], 8)

                def read_out(q):
                    c, hf = q // 2, q % 2
                    dve.wait_ge(S["sm_out"], 8 * (q + 1))
                    if q >= 2:
                        dve.wait_ge(S["sm_g_split"], q - 1)
                    for k in range(4):
                        d = GAIN_AT["ssm_d_2"] + 4 * hf + k
                        ins = stt(sm_y[:, q % 2, k, :], sm_hT[:, 4 * hf + k, c * TC:(c + 1) * TC], gT[:, d:d + 1],
                                  ms[:, hf, k * TC:(k + 1) * TC], ALU.mult, ALU.add)
                    ins.then_inc(S["sm_y_read"], 1)

                def split_gelu(q):
                    c, hf = q // 2, q % 2
                    dve.wait_ge(S["sm_g_hi"], q + 1)
                    ks, cs = slice(4 * hf, 4 * hf + 4), slice(c * TC, (c + 1) * TC)
                    tt(xT_lo[:, ks, cs], sm_y[:, q % 2, :, :], xT_hi[:, ks, cs].bitcast(F32),
                       ALU.subtract).then_inc(S["sm_g_split"], 1)

                half = NJ // 2

                def table(t, s):
                    js = slice(tiles_of(s % half)[0], tiles_of(s % half)[1] + 1, NJ // DK)
                    return t[:, js, :].unsqueeze(2).to_broadcast([P, 2, 2, TC])

                def frame(s):
                    dve.wait_ge(S["sm_bu"], s + 1)
                    if s >= 2:
                        dve.wait_ge(S["sm_states"], s - 1)
                    bu = acc[:, s % 4, :].rearrange("p (j r t) -> p j r t", j=2, r=2)
                    tt(sm_a[:, s % 2, :, :, :], bu, table(sm_cos, s), ALU.mult)
                    tt(sm_z[:, s % 2, :, :, :], bu, table(sm_sin, s), ALU.mult).then_inc(S["sm_read"], 1)

                frame(0)
                for s in range(MT * half):
                    c, jp = divmod(s, half)
                    dve.wait_ge(S["sm_framed"], s + 1)
                    if c:
                        dve.wait_ge(S["sm_carried"], jp + 1)
                    for jj, j in enumerate(tiles_of(jp)):
                        for r in range(2):
                            ins = nc.vector.tensor_tensor_scan(
                                sm_z[:, s % 2, jj, r, :], sm_par[:, 0, j:j + 1].to_broadcast([P, TC]),
                                sm_a[:, s % 2, jj, r, :], sm_carry[:, j, r:r + 1] if c else 0.0, ALU.mult, ALU.add)
                    ins.then_inc(S["sm_scanned"], 1)
                    if s + 1 < MT * half:
                        frame(s + 1)
                    dve.wait_ge(S["sm_scanned"], s + 1)
                    if s >= 2:
                        dve.wait_ge(S["sm_out"], s - 1)
                        dve.wait_ge(S["sm_carried"], min(s - 1, half))
                    z = sm_z[:, s % 2, :, :, :]
                    tt(sm_x[:, s % 2, 0, :, :, :], z, table(sm_cos, s), ALU.mult)
                    tt(sm_x[:, s % 2, 1, :, :, :], z, table(sm_sin, s), ALU.mult).then_inc(S["sm_states"], 1)
                    if s % 8 == 1 and s > 8:
                        if s >= 16:
                            split_gelu(s // 8 - 2)
                        read_out(s // 8 - 1)
                split_gelu(2)
                read_out(3)
                split_gelu(3)
                dve.wait_ge(S["sm_bias"], 16)

                def evac(blk, b, used):
                    dve.wait_ge(S["unit_used"], used)
                    cols = slice(blk % DB * CB, (blk % DB + 1) * CB)
                    bias = sm_bg[:, blk * CB:(blk + 1) * CB]
                    for m in range(MT):
                        dst = y[:, m, cols] if blk < DB else z2(m)
                        tt(dst, acc[:, 2 * (b % 2) + m, :], bias, ALU.add).then_inc(S["acc_dve"], 1)
                    if blk >= DB:
                        for m in range(MT):
                            dve.wait_ge(S["sm_sig"], MT * (blk - DB) + m + 1)
                            tt(y[:, m, cols], y[:, m, cols], z2(m), ALU.mult).then_inc(S["sm_prod"], 1)
                    if blk == 2 * DB - 1:
                        gain_y(name)
                        add_normed(name)

                linear("glu", evac)

            def final(name):
                st = stage[name]
                n, g = st["pre"], st["gb"]
                root(n)
                dve.wait_ge(S["rstd_ready"], n + 1)
                dve.wait_ge(S[f"gain_landed{g % 2}"], 16 * (g // 2 + 1))
                for m in range(MT):
                    stt(x[:, m, :], x[:, m, :], rstd[:, n, m:m + 1], gB[:, g % 2, :], ALU.mult,
                        ALU.mult).then_inc(S["x_upd"], 1)

            for u in range(RING):
                split(u)
            dve.wait_ge(S["gain0_copied"], 1)
            for name in STAGES:
                kind = name.rstrip("0123456789")
                {"ffna": ffn, "ffnb": ffn, "even": even, "odd": odd, "final": final, "diff": diff,
                 "ple": ple, "ssm": ssm}[kind](name)


def kernel(**inputs):
    import numpy as _np
    import concourse.bacc as _bacc
    from concourse import mybir as _mybir
    from concourse.bass_utils import run_bass_kernel_spmd as _run

    nc = _bacc.Bacc("TRN2", target_bir_lowering=False, num_devices=1)
    arrays, aps = {}, {}
    for name, a in [*inputs.items(), *tables().items()]:
        a = _np.ascontiguousarray(a)
        arrays["in_" + name] = a
        aps[name] = nc.dram_tensor("in_" + name, a.shape, _mybir.dt.from_np(a.dtype), kind="ExternalInput").ap()
    out = nc.dram_tensor("out_0", (1, SEQ, D), F32, kind="ExternalOutput").ap()
    scratch = nc.dram_tensor("rel_scratch", (2 * DIFF_HEADS, RELN), F32, kind="Internal").ap()
    build_program(nc, aps, out, scratch)
    r = _run(nc, [arrays], core_ids=[0])
    return r.results[0]["out_0"]
```

```python
import math
from contextlib import ExitStack

import concourse.bass as bass
import numpy as np
from concourse import mybir

F32 = mybir.dt.float32
F32R = mybir.dt.float32r
I32 = mybir.dt.int32
ALU = mybir.AluOpType
ACT = mybir.ActivationFunctionType
AX = mybir.AxisListType

P = 128
SEQ = 256
MT = SEQ // P
D = 1024
DK = D // P
D_FF = 2816
FK = D_FF // P
CB = 512
FB = CB // 2
NFB = D_FF // FB
DB = D // CB
RING = 4
SLOT = 3 * CB
EPS = 1e-6
NEG = -1e30

GLA_HEADS, GLA_DK, GLA_DV, GLA_CHUNK, GLA_TAU, GATE_RANK = 4, 64, 128, 64, 16.0, 16
GLA_QK = GLA_HEADS * GLA_DK
GLA_V = GLA_HEADS * GLA_DV
POOL_WINDOWS = (2, 4, 8, 16)
POOL_DIM = 512
EVEN_IN = 2 * GLA_QK + 2 * GLA_V + GATE_RANK + POOL_DIM
V_AT, G_AT, LR_AT, U_AT = 2 * GLA_QK, 2 * GLA_QK + GLA_V, 2 * GLA_QK + 2 * GLA_V, EVEN_IN - POOL_DIM

ATT_HEADS, KV_HEADS, HD, IDX_HEADS, IDX_DIM = 8, 2, 128, 4, 64
TOPK = min(256, SEQ // 4)
ATT_K, ATT_V, ATT_QI = ATT_HEADS * HD, (ATT_HEADS + KV_HEADS) * HD, (ATT_HEADS + 2 * KV_HEADS) * HD
ATT_WI = ATT_QI + (IDX_HEADS + 1) * IDX_DIM
ODD_IN = ATT_WI + IDX_HEADS
PICKED, BARRED = -3.3e38, -3.0e38

DIFF_HEADS, DIFF_DIM, LAMBDA_INIT = 8, 64, 0.8 - 0.6 * math.exp(-0.3 * 0)
BUCKETS, MAX_DIST = 32, 128
RELN = 384

GROUPS, GCH, STATES = 64, 16, 64
NJ = GROUPS * STATES // P
TC = 128
PLE = 256

ROUND = 1.5 * 2.0 ** 23
TWO_PI = (6.28125, 0.001935243606567383, 6.357301884918343e-08)
SAFE_PI, SAFE_TURN = 3.1415925, 6.283185

LINEAR = {
    "even_in": (DK, EVEN_IN, 1, 1),
    "even_out": (DK, D, 0, MT),
    "odd_in": (DK, ODD_IN, 1, 1),
    "odd_out": (DK, D, 0, MT),
    "qkv": (DK, 3 * D, 1, 1),
    "w_o": (DK, D, MT, MT),
    "glu": (DK, 2 * D, 0, MT),
    "gate0": (DK, D, MT, 0),
    "ple0": (PLE // P, D, 0, MT),
    "gate1": (DK, D, MT, 0),
    "ple1": (PLE // P, D, 0, MT),
}

STAGE_KINDS = {
    "ffna": (["{}"], 4 + NFB, True, False),
    "even": (["even_in", "even_out"], 8, True, False),
    "odd": (["odd_in", "odd_out"], 8, True, False),
    "final": ([], 0, True, False),
    "ffnb": (["{}"], 4 + NFB, True, True),
    "diff": (["qkv", "w_o"], 8, True, True),
    "ssm": (["glu"], 4, True, True),
    "ple": (["gate", "ple"], 5, True, True),
}
STAGES = ["ffna0", "even", "ffna1", "ffna2", "odd", "ffna3", "final",
          "ffnb0", "diff", "ffnb1", "ple0", "ffnb2", "ssm", "ffnb3", "ple1"]

GAIN_AT = {"ffn1_norm": 0, "mix_norm": 16, "ffn2_norm": 32, "norm_g_2": 48, "pool_scale": 176,
           "attn_subln_g_2": 180, "ssm_d_2": 181}
GAIN_ROWS = 189


def gain_row(stage):
    return {"ffna0": 0, "even": 16, "ffna1": 32, "ffna2": 8, "odd": 24, "ffna3": 40,
            "ffnb0": 48 + 0, "diff": 48 + 16, "ffnb1": 48 + 32, "ple0": 48 + 48,
            "ffnb2": 48 + 64, "ssm": 48 + 80, "ffnb3": 48 + 96, "ple1": 48 + 112}[stage]


ROW_GAINS = {"even": ("gla_out_norm", (0,), GLA_V), "final": ("final_norm", (), D),
             "ffnb0": ("norm_g_2", (0, 1), D), "diff": ("norm_g_2", (0, 3), D),
             "ffnb1": ("norm_g_2", (0, 5), D), "ple0": ("norm_g_2", (0, 7), D),
             "ffnb2": ("norm_g_2", (1, 1), D), "ssm": ("norm_g_2", (1, 3), D),
             "ffnb3": ("norm_g_2", (1, 5), D), "ple1": ("norm_g_2", (1, 7), D)}

FFN_W = {"ffna0": ("ffn1_wi", "ffn1_wo", (0,)), "ffna1": ("ffn2_wi", "ffn2_wo", (0,)),
         "ffna2": ("ffn1_wi", "ffn1_wo", (1,)), "ffna3": ("ffn2_wi", "ffn2_wo", (1,)),
         "ffnb0": ("ffn_w_in_2", "ffn_w_out_2", (0, 0)), "ffnb1": ("ffn_w_in_2", "ffn_w_out_2", (0, 1)),
         "ffnb2": ("ffn_w_in_2", "ffn_w_out_2", (1, 0)), "ffnb3": ("ffn_w_in_2", "ffn_w_out_2", (1, 1))}
LINEAR_W = {"even_in": ("even_w_in", 0), "even_out": ("even_w_out", 0), "odd_in": ("odd_w_in", 0),
            "odd_out": ("odd_w_out", 0), "qkv": ("attn_w_qkv_2", 0), "w_o": ("attn_w_o_2", 0),
            "glu": ("ssm_w_glu_2", 0), "gate0": ("ple_w_gate_2", 0), "ple0": ("ple_w_proj_2", 0),
            "gate1": ("ple_w_gate_2", 1), "ple1": ("ple_w_proj_2", 1)}


def k_groups(n):
    return [3] * 6 + [2] * 2 if n == FK else [2] * (n // 2)


def plan():
    units, first, acts, dves, stage = [], {}, [0], [0], {}
    tg = nn = pre = npost = xu = gb = nf = 0

    def add_block(name, kn, c0, cn, act_counts, dve_counts):
        k = 0
        for n in k_groups(kn):
            units.append((name, k, n, c0, cn))
            k += n
        acts.append(acts[-1] + act_counts)
        dves.append(dves[-1] + dve_counts)

    for name in STAGES:
        kind = name.rstrip("0123456789")
        weights, pairs, in_front, behind = STAGE_KINDS[kind]
        stage[name] = dict(tg=tg, pre=nn if in_front else None, npre=pre, npost=npost, post=nn + 1 if behind else None,
                           xu=xu, gb=gb, nf=nf)
        tg += pairs
        pre += in_front
        nn += in_front + behind
        xu += MT * DB if behind or kind == "final" else 0
        npost += behind
        gb += name in ROW_GAINS
        nf += kind.startswith("ffn")
        for w in weights:
            w = w.format(name) if "{}" in w else w + (name[3:] if kind == "ple" else "")
            first[w] = (len(units), len(acts) - 1)
            if kind.startswith("ffn"):
                for fb in range(NFB):
                    add_block(w + ".in", DK, fb * FB, CB, MT, MT)
                for cb in range(DB):
                    add_block(w + ".out", FK, cb * CB, CB, MT if behind else 0, MT)
            else:
                kn, cols, a, d = LINEAR[w]
                starts = list(range(0, cols, CB))
                if w == "odd_in":
                    starts = starts[-1:] + starts[:-1]
                for c0 in starts:
                    add_block(w, kn, c0, min(CB, cols - c0), a, d)
    return units, first, acts, dves, stage, nn, xu


def tables():
    t = np.arange(P)
    same = (t[:, None] // GLA_CHUNK) == (t[None, :] // GLA_CHUNK)
    src, dst = t[:, None] % GLA_CHUNK, t[None, :] % GLA_CHUNK
    upto = (same & (src <= dst)).astype(np.float32)
    mid = (same & (src < GLA_CHUNK // 2)).astype(np.float32)
    whole = same.astype(np.float32)
    chunk = (t[:, None] // GLA_CHUNK == np.arange(2)[None, :]).astype(np.float32)
    gla = np.concatenate([(upto - mid), upto, (whole - upto), chunk], 1) / np.float32(GLA_TAU)
    s, q = np.arange(SEQ)[:, None], np.arange(SEQ)[None, :]
    pool = []
    for w in POOL_WINDOWS:
        band = ((s <= q) & (s > q - w)).astype(np.float32) / np.minimum(q + 1, w).astype(np.float32)
        pool.append(band - (s == q).astype(np.float32))
    pool = np.stack(pool).reshape(4, MT, P, SEQ).transpose(2, 0, 1, 3)
    keep = (t[None, :GLA_CHUNK] >= (t[:, None] % GLA_CHUNK)).astype(np.int32)
    qpos = np.arange(MT)[None, :, None] * P + t[:, None, None]
    barred = (np.arange(SEQ)[None, None, :] > qpos)
    inv = np.concatenate([np.float32(10000.0) ** (-np.arange(0, d, 2, dtype=np.float32) / np.float32(d))
                          for d in (HD, IDX_DIM)]).astype(np.float32)
    dist = SEQ - 1 - np.arange(RELN)
    n = np.maximum(dist, 0)
    exact = BUCKETS // 2
    large = exact + (np.log(np.maximum(n, 1).astype(np.float32) / np.float32(exact))
                     / np.float32(math.log(MAX_DIST / exact)) * np.float32(BUCKETS - exact)).astype(np.int32)
    bucket = np.where(n < exact, n, np.minimum(large, BUCKETS - 1))
    hot = np.zeros((BUCKETS + 1, RELN), np.float32)
    hot[bucket, np.arange(RELN)] = 8.0
    hot[:, dist < 0] = 0.0
    hot[BUCKETS, dist < 0] = 8.0 * NEG
    parity = np.stack([t % 32 < 16, t % 32 >= 16, t < 64, t >= 64], 1).astype(np.float32)
    steps = np.broadcast_to(np.arange(1, TC + 1, dtype=np.float32)[None], (P, TC))
    return {
        "c_ident": np.eye(P, dtype=np.float32),
        "c_flip": np.ascontiguousarray(np.eye(P, dtype=np.float32)[::-1]),
        "c_gla": np.ascontiguousarray(gla, np.float32),
        "c_pool": np.ascontiguousarray(pool, np.float32),
        "c_keep": np.ascontiguousarray(keep),
        "c_barred": np.ascontiguousarray(barred.astype(np.int32)),
        "c_inv": np.ascontiguousarray(np.broadcast_to(inv[None], (P, inv.size))),
        "c_hot": hot,
        "c_parity": np.ascontiguousarray(parity),
        "c_steps": np.ascontiguousarray(steps),
    }


def build_program(nc, A, out, rel_scratch):
    units, first, acts, dves, stage, N_NORMS, X_ALL = plan()
    ctx = ExitStack()
    with ctx:
        class Sems(dict):
            def __missing__(self, name):
                self[name] = ctx.enter_context(nc.semaphore(name))
                return self[name]

        S = Sems()

        def sb(name, shape, dt=F32, where=ctx):
            return where.enter_context(nc.sbuf_tensor(name, shape, dt))

        raw = sb("raw", [P, RING, SLOT])
        w_hi = sb("w_hi", [P, RING, SLOT], F32R)
        w_lo = sb("w_lo", [P, RING, SLOT], F32R)
        with ExitStack() as place:
            xT_hi = sb("xT_hi", [P, DK, SEQ], F32R, place)
            xT_lo = sb("xT_lo", [P, DK, SEQ], F32R, place)
        sm_blocks = sb("sm_blocks", [P, 4, 4 * SEQ])
        x = sb("x", [P, MT, D])
        y = sb("y", [P, MT, D])
        ident = sb("ident", [P, P])
        gT = sb("gT", [P, GAIN_ROWS])
        gB = sb("gB", [P, 2, D])
        ss = sb("ss", [P, N_NORMS, MT, DB])
        std = sb("std", [P, N_NORMS, MT])
        rstd = sb("rstd", [P, N_NORMS, MT])
        trig = sb("trig", [P, 2, MT, 96])
        warm = sb("warm", [P, 16])
        neg_lam = sb("neg_lam", [P, 1])
        sm_par = sb("sm_par", [P, 6, NJ])
        acc = ctx.enter_context(nc.psum_tensor("acc", [P, 2 * MT, CB], F32))
        tp = ctx.enter_context(nc.psum_tensor("tp", [P, 2, CB], F32))
        ms = ctx.enter_context(nc.psum_tensor("ms", [P, 2, CB], F32))

        with ExitStack() as arena:
            hT_hi = sb("hT_hi", [P, FK, SEQ], F32R, arena)
            hT_lo = sb("hT_lo", [P, FK, SEQ], F32R, arena)
            silu = sb("silu", [P, 2, MT, FB], F32, arena)
            h = sb("h", [P, 2, MT, FB], F32, arena)
            with ExitStack() as setup:
                gain_rows = sb("gain_rows", [P, 2, P], F32, setup)
                pos_i = sb("pos_i", [P, MT], I32, setup)
                pos = sb("pos", [P, MT], F32, setup)
                inv = sb("inv", [P, 96], F32, setup)
                ang = sb("ang", [P, MT, 96], F32, setup)
                turns = sb("turns", [P, 2, MT, 96], F32, setup)
                red = sb("red", [P, 2, MT, 96], F32, setup)
                lam_v = sb("lam_v", [P, 2, 2, DIFF_DIM], F32, setup)
                lam_p = sb("lam_p", [P, 2, DIFF_DIM], F32, setup)
                lam_s = sb("lam_s", [P, 4], F32, setup)
                rel_b = sb("rel_b", [BUCKETS + 1, 2 * DIFF_HEADS], F32, setup)
                hot = sb("hot", [BUCKETS + 1, RELN], F32, setup)
                rel_v = sb("rel_v", [2 * DIFF_HEADS, RELN], F32, setup)
                sm_rows = sb("sm_rows", [NJ, 14, P], F32, setup)
                sm_dt = sb("sm_dt", [NJ, 2, 2], F32, setup)
            sm_cos = sb("sm_cos", [P, NJ, TC], F32, arena)
            sm_sin = sb("sm_sin", [P, NJ, TC], F32, arena)
            sm_steps = sb("sm_steps", [P, TC], F32, arena)
            sm_parity = sb("sm_parity", [P, 4], F32, arena)
            sm_t = sb("sm_t", [P, 2, 4, TC], F32, arena)
        with ExitStack() as arena:
            ev = sb("ev", [P, MT, EVEN_IN], F32, arena)
            ev_g = sb("ev_g", [P, MT, GLA_V], F32, arena)
            ev_lrT = sb("ev_lrT", [GATE_RANK + 1, SEQ], F32, arena)
            ev_gw = sb("ev_gw", [GATE_RANK + 1, GLA_QK], F32, arena)
            ev_t = sb("ev_t", [P, MT, GLA_QK], F32, arena)
            ev_la = sb("ev_la", [P, MT, GLA_QK], F32, arena)
            ev_e = sb("ev_e", [P, 4, MT, GLA_QK], F32, arena)
            ev_s = sb("ev_s", [P, 4, MT, GLA_QK], F32, arena)
            ev_T = sb("ev_T", [P, 3, 2, SEQ], F32, arena)
            ev_sc = sb("ev_sc", [P, MT, GLA_HEADS, P], F32, arena)
            ev_dec = sb("ev_dec", [P, 2, 2 * MT], F32, arena)
            ev_st = sb("ev_st", [P, 3, 2, GLA_DV], F32, arena)
            ev_o = sb("ev_o", [P, MT, GLA_V], F32, arena)
            ev_c = sb("ev_c", [P, 3 * P + 2], F32, arena)
            ev_keep = sb("ev_keep", [P, GLA_CHUNK], I32, arena)
            ev_pw = sb("ev_pw", [P, 4, MT, SEQ], F32, arena)
            ev_pT = sb("ev_pT", [P, 4, SEQ], F32, arena)
            ev_pm = sb("ev_pm", [P, 4, P], F32, arena)
            ev_ss = sb("ev_ss", [P, 3, MT * GLA_HEADS], F32, arena)
        with ExitStack() as arena:
            od = sb("od", [P, MT, ODD_IN], F32, arena)
            od_r = sb("od_r", [P, MT, ATT_HEADS + KV_HEADS, HD], F32, arena)
            od_ri = sb("od_ri", [P, MT, IDX_HEADS + 2, IDX_DIM], F32, arena)
            od_t = sb("od_t", [P, 4, ATT_HEADS + KV_HEADS, HD // 2], F32, arena)
            od_ti = sb("od_ti", [P, 4, IDX_HEADS + 1, IDX_DIM // 2], F32, arena)
            od_qT = sb("od_qT", [P, 4, 2, SEQ], F32, arena)
            od_kT = sb("od_kT", [P, KV_HEADS, SEQ], F32, arena)
            od_qiT = sb("od_qiT", [P, 2, SEQ], F32, arena)
            od_kiT = sb("od_kiT", [P, SEQ], F32, arena)
            od_rl = sb("od_rl", [P, MT, IDX_HEADS, SEQ], F32, arena)
            od_is = sb("od_is", [P, MT, SEQ], F32, arena)
            od_m8 = sb("od_m8", [P, 8], F32, arena)
            od_bar = sb("od_bar", [P, MT, SEQ], I32, arena)
            od_fill = sb("od_fill", [P, SEQ], F32, arena)
            od_neg = sb("od_neg", [P, SEQ], F32, arena)
            od_p = sb("od_p", [P, 2, 2, SEQ], F32, arena)
            od_pT = sb("od_pT", [P, 2, CB], F32, arena)
            od_mx = sb("od_mx", [P, 8, 2, 4], F32, arena)
        with ExitStack() as arena:
            df = sb("df", [P, MT, 3 * D], F32, arena)
            df_qT = sb("df_qT", [P, 2, DIFF_HEADS, SEQ], F32, arena)
            df_kT = sb("df_kT", [P, DIFF_HEADS, SEQ], F32, arena)
            df_flip = sb("df_flip", [P, P], F32, arena)
            df_b = sb("df_b", [P, 2, 2, SEQ], F32, arena)
            df_p = sb("df_p", [P, 2, 2, SEQ], F32, arena)
            df_a = sb("df_a", [P, 2, SEQ], F32, arena)
            df_pT = sb("df_pT", [P, 2, SEQ], F32, arena)
            df_mx = sb("df_mx", [P, 16, 5, 2], F32, arena)
            df_o = sb("df_o", [P, MT, D], F32, arena)
            df_ss = sb("df_ss", [P, 3, MT, DIFF_HEADS], F32, arena)
        with ExitStack() as arena:
            pl_g = sb("pl_g", [P, MT, D], F32, arena)
            pl_gg = sb("pl_gg", [P, MT, D], F32, arena)
            pl_p = sb("pl_p", [P, MT, PLE], F32, arena)
            pl_hi = sb("pl_hi", [P, 2, SEQ], F32R, arena)
            pl_lo = sb("pl_lo", [P, 2, SEQ], F32R, arena)
        with ExitStack() as arena:
            sm_BT = sb("sm_BT", [P, 2, DK, P], F32, arena)
            sm_CT = sb("sm_CT", [P, 3, NJ, 2 * GCH], F32, arena)
            sm_a = sb("sm_a", [P, 2, 2, 2, TC], F32, arena)
            sm_z = sb("sm_z", [P, 2, 2, 2, TC], F32, arena)
            sm_x = sb("sm_x", [P, 2, 2, 2, 2, TC], F32, arena)
            sm_carry = sb("sm_carry", [P, NJ, 2], F32, arena)
            sm_y = sb("sm_y", [P, 2, 4, TC], F32, arena)
            sm_bg = sb("sm_bg", [P, 2 * D], F32, arena)
        assert 2 * DK * P + 3 * NJ * 2 * GCH + 4 * 8 * TC + 2 * NJ + 8 * TC + 2 * D <= 2 * FK * SEQ + 4 * MT * FB
        flat4 = "p a b c -> p (a b c)"
        sm_bd = [sm_blocks[:, r, :] for r in range(2)]
        sm_cd = [sm_blocks[:, 2 + r, :] for r in range(2)]
        sm_b = silu[:, :, :, :].rearrange(flat4).rearrange("p (r j c) -> p r j c", r=2, j=NJ)
        sm_c = h[:, :, :, :].rearrange(flat4).rearrange("p (r k s) -> p r k s", r=2, k=DK)
        sm_hT = sm_blocks[:, 2:4, :].rearrange("p a (k t) -> p (a k) t", t=SEQ)


        def rows_of(w, k, kn, c, n):
            return w[k * P:(k + kn) * P, bass.ds(c, n)].rearrange("(k p) c -> p k c", p=P)

        def pieces_of(u, shift=0):
            name, k, kn, c0, cn = units[u]
            layer, _, side = name.partition(".")
            if side == "in":
                w = A[FFN_W[layer][0]]
                for i in FFN_W[layer][2]:
                    w = w[i]
                return [(0, FB, rows_of(w, k, kn, shift + c0, FB)),
                        (FB, FB, rows_of(w, k, kn, shift + c0 + D_FF, FB))]
            if side == "out":
                w = A[FFN_W[layer][1]]
                for i in FFN_W[layer][2]:
                    w = w[i]
            else:
                w = A[LINEAR_W[layer][0]][LINEAR_W[layer][1]]
            return [(0, cn, rows_of(w, k, kn, c0, cn))]

        def slot(ring, u):
            _, _, kn, _, cn = units[u]
            return ring[:, u % RING, 0:kn * cn].rearrange("p (k c) -> p k c", k=kn)

        def flat(ring, u):
            _, _, kn, _, cn = units[u]
            return ring[:, u % RING, 0:kn * cn]

        def pair(tile, k):
            return tile[:, k:k + 2, :].rearrange("p k t -> p (k t)")

        def wait_x(eng, name, cb=DB - 1):
            at = STAGES.index(name) if name else len(STAGES)
            if at == 0:
                eng.wait_ge(S["x_landed"], 16)
                return
            before = STAGES[at - 1]
            if stage[before]["post"] is not None or before == "final":
                eng.wait_ge(S["x_upd"], (stage[name]["xu"] if name else X_ALL) - MT * (DB - 1 - cb))
            else:
                last = STAGE_KINDS[before.rstrip("0123456789")][0][-1].format(before)
                b = first[last][1] + (NFB if before.startswith("ffn") else 0)
                eng.wait_ge(S["acc_dve"], dves[b + cb + 1])

        def follower(name):
            at = STAGES.index(name) + 1
            if stage[name]["post"] is not None or name == "final" or at == len(STAGES) or STAGES[at] in ("final", "ssm"):
                return None
            return STAGES[at]

        def is_follower(name):
            at = STAGES.index(name)
            return at > 0 and follower(STAGES[at - 1]) == name

        def held_back(name):
            at = STAGES.index(name)
            if at == 0 or STAGES[at - 1].rstrip("0123") not in ("ffnb", "diff", "ssm") or name == "ssm":
                return ()
            w = STAGE_KINDS[name.rstrip("0123")][0][0]
            u = first[w.format(name) if "{}" in w else w + (name[3:] if name.startswith("ple") else "")][0]
            return (u + RING - 2, u + RING - 1)

        def holds_back(name):
            at = STAGES.index(name) + 1
            return at < len(STAGES) and len(held_back(STAGES[at])) > 0

        def od_bank(s):
            return (acc[:, 0, :], acc[:, 1, :], ms[:, 0, :], ms[:, 1, :])[s % 4]

        def state_part(hp, c):
            return ms[:, 1, hp * P:(hp + 1) * P] if c == 1 else acc[:, 3, (2 * hp + c // 2) * P:(2 * hp + c // 2 + 1) * P]

        def of_head(m, hd):
            return (2 * m + hd // 2) * P

        def tiles_of(jp):
            per = NJ // DK
            j = 2 * per * (jp // per) + jp % per
            return j, j + per

        def z2(m):
            return sm_y[:, m, :, :].rearrange("p k t -> p (k t)")

        def squared_before(name):
            return 2 * DB * [n for n in STAGES if n in ("ple0", "ssm", "ple1")].index(name)

        with_block = ctx.enter_context(nc.Block())

        @with_block.sync
        def _(sp):
            def load(u, i=0, per=0):
                if u >= RING:
                    sp.wait_ge(S["w_split"], u - RING + 1 + per * i)
                pieces = pieces_of(u, FB * i if per else 0)
                for c, n, src in pieces:
                    sp.dma_start(slot(raw, u)[:, :, c:c + n], src).then_inc(
                        S[f"w_landed{u % RING}"], 32 // len(pieces))

            sp.dma_start(ident[:, :], A["c_ident"]).then_inc(S["ident_landed"], 16)
            sp.dma_start(x[:, :, :], A["x"].rearrange("b (m p) d -> p (b m) d", p=P)).then_inc(S["x_landed"], 16)
            u = 0
            while u < len(units):
                if units[u][0].endswith(".in"):
                    n = DK // 2
                    peel = n if u < RING else 0
                    for v in range(peel):
                        load(u + v)
                    with nc.sync.Fori(0, NFB - peel // n) as i:
                        for v in range(n):
                            load(u + peel + v, i, n)
                    u += n * NFB
                else:
                    load(u)
                    u += 1
            wait_x(sp, None)
            sp.dma_start(out.rearrange("b (m p) d -> p (b m) d", p=P), x[:, :, :]).then_inc(S["stored"], 16)
            sp.wait_ge(S["stored"], 16)

        @with_block.gpsimd
        def _(pool):
            def row_gain(name):
                g = stage[name]["gb"]
                key, index, width = ROW_GAINS[name]
                if g >= 2:
                    before = [n for n in ROW_GAINS if n in stage][g - 2]
                    after = STAGES[STAGES.index(before) + 1]
                    wait_x(pool, after)
                v = A[key]
                for i in index:
                    v = v[i]
                pool.dma_start(gB[:, g % 2, 0:width],
                               v.rearrange("(a n) -> a n", a=1).to_broadcast([P, width])).then_inc(
                    S[f"gain_landed{g % 2}"], 16)

            def spread(v, n):
                return v.rearrange("(a n) -> a n", a=1).to_broadcast([P, n])

            pool.memset(rel_b[:, :], 1.0).then_inc(S["rel_ones"], 1)
            pool.dma_start(gain_rows[0:16, 0, :], A["ffn1_norm"].rearrange("l (k p) -> (l k) p", p=P)).then_inc(
                S["gain0_landed"], 16)
            loads = [
                (gain_rows[16:32, 0, :], A["mix_norm"].rearrange("l (k p) -> (l k) p", p=P)),
                (gain_rows[32:48, 0, :], A["ffn2_norm"].rearrange("l (k p) -> (l k) p", p=P)),
                (gain_rows[48:128, 0, :],
                 A["norm_g_2"].rearrange("i j (k p) -> (i j k) p", p=P)[0:80, :]),
                (gain_rows[0:48, 1, :],
                 A["norm_g_2"].rearrange("i j (k p) -> (i j k) p", p=P)[80:128, :]),
                (gain_rows[48:52, 1, :], A["pool_scale"].rearrange("a (k p) -> (a k) p", p=P)),
                (gain_rows[52:53, 1, :], A["attn_subln_g_2"]),
                (gain_rows[53:61, 1, :], A["ssm_d_2"].rearrange("a (k p) -> (a k) p", p=P)),
            ]
            for dst, src in loads:
                pool.dma_start(dst, src).then_inc(S["gains_landed"], 16)
            pool.wait_ge(S["rel_ones"], 1)
            more = [
                (pos_i[:, :], A["positions"].rearrange("b (m p) -> p (b m)", p=P)),
                (inv[:, :], A["c_inv"]),
                (lam_v[:, :, :, :].rearrange("p a b c -> p (a b c)"),
                 spread(A["attn_lam_2"][0].rearrange("a b -> (a b)"), 4 * DIFF_DIM)),
                (rel_b[0:BUCKETS, :], A["rel_bias_2"]),
                (hot[:, :], A["c_hot"]),
            ]
            for dst, src in [
                (sm_rows[:, 0, :], A["ssm_lam_re_2"][0].rearrange("(j g) s -> j (g s)", g=2)),
                (sm_rows[:, 1, :], A["ssm_lam_im_2"][0].rearrange("(j g) s -> j (g s)", g=2)),
                (sm_dt[:, 0, :], A["ssm_log_dt_2"][0].rearrange("(j g) -> j g", g=2)),
            ]:
                pool.dma_start(dst, src).then_inc(S["sm_landed"], 16)
            for dst, src in more:
                pool.dma_start(dst, src, allow_slow_non_contiguous=True).then_inc(S["setup_landed"], 16)
            pool.wait_ge(S["rel_copied"], 1)
            pool.dma_start(rel_scratch, rel_v[:, :]).then_inc(S["rel_stored"], 16)
            pool.wait_ge(S["rel_stored"], 16)

            steps_done = [0]

            def link(ins):
                steps_done[0] += 1
                ins.then_inc(S["pool_step"], 1)
                pool.wait_ge(S["pool_step"], steps_done[0])

            def prepare_ssm(name):
                u0, b0 = first[name]
                tt, ts = nc.gpsimd.tensor_tensor, nc.gpsimd.tensor_scalar
                wait_x(pool, name)
                pool.dma_start(sm_steps[:, :], A["c_steps"]).then_inc(S["sm_consts"], 16)
                pool.dma_start(sm_parity[:, :], A["c_parity"]).then_inc(S["sm_consts"], 16)
                pool.wait_ge(S["sm_consts"], 32)
                pool.wait_ge(S["sm_par_ready"], 1)
                for g in range(8):
                    js = slice(4 * g, 4 * g + 4)
                    steps = sm_steps[:, :].unsqueeze(1).to_broadcast([P, 4, TC])
                    part = lambda k: sm_par[:, k, js].unsqueeze(2).to_broadcast([P, 4, TC])
                    a, b, c = sm_sin[:, js, :], sm_t[:, 0, :, :], sm_t[:, 1, :, :]
                    tt(c, steps, part(5), ALU.mult)
                    link(tt(a, steps, part(4), ALU.mult))
                    link(ts(b, a, ROUND, ROUND, ALU.add, ALU.subtract))
                    link(tt(a, a, b, ALU.subtract))
                    link(tt(a, a, c, ALU.add))
                    link(ts(b, a, ROUND, ROUND, ALU.add, ALU.subtract))
                    ins = tt(a, a, b, ALU.subtract)
                    ins.then_inc(S["sm_turns"], 1)
                    pool.wait_ge(S["sm_turns"], g + 1)
                pool.wait_ge(S["acc_dve"], dves[b0 + NFB])
                pool.wait_ge(S["tp_full"], stage[name]["tg"] + 4 + NFB)
                for dst, src in [
                    (sm_b[:, 0, :, :], A["ssm_b_re_2"][0].rearrange("(j g) s c -> (g s) j c", g=2)),
                    (sm_b[:, 1, :, :], A["ssm_b_im_2"][0].rearrange("(j g) s c -> (g s) j c", g=2)),
                    (sm_c[:, 0, :, :], A["ssm_c_re_2"][0].rearrange("(k g) c s -> (g c) k s", k=DK)),
                    (sm_c[:, 1, :, :], A["ssm_c_im_2"][0].rearrange("(k g) c s -> (g c) k s", k=DK)),
                ]:
                    pool.dma_start(dst, src).then_inc(S["sm_bc_landed"], 16)
                pool.wait_ge(S["sm_bc_landed"], 64)
                fb = lambda k: sm_par[:, k, :].unsqueeze(2).to_broadcast([P, NJ, GCH])
                br, bi = sm_b[:, 0, :, :], sm_b[:, 1, :, :]
                t1, t2 = [sm_t[:, k, :, :].rearrange("p a t -> p (a t)").rearrange("p (j c) -> p j c", c=GCH)
                          for k in range(2)]
                tt(t1, bi, fb(3), ALU.mult)
                link(tt(t2, br, fb(3), ALU.mult))
                tt(br, br, fb(2), ALU.mult)
                link(tt(bi, bi, fb(2), ALU.mult))
                tt(br, br, t1, ALU.subtract)
                link(tt(bi, bi, t2, ALU.add))
                pool.wait_ge(S["unit_used"], u0 + NFB * (DK // 2))
                for r in range(2):
                    bd = sm_bd[r].rearrange("p (j g c) -> p j g c", j=NJ, g=2)
                    cd = sm_cd[r].rearrange("p (k g s) -> p k g s", k=DK, g=2)
                    for g in range(2):
                        ts(bd[:, :, g, :], sm_b[:, r, :, :], sm_parity[:, 2 + g:3 + g], None, ALU.mult)
                    for g in range(2):
                        ins = ts(cd[:, :, g, :], sm_c[:, r, :, :], sm_parity[:, g:g + 1], None, ALU.mult)
                ins.then_inc(S["sm_blocks"], 1)

            def run_ssm():
                half = NJ // 2
                tt = nc.gpsimd.tensor_tensor

                def carry(s):
                    js = slice(tiles_of(s)[0], tiles_of(s)[1] + 1, NJ // DK)
                    pool.wait_ge(S["sm_states"], s + 1)
                    xa, xb = sm_x[:, s % 2, 0, :, :, TC - 1], sm_x[:, s % 2, 1, :, :, TC - 1]
                    tt(sm_carry[:, js, 0], xa[:, :, 0], xb[:, :, 1], ALU.subtract)
                    tt(sm_carry[:, js, 1], xa[:, :, 1], xb[:, :, 0], ALU.add).then_inc(S["sm_carried"], 1)

                for s in range(MT * half):
                    pool.wait_ge(S["sm_read"], s + 1)
                    a, b = sm_a[:, s % 2, :, :, :], sm_z[:, s % 2, :, :, :]
                    tt(a[:, :, 0, :], a[:, :, 0, :], b[:, :, 1, :], ALU.add)
                    tt(a[:, :, 1, :], a[:, :, 1, :], b[:, :, 0, :], ALU.subtract).then_inc(S["sm_framed"], 1)
                    if 1 <= s <= half:
                        carry(s - 1)

            for name in STAGES:
                st = stage[name]
                if name == "ffnb2":
                    prepare_ssm(name)
                if name == "even":
                    wait_x(pool, name)
                    pool.memset(ev_lrT[:, :], 1.0).then_inc(S["ev_cleared"], 1)
                    pool.memset(ev_sc[:, :, :, :], 0.0).then_inc(S["ev_cleared"], 1)
                    for dst, src in [
                        (ev_gw[0:GATE_RANK, :], A["gla_gate_w"][0]),
                        (ev_gw[GATE_RANK:GATE_RANK + 1, :], A["gla_gate_b"]),
                        (ev_c[:, :], A["c_gla"]),
                        (ev_keep[:, :], A["c_keep"]),
                        (ev_pw[:, :, :, :], A["c_pool"]),
                        (ev_pm[:, :, :], A["pool_w"][0].rearrange("g c d -> c g d")),
                    ]:
                        pool.dma_start(dst, src).then_inc(S["ev_landed"], 16)
                if name == "odd":
                    wait_x(pool, name)
                    pool.memset(od_fill[:, :], BARRED).then_inc(S["od_cleared"], 1)
                    pool.memset(od_neg[:, :], NEG).then_inc(S["od_cleared"], 1)
                    pool.dma_start(od_bar[:, :, :], A["c_barred"]).then_inc(S["od_landed"], 16)
                    b = first["odd_in"][1]
                    pool.wait_ge(S["trig_ready"], 2)
                    tt = nc.gpsimd.tensor_tensor
                    half = HD // 2
                    for part, (h0, h1) in enumerate([(0, ATT_HEADS), (ATT_HEADS, ATT_HEADS + KV_HEADS)]):
                        pool.wait_ge(S["acc_act"], acts[b + 3 + part])
                        pool.wait_ge(S["acc_dve"], dves[b + 3 + part])
                        for m in range(MT):
                            src = od[:, m, h0 * HD:h1 * HD].rearrange("p (h a c) -> p h a c", a=2, c=half)
                            dst = od_r[:, m, h0:h1, :].rearrange("p h (a c) -> p h a c", a=2)
                            cos, sin = [trig[:, a, m, 0:half].unsqueeze(1).to_broadcast([P, h1 - h0, half]) for a in range(2)]
                            x1, x2 = src[:, :, 0, :], src[:, :, 1, :]
                            t = [od_t[:, k, h0:h1, :] for k in range(4)]
                            if m:
                                pool.wait_ge(S["od_qk_roped"], MT * part + 1)
                            tt(t[0], x1, cos, ALU.mult)
                            tt(t[1], x2, sin, ALU.mult)
                            tt(t[2], x2, cos, ALU.mult)
                            link(tt(t[3], x1, sin, ALU.mult))
                            tt(dst[:, :, 0, :], t[0], t[1], ALU.subtract)
                            tt(dst[:, :, 1, :], t[2], t[3], ALU.add).then_inc(S["od_qk_roped"], 1)
                if name == "diff":
                    wait_x(pool, name)
                    pool.dma_start(df_flip[:, :], A["c_flip"]).then_inc(S["df_landed"], 16)
                    pool.memset(df_qT[64:128, 0, :, :], 0.0).then_inc(S["df_cleared"], 1)
                    pool.memset(df_qT[0:64, 1, :, :], 0.0).then_inc(S["df_cleared"], 1)
                    for hd in range(DIFF_HEADS):
                        if hd >= 2:
                            pool.wait_ge(S["df_scores"], MT * (hd - 1))
                        src = bass.AP(rel_scratch.tensor, 2 * hd * RELN, [[1, P], [RELN, 2], [1, SEQ]])
                        pool.dma_start(df_b[:, hd % 2, :, :], src).then_inc(S[f"df_bias{hd % 2}"], 16)
                if name.startswith("ple"):
                    wait_x(pool, name)
                    pool.dma_start(pl_p[:, :, :], A["p_2"][int(name[3])].rearrange("b (m p) c -> p (b m) c", p=P)
                                   ).then_inc(S["pl_landed"], 16)
                if name == "ssm":
                    wait_x(pool, name)
                    pool.wait_ge(S["sm_blocks"], 1)
                    pool.dma_start(sm_bg[:, :], spread(A["ssm_b_glu_2"][0], 2 * D)).then_inc(S["sm_bias"], 16)
                if name in ROW_GAINS:
                    row_gain(name)
                if name == "ssm":
                    run_ssm()

        @with_block.tensor
        def _(pe):
            mm = nc.tensor.matmul

            def unit(u, b, lhs_hi, lhs_lo, i=0, per=0, per_b=0, da=0, dd=0):
                _, k, kn, _, cn = units[u]
                if k == 0 and b >= 2:
                    if acts[b - 1]:
                        pe.wait_ge(S["acc_act"], acts[b - 1] + da * i)
                    if dves[b - 1]:
                        pe.wait_ge(S["acc_dve"], dves[b - 1] + dd * i)
                pe.wait_ge(S["w_split"], u + 1 + per * i)
                first_u = u if k == 0 else u - k_at(u)
                last = u + 1 == len(units) or units[u + 1][1] == 0
                for kk in range(kn):
                    hi, lo = slot(w_hi, u)[:, kk, :], slot(w_lo, u)[:, kk, :]
                    for m in range(MT):
                        o = acc[:, 2 * (b % 2) + m, 0:cn]
                        toks = slice(m * P, (m + 1) * P)
                        end = last and kk == kn - 1
                        mm(o, lhs_hi[:, k + kk, toks], hi, start=(k + kk == 0), stop=False)
                        mm(o, lhs_hi[:, k + kk, toks], lo, start=False, stop=False)
                        ins = mm(o, lhs_lo[:, k + kk, toks], hi, start=False, stop=end)
                ins.then_inc(S["unit_used"], 1)

            def k_at(u):
                n = 0
                while units[u - n][1]:
                    n += 1
                return n

            def turns_early(name):
                if follower(name):
                    for t in turns_of_x(follower(name))[0:2]:
                        t()

            def linear(name, lhs_hi, lhs_lo, tg_need, turns=(), first_turns=True, before_last=None, between=None):
                u, b = first[name]
                kn, cols, a, d = LINEAR[name]
                blocks = [v for v in range(u, u + len(units)) if v < len(units) and units[v][0] == name and units[v][1] == 0]
                n = len(k_groups(kn))

                def one(u, b, need, i=0, per=0, per_b=0, da=0, dd=0):
                    for v in range(n):
                        if between:
                            between(b - first[name][1], v)
                        if before_last and u + v + 1 == blocks[-1] + n:
                            before_last()
                        if need:
                            if v or first_turns:
                                turns_before(v, turns)
                            pe.wait_ge(S["tp_lo"], tg_need[v])
                        unit(u + v, b, lhs_hi, lhs_lo, i, per, per_b, da, dd)

                full = sum(units[v][4] == CB for v in blocks)
                loops = (full - 2) // 2 if full > 2 else 0
                for v in range(2):
                    one(u + v * n, b + v, v == 0)
                if loops:
                    with nc.tensor.Fori(0, loops) as i:
                        for v in range(2):
                            one(u + (2 + v) * n, b + 2 + v, False, i, 2 * n, 2, 2 * a, 2 * d)
                for v in range(2 + 2 * loops, len(blocks)):
                    one(u + v * n, b + v, False)

            def turn(dst, src, n=P):
                return nc.tensor.transpose(dst, src, ident[0:n, 0:n])

            def turn_pair(tg, i, per, src, ready):
                ready()
                if tg >= 2:
                    pe.wait_ge(S["tp_lo"], tg - 1 + per * i)
                for j in range(2):
                    for m in range(MT):
                        ins = turn(tp[:, tg % 2, j * SEQ + m * P:j * SEQ + (m + 1) * P], src(j, m))
                ins.then_inc(S["tp_full"], 1)

            def turns_of(tg, src, ready):
                def one(kp):
                    return lambda: turn_pair(tg + kp, 0, 0, lambda j, m: src[:, m, (2 * kp + j) * P:(2 * kp + j + 1) * P],
                                             lambda: ready(kp))
                return [one(kp) for kp in range(src.shape[2] // (2 * P))]

            def turns_of_x(name):
                return turns_of(stage[name]["tg"], x, lambda kp: wait_x(pe, name, kp // 2))

            def turns_before(v, turns):
                for t in turns[0:2] if v == 0 else turns[v + 1:v + 2]:
                    t()

            def setup_rest():
                pe.wait_ge(S["gain0_copied"], 1)
                pe.wait_ge(S["gains_landed"], 16 * 7)
                turn(ms[:, 0, 0:P], gain_rows[:, 0, :])
                turn(ms[:, 0, P:GAIN_ROWS], gain_rows[0:GAIN_ROWS - P, 1, :], GAIN_ROWS - P).then_inc(S["gains_turned"], 1)
                pe.wait_ge(S["setup_landed"], 16 * 5)
                mm(ms[0:2 * DIFF_HEADS, 1, 0:RELN], rel_b[:, :], hot[:, :], start=True, stop=True)
                pe.wait_ge(S["sm_params"], 1)
                for r in range(4):
                    ins = turn(ms[:, 1, RELN + r * NJ:RELN + (r + 1) * NJ], sm_rows[:, r, :], NJ)
                ins.then_inc(S["rel_done"], 1)

            def ffn(name):
                st = stage[name]
                tg, nf = st["tg"], st["nf"]
                u0, b0 = first[name]
                n = DK // 2
                turns = turns_of_x(name)

                def turn_h(fb, i=0):
                    count = dves[b0 + fb + 1]
                    turn_pair(tg + 4 + fb, i, 2, lambda j, m: h[:, fb % 2, m, j * P:(j + 1) * P],
                              lambda: pe.wait_ge(S["acc_dve"], count + 2 * MT * i))

                for v in range(n):
                    if v or not is_follower(name):
                        turns_before(v, turns)
                    pe.wait_ge(S["tp_lo"], tg + v + 1)
                    unit(u0 + v, b0, xT_hi, xT_lo)
                with nc.tensor.Fori(0, (NFB - 1) // 2) as i:
                    for j in range(2):
                        fb = 1 + j
                        for v in range(n):
                            if v == 2:
                                turn_h(fb - 1, i)
                            unit(u0 + fb * n + v, b0 + fb, xT_hi, xT_lo, i, 2 * n, 2, 2 * MT, 2 * MT)
                u1, b1 = u0 + NFB * n, b0 + NFB
                per_cb = len(k_groups(FK))
                for cb in range(DB):
                    if cb and name == STAGES[0]:
                        setup_rest()
                    for v in range(per_cb):
                        if cb == DB - 1 and v == per_cb - 1:
                            turns_early(name)
                        if cb == 0:
                            if v == 1:
                                turn_h(NFB - 1)
                            k_last = units[u1 + v][1] + units[u1 + v][2] - 1
                            pe.wait_ge(S["tp_lo"], tg + 4 + k_last // 2 + 1)
                        unit(u1 + cb * per_cb + v, b1 + cb, hT_hi, hT_lo)

            def emptied(b):
                pe.wait_ge(S["acc_act"], acts[b])
                pe.wait_ge(S["acc_dve"], dves[b])

            def even(name):
                st = stage[name]
                tg = st["tg"]
                linear("even_in", xT_hi, xT_lo, [tg + v + 1 for v in range(4)], turns_of_x(name),
                       first_turns=not is_follower(name))
                emptied(first["even_in"][1] + 5)
                pe.wait_ge(S["ev_landed"], 96)
                for g in range(4):
                    for t in range(MT):
                        ins = mm(acc[:, g // 2, (g % 2) * SEQ:(g % 2 + 1) * SEQ],
                                 ev[:, t, U_AT + g * P:U_AT + (g + 1) * P], ev_pw[:, g, t, :],
                                 start=(t == 0), stop=(t == MT - 1))
                    if g % 2:
                        ins.then_inc(S["ev_pooled"], 1)
                for m in range(MT):
                    ins = turn(ms[0:GATE_RANK, 0, m * P:(m + 1) * P], ev[:, m, LR_AT:LR_AT + GATE_RANK])
                ins.then_inc(S["ev_lr_turned"], 1)
                pe.wait_ge(S["ev_lr_copied"], 1)
                for m in range(MT):
                    ins = mm(ms[:, 1, m * GLA_QK:(m + 1) * GLA_QK], ev_lrT[:, m * P:(m + 1) * P], ev_gw[:, :],
                             start=True, stop=True)
                ins.then_inc(S["ev_gated"], 1)
                for gp in range(2):
                    pe.wait_ge(S["ev_pool_copied"], gp + 1)
                    pe.wait_ge(S["tp_lo"], tg + 4 + gp - 1)
                    for j in range(2):
                        g = 2 * gp + j
                        ins = mm(tp[:, (tg + 4 + gp) % 2, j * SEQ:(j + 1) * SEQ], ev_pm[:, g, :], ev_pT[:, g, :],
                                 start=True, stop=True)
                    ins.then_inc(S["tp_full"], 1)
                pe.wait_ge(S["ev_decays"], 1)
                for f in range(3):
                    for m in range(MT):
                        ins = mm(acc[:, f, m * GLA_QK:(m + 1) * GLA_QK], ev_c[:, f * P:(f + 1) * P], ev_la[:, m, :],
                                 start=True, stop=True)
                    ins.then_inc(S["ev_summed"], 1)
                for hp in range(2):
                    for m in range(MT):
                        ins = mm(ms[:, 0, hp * 4 + 2 * m:hp * 4 + 2 * m + 2], ev_la[:, m, hp * P:(hp + 1) * P],
                                 ev_c[:, 3 * P:3 * P + 2], start=True, stop=True)
                ins.then_inc(S["ev_summed"], 1)
                for f in range(3):
                    pe.wait_ge(S["ev_scaled"], f + 1)
                    pe.wait_ge(S["ev_exp"], (2, 3, 4)[f])
                    for hp in range(2):
                        for m in range(MT):
                            ins = turn(acc[:, f, hp * SEQ + m * P:hp * SEQ + (m + 1) * P],
                                       ev_s[:, f, m, hp * P:(hp + 1) * P])
                    ins.then_inc(S["ev_turned"], 1)
                pe.wait_ge(S["ev_scaled"], 4)
                for hd in range(GLA_HEADS):
                    half = slice((hd % 2) * 64, (hd % 2) * 64 + 64)
                    for c in range(3):
                        rows = slice((c % 2) * 64, (c % 2) * 64 + 64)
                        ins = mm(state_part(hd // 2, c)[half, :], ev_s[rows, 3, c // 2, hd * 64:(hd + 1) * 64],
                                 ev[rows, c // 2, V_AT + hd * P:V_AT + (hd + 1) * P], start=True, stop=True,
                                 skip_group_check=True)
                ins.then_inc(S["ev_added"], 1)
                pe.wait_ge(S["ev_T_copied"], 2)
                for m in range(MT):
                    for hd in range(GLA_HEADS):
                        half = slice((hd % 2) * 64, (hd % 2) * 64 + 64)
                        for c in range(2):
                            toks = slice(m * P + c * 64, m * P + c * 64 + 64)
                            at = of_head(m, hd) + c * 64
                            ins = mm(acc[c * 64:c * 64 + 64, hd % 2, at:at + 64],
                                     ev_T[half, 1, hd // 2, toks], ev_T[half, 0, hd // 2, toks],
                                     start=True, stop=True, skip_group_check=True)
                ins.then_inc(S["ev_scores"], 1)
                pe.wait_ge(S["ev_T_copied"], 3)
                pe.wait_ge(S["ev_state"], 6)
                pe.wait_ge(S["ev_masked"], 4)
                for m in range(MT):
                    for hd in range(GLA_HEADS):
                        half = slice((hd % 2) * 64, (hd % 2) * 64 + 64)
                        o = acc[:, 2 + hd % 2, of_head(m, hd):of_head(m, hd) + P]
                        ins = mm(o, ev_sc[:, m, hd, :], ev[:, m, V_AT + hd * P:V_AT + (hd + 1) * P],
                                 start=True, stop=False, skip_group_check=True)
                        for c in range(2):
                            if 2 * m + c:
                                ins = mm(o[c * 64:c * 64 + 64, :],
                                         ev_T[half, 2, hd // 2, m * P + c * 64:m * P + c * 64 + 64],
                                         ev_st[half, 2 * m + c - 1, hd // 2, :],
                                         start=False, stop=True, skip_group_check=True)
                ins.then_inc(S["ev_out"], 1)
                linear("even_out", xT_hi, xT_lo, [tg + 7] + [tg + 8] * 3,
                       turns_of(tg + 6, ev_o, lambda kp: pe.wait_ge(S["ev_normed"], MT * GLA_HEADS)),
                       before_last=lambda: turns_early(name))

            def odd(name):
                st = stage[name]
                tg = st["tg"]
                def turned(f):
                    if f >= 6:
                        pe.wait_ge(S["od_T_copied"], f - 3)
                    for j in range(2):
                        for m in range(MT):
                            at = slice(j * SEQ + m * P, j * SEQ + (m + 1) * P)
                            if f == 0:
                                ins = turn(ms[:, 0, at], od_ri[:, m, 2 * j:2 * j + 2, :].rearrange("p a b -> p (a b)"))
                            elif f == 1:
                                if j:
                                    continue
                                ins = turn(ms[:, 1, at], od_ri[:, m, 4:6, :].rearrange("p a b -> p (a b)"))
                            elif f == 2:
                                ins = turn(acc[:, 2, at], od_r[:, m, ATT_HEADS + j, :])
                            else:
                                ins = turn(acc[:, f % 4, at], od_r[:, m, 2 * (f - 3) + j, :])
                    ins.then_inc(S["od_turned"], 1)

                def logits(m):
                    n = (m + 1) * P
                    if m:
                        pe.wait_ge(S["od_relu"], 2)
                    else:
                        pe.wait_ge(S["od_T_copied"], 2)
                        pe.wait_ge(S["tp_lo"], tg + 4)
                    for hd in range(IDX_HEADS):
                        half = slice((hd % 2) * 64, (hd % 2) * 64 + 64)
                        ins = mm(tp[:, hd % 2, (hd // 2) * SEQ:(hd // 2) * SEQ + n],
                                 od_qiT[half, hd // 2, m * P:(m + 1) * P], od_kiT[half, 0:n],
                                 start=True, stop=True, skip_group_check=True)
                    ins.then_inc(S["od_logits"], 1)

                def indexer(blk, v):
                    if (blk, v) == (1, 3):
                        pe.wait_ge(S["od_roped"], 1)
                        turned(0)
                        turned(1)
                    if blk == 2 and v in (1, 2):
                        logits(v - 1)

                linear("odd_in", xT_hi, xT_lo, [tg + v + 1 for v in range(4)], turns_of_x(name),
                       first_turns=not is_follower(name), between=indexer)
                emptied(first["odd_in"][1] + 4)
                pe.wait_ge(S["od_qk_roped"], 2 * MT)
                for f in range(2, 7):
                    turned(f)

                def scores(s):
                    hp, m = s // 2, s % 2
                    n = (m + 1) * P
                    if s >= 4:
                        pe.wait_ge(S["od_scored"], 2 * (s - 3))
                    for j in range(2):
                        ins = mm(od_bank(s)[:, j * SEQ:j * SEQ + n], od_qT[:, hp, j, m * P:(m + 1) * P],
                                 od_kT[:, hp // 2, 0:n], start=True, stop=True, skip_group_check=True)
                    ins.then_inc(S["od_scores"], 1)

                def turn_probs(s):
                    m = s % 2
                    pe.wait_ge(S["od_probs"], s + 1)
                    if s >= 2:
                        pe.wait_ge(S["od_pT_copied"], s - 1)
                    for j in range(2):
                        for t in range(m + 1):
                            ins = turn(acc[:, 2 + s % 2, (j * (m + 1) + t) * P:(j * (m + 1) + t + 1) * P],
                                       od_p[:, s % 2, j, t * P:(t + 1) * P])
                    ins.then_inc(S["od_pT_turned"], 1)

                def values(s):
                    hp, m = s // 2, s % 2
                    g = tg + 4 + hp
                    pe.wait_ge(S["od_pT_copied"], s + 1)
                    if m == 0:
                        pe.wait_ge(S["tp_lo"], g - 1)
                    for j in range(2):
                        for t in range(m + 1):
                            ins = mm(tp[:, g % 2, j * SEQ + m * P:j * SEQ + (m + 1) * P],
                                     od[:, t, ATT_V + (hp // 2) * HD:ATT_V + (hp // 2 + 1) * HD],
                                     od_pT[:, s % 2, (j * (m + 1) + t) * P:(j * (m + 1) + t + 1) * P],
                                     start=(t == 0), stop=(t == m), skip_group_check=True)
                    if m:
                        ins.then_inc(S["tp_full"], 1)

                steps = 2 * ATT_HEADS // 2
                pe.wait_ge(S["od_T_copied"], 7)
                pe.wait_ge(S["od_relu"], 4)
                for s in range(3):
                    scores(s)
                for s in range(steps):
                    if s + 3 < steps:
                        scores(s + 3)
                    turn_probs(s)
                    if s:
                        values(s - 1)
                values(steps - 1)
                linear("odd_out", xT_hi, xT_lo, [tg + 4 + v + 1 for v in range(4)],
                       before_last=lambda: turns_early(name))

            def diff(name):
                st = stage[name]
                tg = st["tg"]
                linear("qkv", xT_hi, xT_lo, [tg + v + 1 for v in range(4)], turns_of_x(name),
                       first_turns=not is_follower(name))
                emptied(first["qkv"][1] + 6)
                for k in range(4):
                    for part, copied in enumerate(("df_T_copied", "df_k_copied")):
                        bank = (2 * k + part) % 4
                        if k >= 2:
                            pe.wait_ge(S[copied], k - 1)
                        for j in range(2):
                            hd = 2 * k + j
                            for m in range(MT):
                                ins = turn(acc[:, bank, j * SEQ + m * P:j * SEQ + (m + 1) * P],
                                           df[:, m, part * D + hd * P:part * D + (hd + 1) * P])
                        ins.then_inc(S["df_turned"], 1)

                def scores(s):
                    hd, m = s // 2, s % 2
                    n = (m + 1) * P
                    if s >= 4:
                        pe.wait_ge(S["df_exp"], 2 * (s - 3))
                    if s == 0:
                        pe.wait_ge(S["df_landed"], 16)
                    if m == 0:
                        pe.wait_ge(S[f"df_bias{hd % 2}"], 16 * (hd // 2 + 1))
                    for j in range(2):
                        o = acc[:, s % 4, j * SEQ:j * SEQ + n]
                        mm(o, df_qT[:, j, hd, m * P:(m + 1) * P], df_kT[:, hd, 0:n], start=True, stop=False,
                           skip_group_check=True)
                        ins = mm(o, df_flip[:, :], df_b[:, hd % 2, j, SEQ - n:SEQ], start=False, stop=True,
                                 skip_group_check=True)
                    ins.then_inc(S["df_scores"], 1)

                def turn_probs(s):
                    m = s % 2
                    pe.wait_ge(S["df_probs"], s + 1)
                    if s >= 2:
                        pe.wait_ge(S["df_pT_copied"], s - 1)
                    for t in range(m + 1):
                        ins = turn(tp[:, s % 2, t * P:(t + 1) * P], df_a[:, s % 2, t * P:(t + 1) * P])
                    ins.then_inc(S["df_pT_turned"], 1)

                def values(s):
                    hd, m = s // 2, s % 2
                    pe.wait_ge(S["df_pT_copied"], s + 1)
                    if m == 0 and hd >= 2:
                        pe.wait_ge(S["df_o_copied"], hd - 1)
                    for t in range(m + 1):
                        ins = mm(ms[:, hd % 2, m * P:(m + 1) * P], df_pT[:, s % 2, t * P:(t + 1) * P],
                                 df[:, t, 2 * D + hd * P:2 * D + (hd + 1) * P],
                                 start=(t == 0), stop=(t == m), skip_group_check=True)
                    ins.then_inc(S["df_out"], 1)

                steps = 2 * DIFF_HEADS
                pe.wait_ge(S["df_T_copied"], 4)
                pe.wait_ge(S["df_k_copied"], 4)
                pe.wait_ge(S["df_cleared"], 2)
                ahead = 2
                for s in range(ahead):
                    scores(s)
                for s in range(steps):
                    if s + ahead < steps:
                        scores(s + ahead)
                    turn_probs(s)
                    if s:
                        values(s - 1)
                values(steps - 1)
                linear("w_o", xT_hi, xT_lo, [tg + 4 + v + 1 for v in range(4)],
                       turns_of(tg + 4, df_o, lambda kp: pe.wait_ge(S["df_normed"], kp + 1)))

            def ple(name):
                st = stage[name]
                tg = st["tg"]
                n = name[3]
                linear("gate" + n, xT_hi, xT_lo, [tg + v + 1 for v in range(4)], turns_of_x(name),
                       first_turns=not is_follower(name),
                       before_last=lambda: turn_pair(tg + 4, 0, 0, lambda j, m: pl_p[:, m, j * P:(j + 1) * P],
                                                     lambda: pe.wait_ge(S["pl_landed"], 16 * (int(n) + 1))))
                linear("ple" + n, pl_hi, pl_lo, [tg + 5])

            def ssm(name):
                st = stage[name]
                tg = st["tg"]
                pe.wait_ge(S["sm_blocks"], 1)
                emptied(first["glu"][1])
                for r in range(2):
                    for k in range(DK):
                        if r and k == 0:
                            pe.wait_ge(S["sm_BT_copied"], 2)
                        ins = turn(acc[:, k // 4, (k % 4) * P:(k % 4 + 1) * P], sm_bd[r][:, k * P:(k + 1) * P])
                    ins.then_inc(S["sm_b_turned"], 1)
                    for k in range(DK):
                        if r and k == 0:
                            pe.wait_ge(S["sm_CT_copied"], 4)
                        ins = turn(acc[:, 2 + k // 4, (k % 4) * P:(k % 4 + 1) * P], sm_cd[r][:, k * P:(k + 1) * P])
                    ins.then_inc(S["sm_c_turned"], 1)
                for t in turns_of(tg, y, lambda kp: pe.wait_ge(S["sm_xn"], MT)):
                    t()
                pe.wait_ge(S["tp_lo"], tg + 4)
                pe.wait_ge(S["tp_hi"], tg + 4)
                pe.wait_ge(S["sm_BT_copied"], 4)
                pe.wait_ge(S["sm_CT_copied"], 6)

                def inputs(s):
                    c, jp = divmod(s, NJ // 2)
                    if s >= 4:
                        pe.wait_ge(S["sm_read"], s - 3)
                    for jj, j in enumerate(tiles_of(jp)):
                        rows = slice(32 * (j % 4), 32 * (j % 4) + 32)
                        for r in range(2):
                            ins = mm(acc[:, s % 4, (2 * jj + r) * TC:(2 * jj + r + 1) * TC],
                                     sm_BT[rows, r, j // 4, :], sm_hT[rows, j // 4, c * TC:(c + 1) * TC],
                                     start=True, stop=True, skip_group_check=True,
                                     tile_position=(32 * (j % 4), 0))
                    ins.then_inc(S["sm_bu"], 1)

                def outputs(s):
                    c, jp = divmod(s, NJ // 2)
                    pe.wait_ge(S["sm_states"], s + 1)
                    if jp % 8 == 0 and c:
                        pe.wait_ge(S["sm_y_read"], jp // 8 + 1)
                    for jj, j in enumerate(tiles_of(jp)):
                        k = j // 4
                        o = ms[32 * (j % 4):32 * (j % 4) + 32, k // 4, (k % 4) * TC:(k % 4 + 1) * TC]
                        xa, xb = sm_x[:, s % 2, 0, jj, :, :], sm_x[:, s % 2, 1, jj, :, :]
                        for n, (part, v) in enumerate([(0, xa[:, 0, :]), (2, xb[:, 1, :]), (1, xa[:, 1, :]), (1, xb[:, 0, :])]):
                            ins = mm(o, sm_CT[:, part, j, :], v, start=(n == 0), stop=(n == 3),
                                     skip_group_check=True, tile_position=(0, 32 * (j % 4)))
                    ins.then_inc(S["sm_out"], 1)

                steps = MT * NJ // 2
                ahead = 3
                for s in range(ahead):
                    inputs(s)
                for s in range(steps):
                    if s + ahead < steps:
                        inputs(s + ahead)
                    outputs(s)
                pe.wait_ge(S["sm_g_split"], 4)
                linear("glu", xT_hi, xT_lo, [tg + 4] * 4)

            pe.wait_ge(S["ident_landed"], 16)
            pe.wait_ge(S["gain0_landed"], 16)
            turn(ms[:, 0, 0:16], gain_rows[0:16, 0, :], 16).then_inc(S["gain0_turned"], 1)
            for name in STAGES:
                kind = name.rstrip("0123456789")
                if kind in ("ffna", "ffnb"):
                    ffn(name)
                elif kind != "final":
                    {"even": even, "odd": odd, "diff": diff, "ple": ple, "ssm": ssm}[kind](name)

        @with_block.scalar
        def _(act):
            f = nc.scalar.activation

            def split(u, i=0, per=0):
                if u >= len(units):
                    return
                act.wait_ge(S[f"w_landed{u % RING}"], 32 * (u // RING + 1) + 32 * (per // RING) * i)
                if u >= RING:
                    act.wait_ge(S["unit_used"], u - RING + 1 + per * i)
                f(flat(w_hi, u), flat(raw, u), ACT.Copy).then_inc(S["w_rounded"], 1)

            def pair_hi(tg, dst, i=0, per=0, gains=None, base=0):
                act.wait_ge(S["tp_full"], tg + 1 + per * i)
                bank = tp[:, tg % 2, :]
                if gains is None:
                    f(dst, bank, ACT.Copy).then_inc(S["tp_hi"], 1)
                elif gains == "same":
                    f(dst, bank, ACT.Copy, scale=gT[:, base:base + 1]).then_inc(S["tp_hi"], 1)
                else:
                    for j in range(2):
                        ins = f(dst[:, j * SEQ:(j + 1) * SEQ], bank[:, j * SEQ:(j + 1) * SEQ], ACT.Copy,
                                scale=gT[:, base + j:base + j + 1])
                    ins.then_inc(S["tp_hi"], 1)

            def hi_x(name, pairs=None):
                for kp in pairs or range(2 if is_follower(name) else 0, 4):
                    if name == STAGES[0] and kp:
                        split(kp - 1)
                    if kp >= 2 and held_back(name):
                        split(held_back(name)[kp - 2])
                    pair_hi(stage[name]["tg"] + kp, pair(xT_hi, 2 * kp), gains="each",
                            base=gain_row(name) + 2 * kp)

            def norm_in_front(name):
                st = stage[name]
                n = st["pre"]
                wait_x(act, name)
                for m in range(MT):
                    ins = f(y[:, m, :], x[:, m, :], ACT.Square, scale=D ** -0.5, accum_out=ss[:, n, m, 0:1])
                ins.then_inc(S["ss_ready"], 1)
                act.wait_ge(S["ss_ready"], st["npre"] + 1)
                f(std[:, n, :], ss[:, n, :, 0], ACT.Sqrt, bias=EPS).then_inc(S["std_ready"], 1)

            def norm_behind(name, half):
                st = stage[name]
                act.wait_ge(S["var_ready"], st["npost"] + 1)
                f(std[:, st["post"], :], ss[:, st["post"], :, 0], ACT.Sqrt,
                  scale=4.0 if half else 1.0).then_inc(S["std_ready"], 1)

            warmed = [0]

            def load_root():
                f(warm[:, warmed[0]:warmed[0] + 1], ident[:, 0:1], ACT.Sqrt)
                warmed[0] += 1

            def hi_early(name):
                if follower(name):
                    hi_x(follower(name), (0, 1))

            def linear(name, evac, before_last=None, between=None, end=None, hold=False):
                u, b = first[name]
                kn, cols, _, _ = LINEAR[name]
                n = len(k_groups(kn))
                for blk in range(-(-cols // CB)):
                    for v in range(n):
                        if v == n - 1:
                            if before_last and (blk + 1) * CB >= cols:
                                before_last()
                            evac(blk, b + blk, u + blk * n + n)
                        if end and (blk + 1) * CB >= cols and v == n - 1:
                            end()
                        if hold and (blk + 1) * CB >= cols and v >= n - 2:
                            continue
                        split(u + blk * n + v + RING)
                        if between:
                            between(blk, v)

            def front(dst, nn):
                def evac(blk, b, used):
                    act.wait_ge(S["unit_used"], used)
                    act.wait_ge(S["rstd_ready"], nn + 1)
                    c0, cn = units[used - 1][3:5]
                    f(dst[:, 0, c0:c0 + cn], acc[:, 2 * (b % 2), 0:cn], ACT.Copy,
                      scale=rstd[:, nn, 0:1]).then_inc(S["acc_act"], 1)
                return evac

            def squares_behind(nn):
                def evac(blk, b, used):
                    act.wait_ge(S["unit_used"], used)
                    if blk:
                        act.wait_ge(S["acc_act"], acts[b])
                    for m in range(MT):
                        f(ms[:, m, :], acc[:, 2 * (b % 2) + m, :], ACT.Square, scale=D ** -0.5,
                          accum_out=ss[:, nn, m, blk:blk + 1]).then_inc(S["acc_act"], 1)
                return evac

            def exponents():
                act.wait_ge(S["sm_landed"], 16 * 3)
                f(sm_dt[:, 1, :], sm_dt[:, 0, :], ACT.Exp).then_inc(S["sm_a1"], 1)
                act.wait_ge(S["lam_summed"], 1)
                f(lam_s[:, 2:4], lam_s[:, 0:2], ACT.Exp).then_inc(S["lam_exp"], 1)

            def ssm_rows():
                act.wait_ge(S["sm_v1"], 1)
                f(sm_rows[:, 4, :], sm_rows[:, 2, :], ACT.Exp).then_inc(S["sm_a1"], 1)
                act.wait_ge(S["sm_v1"], 2)
                f(sm_rows[:, 6, :], sm_rows[:, 5, :], ACT.Abs).then_inc(S["sm_a1"], 1)
                act.wait_ge(S["sm_a1"], 3)
                f(sm_rows[:, 8, :], sm_rows[:, 5, :], ACT.Sin).then_inc(S["sm_a1"], 1)
                f(sm_rows[:, 7, :], sm_rows[:, 6, :], ACT.Sin, scale=-1.0, bias=math.pi / 2).then_inc(S["sm_a1"], 1)

            def position_trig():
                act.wait_ge(S["reduced"], 1)
                f(trig[:, 1, :, :], red[:, 0, :, :], ACT.Sin).then_inc(S["trig_ready"], 1)
                f(red[:, 1, :, :], red[:, 0, :, :], ACT.Abs).then_inc(S["trig_abs"], 1)
                act.wait_ge(S["trig_abs"], 1)
                f(trig[:, 0, :, :], red[:, 1, :, :], ACT.Sin, scale=-1.0, bias=math.pi / 2).then_inc(S["trig_ready"], 1)

            def all_gains():
                act.wait_ge(S["gains_turned"], 1)
                f(gT[:, :], ms[:, 0, 0:GAIN_ROWS], ACT.Copy).then_inc(S["gains_copied"], 1)
                act.wait_ge(S["gains_copied"], 1)

            setup_steps = [exponents, ssm_rows, lambda: None, lambda: None, position_trig] + 5 * [lambda: None] + [all_gains]

            def ffn(name):
                st = stage[name]
                tg, nn = st["tg"], st["pre"]
                u0, b0 = first[name]
                behind = st["post"] is not None
                hi_x(name)
                if name == STAGES[0]:
                    split(RING - 1)
                norm_in_front(name)
                act.wait_ge(S["rstd_ready"], nn + 1)

                def silus(fb, i=0):
                    act.wait_ge(S["unit_used"], u0 + 4 * (fb + 1) + 8 * i)
                    if fb:
                        act.wait_ge(S["acc_dve"], dves[b0 + fb] - MT + 2 * MT * i)
                    for m in range(MT):
                        f(silu[:, fb % 2, m, :], acc[:, 2 * ((b0 + fb) % 2) + m, 0:FB], ACT.Silu,
                          scale=rstd[:, nn, m:m + 1]).then_inc(S["acc_act"], 1)

                def turn(fb, i=0, per=0):
                    u = u0 + 4 * fb + RING
                    split(u, i, per)
                    split(u + 1, i, per)
                    if fb:
                        dst = hT_hi[:, bass.ds(2 * (fb - 1) + 4 * i, 2), :] if per else hT_hi[:, 2 * (fb - 1):2 * fb, :]
                        pair_hi(tg + 4 + fb - 1, dst.rearrange("p k t -> p (k t)"), i, 2 if per else 0)
                    split(u + 2, i, per)
                    silus(fb, i)
                    split(u + 3, i, per)

                turn(0)
                with nc.scalar.Fori(0, (NFB - 3) // 2) as i:
                    for j in range(2):
                        turn(1 + j, i, 8)
                turn(NFB - 2)
                turn(NFB - 1)
                u1, b1 = u0 + 4 * NFB, b0 + NFB
                n = len(k_groups(FK))
                for cb in range(DB):
                    for v in range(n):
                        if cb == DB - 1 and v == n - 3:
                            load_root()
                        if cb == 0 and v == 1:
                            pair_hi(tg + 4 + NFB - 1, pair(hT_hi, FK - 2))
                        if v == n - 1 and cb == DB - 1:
                            hi_early(name)
                        if v == n - 1 and behind:
                            squares_behind(st["post"])(cb, b1 + cb, u1 + (cb + 1) * n)
                            if cb == DB - 1:
                                norm_behind(name, True)
                        if cb == DB - 1 and v >= n - 2 and holds_back(name):
                            continue
                        split(u1 + cb * n + v + RING)
                        if name == STAGES[0] and cb * n + v < len(setup_steps):
                            setup_steps[cb * n + v]()
                        if name == "ffnb2" and 4 <= cb * n + v < 12:
                            ssm_trig(cb * n + v - 4)

            def ssm_trig(g):
                js = slice(4 * g, 4 * g + 4)
                act.wait_ge(S["sm_turns"], g + 1)
                f(sm_cos[:, js, :], sm_sin[:, js, :], ACT.Abs).then_inc(S["sm_abs"], 1)
                f(sm_sin[:, js, :], sm_sin[:, js, :], ACT.Sin, scale=SAFE_TURN)
                act.wait_ge(S["sm_abs"], g + 1)
                f(sm_cos[:, js, :], sm_cos[:, js, :], ACT.Sin, scale=-SAFE_TURN, bias=math.pi / 2).then_inc(S["sm_trig"], 1)

            def even(name):
                act.wait_ge(S["rel_stored"], 16)
                st = stage[name]
                tg, nn = st["tg"], st["pre"]
                hi_x(name)
                norm_in_front(name)
                linear("even_in", front(ev, nn))
                b = first["even_in"][1]
                act.wait_ge(S["acc_act"], acts[b + 5])
                act.wait_ge(S["acc_dve"], dves[b + 5])
                for gp in range(2):
                    act.wait_ge(S["ev_pooled"], gp + 1)
                    f(pair(ev_pT, 2 * gp), acc[:, gp, :], ACT.Copy).then_inc(S["ev_pool_copied"], 1)
                act.wait_ge(S["ev_gated"], 1)
                t = ev_t[:, :, :].rearrange("p m c -> p (m c)")
                f(t, ms[:, 1, :], ACT.Abs).then_inc(S["ev_soft"], 1)
                act.wait_ge(S["ev_soft"], 1)
                f(t, t, ACT.Exp, scale=-1.0).then_inc(S["ev_soft"], 1)
                act.wait_ge(S["ev_soft"], 2)
                f(t, t, ACT.Ln, bias=1.0).then_inc(S["ev_soft"], 1)
                for e, (bank, sign) in enumerate([(0, 1.0), (0, -1.0), (1, 1.0), (2, 1.0)]):
                    act.wait_ge(S["ev_summed"], bank + 1)
                    f(ev_e[:, e, :, :].rearrange("p m c -> p (m c)"), acc[:, bank, :], ACT.Exp,
                      scale=sign).then_inc(S["ev_exp"], 1)
                act.wait_ge(S["ev_summed"], 4)
                f(ev_dec[:, :, :].rearrange("p a b -> p (a b)"), ms[:, 0, 0:8], ACT.Exp).then_inc(S["ev_exp"], 1)
                for e in range(3):
                    act.wait_ge(S["ev_turned"], e + 1)
                    f(ev_T[:, e, :, :].rearrange("p h t -> p (h t)"), acc[:, e, :], ACT.Copy).then_inc(S["ev_T_copied"], 1)
                for gp in range(2):
                    pair_hi(tg + 4 + gp, pair(xT_hi, 4 + 2 * gp), gains="each", base=GAIN_AT["pool_scale"] + 2 * gp)
                for m in range(MT):
                    f(ev_g[:, m, :], ev[:, m, G_AT:G_AT + GLA_V], ACT.Silu).then_inc(S["ev_silu"], 1)
                load_root()
                act.wait_ge(S["ev_out"], 1)
                for m in range(MT):
                    for hd in range(GLA_HEADS):
                        n = m * GLA_HEADS + hd
                        ins = f(y[:, 0, n * P:(n + 1) * P], acc[:, 2 + hd % 2, of_head(m, hd):of_head(m, hd) + P], ACT.Square, scale=GLA_DV ** -0.5,
                                accum_out=ev_ss[:, 0, n:n + 1])
                    ins.then_inc(S["ev_squared"], 1)
                act.wait_ge(S["ev_squared"], MT)
                f(ev_ss[:, 1, :], ev_ss[:, 0, :], ACT.Sqrt, bias=EPS).then_inc(S["ev_rooted"], 1)
                for kp in range(2):
                    pair_hi(tg + 6 + kp, pair(xT_hi, 2 * kp))
                linear("even_out", lambda *a: None, lambda: hi_early(name))

            def odd(name):
                st = stage[name]
                tg, nn = st["tg"], st["pre"]
                hi_x(name)
                norm_in_front(name)
                dsts = [od_qiT[:, :, :].rearrange("p a b -> p (a b)"), od_kiT[:, :],
                        od_kT[:, :, :].rearrange("p a b -> p (a b)")] + \
                       [od_qT[:, k, :, :].rearrange("p a b -> p (a b)") for k in range(4)]

                def copy(k):
                    act.wait_ge(S["od_turned"], k + 1)
                    n = dsts[k].shape[1]
                    bank = ms[:, k, 0:n] if k < 2 else acc[:, k % 4, 0:n]
                    f(dsts[k], bank, ACT.Copy).then_inc(S["od_T_copied"], 1)

                def relus(m):
                    act.wait_ge(S["od_logits"], m + 1)
                    n = (m + 1) * P
                    for hp in range(2):
                        f(od_rl[:, m, :, :].rearrange("p (a b) s -> p a b s", b=2)[:, :, hp, 0:n],
                          tp[:, hp, :].rearrange("p (h s) -> p h s", h=2)[:, :, 0:n], ACT.Relu,
                          scale=IDX_DIM ** -0.5 * IDX_HEADS ** -0.5).then_inc(S["od_relu"], 1)

                def indexer(blk, v):
                    if (blk, v) == (1, 2):
                        copy(0)
                        copy(1)
                    if blk == 2 and v in (0, 1):
                        relus(v)

                linear("odd_in", front(od, nn), between=indexer)
                for k in range(2, 7):
                    copy(k)

                def exps(s):
                    m = s % 2
                    n = (m + 1) * P
                    act.wait_ge(S["od_maxed"], s + 1)
                    for j in range(2):
                        f(od_p[:, s % 2, j, 0:n], od_p[:, s % 2, j, 0:n], ACT.Exp,
                          bias=od_mx[:, s, j, 1:2], accum_out=od_mx[:, s, j, 2:3]).then_inc(S["od_exp"], 1)

                def copy_probs(s):
                    n = 2 * (s % 2 + 1) * P
                    act.wait_ge(S["od_pT_turned"], s + 1)
                    f(od_pT[:, s % 2, 0:n], acc[:, 2 + s % 2, 0:n], ACT.Copy).then_inc(S["od_pT_copied"], 1)

                for s in range(8):
                    exps(s)
                    if s:
                        copy_probs(s - 1)
                    if s >= 3 and s % 2:
                        pair_hi(tg + 4 + (s - 3) // 2, pair(xT_hi, s - 3))
                copy_probs(7)
                load_root()
                pair_hi(tg + 7, pair(xT_hi, 6))
                linear("odd_out", lambda *a: None, lambda: hi_early(name))

            def diff(name):
                st = stage[name]
                tg, nn = st["tg"], st["pre"]
                hi_x(name)
                norm_in_front(name)
                linear("qkv", front(df, nn))
                for k in range(4):
                    act.wait_ge(S["df_turned"], 2 * k + 1)
                    for j in range(2):
                        half = slice(64 * j, 64 * j + 64)
                        ins = f(df_qT[half, j, 2 * k:2 * k + 2, :].rearrange("p h t -> p (h t)"), acc[half, 2 * k % 4, :],
                                ACT.Copy)
                    ins.then_inc(S["df_T_copied"], 1)

                def exps(s):
                    m = s % 2
                    n = (m + 1) * P
                    act.wait_ge(S["df_maxed"], s + 1)
                    if s >= 2:
                        act.wait_ge(S["df_probs"], s - 1)
                    for j in range(2):
                        f(df_p[:, s % 2, j, 0:n], acc[:, s % 4, j * SEQ:j * SEQ + n], ACT.Exp, scale=DIFF_DIM ** -0.5,
                          bias=df_mx[:, s, 1, j:j + 1], accum_out=df_mx[:, s, 2, j:j + 1]).then_inc(S["df_exp"], 1)

                def copy_probs(s):
                    n = (s % 2 + 1) * P
                    act.wait_ge(S["df_pT_turned"], s + 1)
                    f(df_pT[:, s % 2, 0:n], tp[:, s % 2, 0:n], ACT.Copy).then_inc(S["df_pT_copied"], 1)

                def squares(hd):
                    act.wait_ge(S["df_out"], 2 * (hd + 1))
                    for m in range(MT):
                        ins = f(y[:, m, hd * P:(hd + 1) * P], ms[:, hd % 2, m * P:(m + 1) * P], ACT.Square, scale=HD ** -0.5,
                                accum_out=df_ss[:, 0, m, hd:hd + 1])
                    ins.then_inc(S["df_squared"], 1)

                for s in range(16):
                    exps(s)
                    if s:
                        copy_probs(s - 1)
                    if s >= 3 and s % 2:
                        squares((s - 3) // 2)
                copy_probs(15)
                load_root()
                squares(7)
                act.wait_ge(S["df_squared"], 8)
                f(df_ss[:, 1, :, :], df_ss[:, 0, :, :], ACT.Sqrt, bias=EPS).then_inc(S["df_rooted"], 1)
                for kp in range(4):
                    pair_hi(tg + 4 + kp, pair(xT_hi, 2 * kp), gains="same", base=GAIN_AT["attn_subln_g_2"])
                linear("w_o", squares_behind(st["post"]), end=lambda: norm_behind(name, False),
                       hold=holds_back(name))

            def ple(name):
                st = stage[name]
                tg, nn, n = st["tg"], st["pre"], name[3]
                hi_x(name)
                norm_in_front(name)

                def gate(blk, b, used):
                    act.wait_ge(S["unit_used"], used)
                    act.wait_ge(S["rstd_ready"], nn + 1)
                    for m in range(MT):
                        f(pl_g[:, m, blk * CB:(blk + 1) * CB], acc[:, 2 * (b % 2) + m, :], ACT.Sigmoid,
                          scale=rstd[:, nn, m:m + 1]).then_inc(S["acc_act"], 1)

                linear("gate" + n, gate, lambda: pair_hi(tg + 4, pair(pl_hi, 0)))

                def squares(blk, b, used):
                    if blk == 0:
                        load_root()
                    if blk:
                        act.wait_ge(S["y_squared"], squared_before(name) + MT * blk)
                    for m in range(MT):
                        act.wait_ge(S["y_gated"], MT * DB * int(n) + MT * blk + m + 1)
                        f(ms[:, m, :], y[:, m, blk * CB:(blk + 1) * CB], ACT.Square, scale=D ** -0.5,
                          accum_out=ss[:, st["post"], m, blk:blk + 1]).then_inc(S["y_squared"], 1)

                u, b = first["ple" + n]
                for blk in range(DB):
                    squares(blk, b + blk, None)
                norm_behind(name, False)
                for blk in range(DB):
                    split(u + blk + RING)

            def ssm(name):
                st = stage[name]
                tg, nn = st["tg"], st["pre"]
                wait_x(act, name)
                f(y[:, 0, :], x[:, 0, :], ACT.Square, scale=D ** -0.5, accum_out=ss[:, nn, 0, 0:1]).then_inc(
                    S["ss_ready"], 1)
                act.wait_ge(S["ss_ready"], st["npre"] + 1)
                act.wait_ge(S["sm_squared"], 1)
                f(std[:, nn, :], ss[:, nn, :, 0], ACT.Sqrt, bias=EPS).then_inc(S["std_ready"], 1)
                act.wait_ge(S["rstd_ready"], nn + 1)
                f(y[:, 0, :], x[:, 0, :], ACT.Copy, scale=rstd[:, nn, 0:1]).then_inc(S["sm_xn"], 1)
                for r in range(2):
                    act.wait_ge(S["sm_b_turned"], r + 1)
                    for hf in range(2):
                        f(sm_BT[:, r, 4 * hf:4 * hf + 4, :].rearrange("p k s -> p (k s)"), acc[:, hf, :],
                          ACT.Copy).then_inc(S["sm_BT_copied"], 1)
                for kp in range(4):
                    act.wait_ge(S["tp_full"], tg + kp + 1)
                    f(sm_hT[:, 2 * kp, :], tp[:, (tg + kp) % 2, 0:SEQ], ACT.Copy,
                      scale=gT[:, gain_row(name) + 2 * kp:gain_row(name) + 2 * kp + 1]).then_inc(S["tp_hi"], 1)
                for q in range(4):
                    c, hf = q // 2, q % 2
                    act.wait_ge(S["sm_y_read"], q + 1)
                    f(sm_y[:, q % 2, :, :], sm_y[:, q % 2, :, :], ACT.Gelu_apprx_tanh).then_inc(S["sm_gelu"], 1)
                    act.wait_ge(S["sm_gelu"], q + 1)
                    f(xT_hi[:, 4 * hf:4 * hf + 4, c * TC:(c + 1) * TC], sm_y[:, q % 2, :, :],
                      ACT.Copy).then_inc(S["sm_g_hi"], 1)

                def evac(blk, b, used):
                    for m in range(MT):
                        if blk < DB:
                            continue
                        cols = slice((blk - DB) * CB, (blk - DB + 1) * CB)
                        act.wait_ge(S["acc_dve"], dves[b] + m + 1)
                        if blk > DB:
                            act.wait_ge(S["y_squared"], squared_before(name) + MT * (blk - DB))
                        f(z2(m), z2(m), ACT.Sigmoid).then_inc(S["sm_sig"], 1)
                        if blk == 2 * DB - 1 and m == MT - 1:
                            load_root()
                        act.wait_ge(S["sm_prod"], MT * (blk - DB) + m + 1)
                        f(ms[:, m, :], y[:, m, cols], ACT.Square, scale=D ** -0.5,
                          accum_out=ss[:, st["post"], m, blk - DB:blk - DB + 1]).then_inc(S["y_squared"], 1)

                linear("glu", evac, end=lambda: norm_behind(name, False),
                       hold=holds_back(name))

            def final(name):
                norm_in_front(name)

            act.wait_ge(S["gain0_turned"], 1)
            f(gT[:, 0:16], ms[:, 0, 0:16], ACT.Copy).then_inc(S["gain0_copied"], 1)
            act.wait_ge(S["gain0_copied"], 1)
            for name in STAGES:
                kind = name.rstrip("0123456789")
                {"ffna": ffn, "ffnb": ffn, "even": even, "odd": odd, "final": final, "diff": diff,
                 "ple": ple, "ssm": ssm}[kind](name)

        @with_block.vector
        def _(dve):
            tt, ts, stt = nc.vector.tensor_tensor, nc.vector.tensor_scalar, nc.vector.scalar_tensor_tensor
            chain = [0]

            def link(ins):
                chain[0] += 1
                ins.then_inc(S["dve_step"], 1)
                dve.wait_ge(S["dve_step"], chain[0])

            def split(u, i=0, per=0):
                if u >= len(units):
                    return
                dve.wait_ge(S["w_rounded"], u + 1 + per * i)
                tt(flat(w_lo, u), flat(raw, u), flat(w_hi, u).bitcast(F32), ALU.subtract).then_inc(S["w_split"], 1)

            def pair_lo(tg, lo, hi, i=0, per=0, gains=None, base=0):
                dve.wait_ge(S["tp_hi"], tg + 1 + per * i)
                bank = tp[:, tg % 2, :]
                hi = hi.bitcast(F32)
                if gains is None:
                    tt(lo, bank, hi, ALU.subtract).then_inc(S["tp_lo"], 1)
                elif gains == "same":
                    stt(lo, bank, gT[:, base:base + 1], hi, ALU.mult, ALU.subtract).then_inc(S["tp_lo"], 1)
                else:
                    for j in range(2):
                        c = slice(j * SEQ, (j + 1) * SEQ)
                        ins = stt(lo[:, c], bank[:, c], gT[:, base + j:base + j + 1], hi[:, c], ALU.mult, ALU.subtract)
                    ins.then_inc(S["tp_lo"], 1)

            def lo_x(name, pairs=None):
                for kp in pairs or range(2 if is_follower(name) else 0, 4):
                    if name == STAGES[0] and kp:
                        split(kp - 1)
                    if kp >= 2 and held_back(name):
                        split(held_back(name)[kp - 2])
                    pair_lo(stage[name]["tg"] + kp, pair(xT_lo, 2 * kp), pair(xT_hi, 2 * kp), gains="each",
                            base=gain_row(name) + 2 * kp)

            def root(nn):
                dve.wait_ge(S["std_ready"], nn + 1)
                nc.vector.reciprocal(rstd[:, nn, :], std[:, nn, :]).then_inc(S["rstd_ready"], 1)

            def lo_early(name):
                if follower(name):
                    lo_x(follower(name), (0, 1))

            def linear(name, evac, before_last=None, between=None, hold=False):
                u, b = first[name]
                kn, cols, _, _ = LINEAR[name]
                n = len(k_groups(kn))
                for blk in range(-(-cols // CB)):
                    for v in range(n):
                        if v == n - 1:
                            if before_last and (blk + 1) * CB >= cols:
                                before_last()
                            evac(blk, b + blk, u + blk * n + n)
                        if hold and (blk + 1) * CB >= cols and v >= n - 2:
                            continue
                        split(u + blk * n + v + RING)
                        if between:
                            between(blk, v)

            def front(dst, nn):
                def evac(blk, b, used):
                    dve.wait_ge(S["unit_used"], used)
                    dve.wait_ge(S["rstd_ready"], nn + 1)
                    c0, cn = units[used - 1][3:5]
                    ts(dst[:, 1, c0:c0 + cn], acc[:, 2 * (b % 2) + 1, 0:cn], rstd[:, nn, 1:2], None,
                       ALU.mult).then_inc(S["acc_dve"], 1)
                return evac

            def add_to_x(scale):
                def evac(blk, b, used):
                    dve.wait_ge(S["unit_used"], used)
                    for m in range(MT):
                        xs = x[:, m, blk * CB:(blk + 1) * CB]
                        stt(xs, acc[:, 2 * (b % 2) + m, :], scale, xs, ALU.mult, ALU.add).then_inc(S["acc_dve"], 1)
                return evac

            def variance(name):
                n = stage[name]["post"]
                stt(ss[:, n, :, 0], ss[:, n, :, 0], EPS, ss[:, n, :, 1], ALU.add, ALU.add).then_inc(S["var_ready"], 1)

            def gained(name):
                g, n = stage[name]["gb"], stage[name]["post"]

                def product(blk, b, m):
                    cols = slice(blk * CB, (blk + 1) * CB)
                    return tt(y[:, m, cols], acc[:, 2 * (b % 2) + m, :], gB[:, g % 2, cols], ALU.mult)

                def add(cb):
                    c = slice(cb * CB, (cb + 1) * CB)
                    for m in range(MT):
                        stt(x[:, m, c], y[:, m, c], rstd[:, n, m:m + 1], x[:, m, c], ALU.mult,
                            ALU.add).then_inc(S["x_upd"], 1)

                def evac(blk, b, used):
                    dve.wait_ge(S[f"gain_landed{g % 2}"], 16 * (g // 2 + 1))
                    if blk < DB - 1:
                        for m in range(MT):
                            dve.wait_ge(S["acc_act"], acts[b] + m + 1)
                            product(blk, b, m).then_inc(S["acc_dve"], 1)
                        return
                    dve.wait_ge(S["acc_act"], acts[b] + MT)
                    variance(name)
                    product(blk, b, 0).then_inc(S["acc_dve"], 1)
                    root(n)
                    dve.wait_ge(S["rstd_ready"], n + 1)
                    add(0)
                    product(blk, b, 1).then_inc(S["acc_dve"], 1)
                    dve.wait_ge(S["acc_dve"], dves[b] + MT)
                    add(1)
                return evac

            def add_normed(name, y=y):
                n = stage[name]["post"]
                root(n)
                dve.wait_ge(S["rstd_ready"], n + 1)
                for cb in range(DB):
                    c = slice(cb * CB, (cb + 1) * CB)
                    for m in range(MT):
                        stt(x[:, m, c], y[:, m, c], rstd[:, n, m:m + 1], x[:, m, c], ALU.mult,
                            ALU.add).then_inc(S["x_upd"], 1)

            def wait_squared(name):
                dve.wait_ge(S["y_squared"], squared_before(name) + 2 * DB)

            def R(k):
                return sm_rows[:, k, :]

            def lambda_sums():
                dve.wait_ge(S["setup_landed"], 16 * 5)
                link(tt(lam_p[:, :, :], lam_v[:, :, 0, :], lam_v[:, :, 1, :], ALU.mult))
                nc.vector.tensor_reduce(lam_s[:, 0:2], lam_p[:, :, :], AX.X, ALU.add).then_inc(S["lam_summed"], 1)

            def ssm_angles():
                dve.wait_ge(S["sm_a1"], 1)
                dt = sm_dt[:, 1, :].unsqueeze(2).to_broadcast([NJ, 2, STATES])
                v3 = lambda k: R(k).rearrange("p (g s) -> p g s", g=2)
                tt(v3(2), v3(0), dt, ALU.mult).then_inc(S["sm_v1"], 1)
                link(tt(v3(3), v3(1), dt, ALU.mult))
                link(ts(R(5), R(3), 1 / (2 * math.pi), ROUND, ALU.mult, ALU.add))
                link(ts(R(5), R(5), ROUND, None, ALU.subtract))
                link(stt(R(12), R(5), -TWO_PI[0], R(3), ALU.mult, ALU.add))
                link(stt(R(12), R(5), -TWO_PI[1], R(12), ALU.mult, ALU.add))
                link(stt(R(5), R(5), -TWO_PI[2], R(12), ALU.mult, ALU.add))
                ts(R(5), R(5), -SAFE_PI, SAFE_PI, ALU.max, ALU.min).then_inc(S["sm_v1"], 1)

            def ssm_factors():
                dve.wait_ge(S["sm_a1"], 5)
                link(tt(R(9), R(4), R(7), ALU.mult))
                link(ts(R(9), R(9), -1.0, None, ALU.add))
                tt(R(10), R(4), R(8), ALU.mult)
                tt(R(11), R(0), R(0), ALU.mult)
                link(tt(R(12), R(1), R(1), ALU.mult))
                link(tt(R(11), R(11), R(12), ALU.add))
                link(nc.vector.reciprocal(R(11), R(11)))
                tt(R(12), R(9), R(0), ALU.mult)
                link(tt(R(13), R(10), R(1), ALU.mult))
                link(tt(R(12), R(12), R(13), ALU.add))
                tt(R(2), R(12), R(11), ALU.mult)
                link(tt(R(13), R(10), R(0), ALU.mult))
                link(tt(R(12), R(9), R(1), ALU.mult))
                link(tt(R(13), R(13), R(12), ALU.subtract))
                tt(R(3), R(13), R(11), ALU.mult)
                ts(R(1), R(5), 1 / (2 * math.pi), None, ALU.mult)
                nc.vector.tensor_copy(R(0), R(4)).then_inc(S["sm_params"], 1)

            def angles():
                dve.wait_ge(S["lam_exp"], 1)
                link(stt(neg_lam[:, :], lam_s[:, 3:4], -LAMBDA_INIT, lam_s[:, 2:3], ALU.add, ALU.subtract))
                link(nc.vector.tensor_copy(pos[:, :], pos_i[:, :]))
                for m in range(MT):
                    ins = ts(ang[:, m, :], inv[:, :], pos[:, m:m + 1], None, ALU.mult)
                link(ins)
                link(ts(turns[:, 0, :, :], ang[:, :, :], 1 / (2 * math.pi), ROUND, ALU.mult, ALU.add))
                link(ts(turns[:, 1, :, :], turns[:, 0, :, :], ROUND, None, ALU.subtract))
                link(stt(red[:, 0, :, :], turns[:, 1, :, :], -TWO_PI[0], ang[:, :, :], ALU.mult, ALU.add))
                link(stt(red[:, 0, :, :], turns[:, 1, :, :], -TWO_PI[1], red[:, 0, :, :], ALU.mult, ALU.add))
                link(stt(red[:, 0, :, :], turns[:, 1, :, :], -TWO_PI[2], red[:, 0, :, :], ALU.mult, ALU.add))
                ts(red[:, 0, :, :], red[:, 0, :, :], -SAFE_PI, SAFE_PI, ALU.max, ALU.min).then_inc(S["reduced"], 1)

            def turned_rows():
                dve.wait_ge(S["rel_done"], 1)
                nc.vector.tensor_copy(rel_v[:, :], ms[0:2 * DIFF_HEADS, 1, 0:RELN]).then_inc(S["rel_copied"], 1)
                link(nc.vector.tensor_copy(sm_par[:, 0:4, :].rearrange("p a b -> p (a b)"), ms[:, 1, RELN:CB]))
                short = 1.5 * 2.0 ** 10
                link(ts(sm_par[:, 4, :], sm_par[:, 1, :], short, None, ALU.add))
                link(ts(sm_par[:, 4, :], sm_par[:, 4, :], short, None, ALU.subtract))
                tt(sm_par[:, 5, :], sm_par[:, 1, :], sm_par[:, 4, :], ALU.subtract).then_inc(S["sm_par_ready"], 1)
                dve.wait_ge(S["gains_copied"], 1)

            setup_steps = [lambda_sums, ssm_angles, ssm_factors, angles] + 6 * [lambda: None] + [turned_rows]

            def ffn(name):
                st = stage[name]
                tg, nn = st["tg"], st["pre"]
                u0, b0 = first[name]
                behind = st["post"] is not None
                lo_x(name)
                if name == STAGES[0]:
                    split(RING - 1)
                root(nn)
                dve.wait_ge(S["rstd_ready"], nn + 1)

                def products(fb, i=0):
                    if fb:
                        dve.wait_ge(S["tp_full"], tg + 4 + fb - 1 + 2 * i)
                    for m in range(MT):
                        dve.wait_ge(S["acc_act"], acts[b0 + fb] + m + 1 + 2 * MT * i)
                        stt(h[:, fb % 2, m, :], acc[:, 2 * ((b0 + fb) % 2) + m, FB:CB], rstd[:, nn, m:m + 1],
                            silu[:, fb % 2, m, :], ALU.mult, ALU.mult).then_inc(S["acc_dve"], 1)

                def turn(fb, i=0, per=0):
                    u = u0 + 4 * fb + RING
                    split(u, i, per)
                    split(u + 1, i, per)
                    if fb:
                        def of(t):
                            part = t[:, bass.ds(2 * (fb - 1) + 4 * i, 2), :] if per else t[:, 2 * (fb - 1):2 * fb, :]
                            return part.rearrange("p k t -> p (k t)")
                        pair_lo(tg + 4 + fb - 1, of(hT_lo), of(hT_hi), i, 2 if per else 0)
                    split(u + 2, i, per)
                    products(fb, i)
                    split(u + 3, i, per)

                turn(0)
                with nc.vector.Fori(0, (NFB - 3) // 2) as i:
                    for j in range(2):
                        turn(1 + j, i, 8)
                turn(NFB - 2)
                turn(NFB - 1)
                u1, b1 = u0 + 4 * NFB, b0 + NFB
                n = len(k_groups(FK))
                for cb in range(DB):
                    for v in range(n):
                        if cb == 0 and v == 1:
                            pair_lo(tg + 4 + NFB - 1, pair(hT_lo, FK - 2), pair(hT_hi, FK - 2))
                        if v == n - 1 and cb == DB - 1:
                            lo_early(name)
                        if v == n - 1:
                            (gained(name) if behind else add_to_x(0.5))(cb, b1 + cb, u1 + (cb + 1) * n)
                        if cb == DB - 1 and v >= n - 2 and holds_back(name):
                            continue
                        split(u1 + cb * n + v + RING)
                        if name == STAGES[0] and cb * n + v < len(setup_steps):
                            setup_steps[cb * n + v]()

            def even(name):
                dve.wait_ge(S["rel_stored"], 16)
                st = stage[name]
                tg, nn = st["tg"], st["pre"]
                lo_x(name)
                root(nn)
                linear("even_in", front(ev, nn))
                b = first["even_in"][1]
                dve.wait_ge(S["acc_act"], acts[b + 5])
                dve.wait_ge(S["acc_dve"], dves[b + 5])
                dve.wait_ge(S["ev_lr_turned"], 1)
                dve.wait_ge(S["ev_cleared"], 2)
                nc.vector.tensor_copy(ev_lrT[0:GATE_RANK, :], ms[0:GATE_RANK, 0, 0:SEQ]).then_inc(S["ev_lr_copied"], 1)
                dve.wait_ge(S["ev_soft"], 3)
                stt(ev_la[:, :, :].rearrange("p m c -> p (m c)"), ms[:, 1, :], 0.0,
                    ev_t[:, :, :].rearrange("p m c -> p (m c)"), ALU.min, ALU.subtract).then_inc(S["ev_decays"], 1)
                for e, (at, scale) in enumerate([(0, GLA_DK ** -0.5), (GLA_QK, 1.0), (0, GLA_DK ** -0.5), (GLA_QK, 1.0)]):
                    dve.wait_ge(S["ev_exp"], e + 1)
                    stt(ev_s[:, e, :, :], ev[:, :, at:at + GLA_QK], scale, ev_e[:, e, :, :], ALU.mult,
                        ALU.mult).then_inc(S["ev_scaled"], 1)
                dve.wait_ge(S["ev_added"], 1)
                dve.wait_ge(S["ev_exp"], 5)
                for c in range(3):
                    if c:
                        dve.wait_ge(S["ev_state"], 2 * c)
                    for hp in range(2):
                        new = state_part(hp, c)
                        if c == 0:
                            ins = nc.vector.tensor_copy(ev_st[:, c, hp, :], new)
                        else:
                            ins = stt(ev_st[:, c, hp, :], ev_st[:, c - 1, hp, :], ev_dec[:, hp, c:c + 1], new,
                                      ALU.mult, ALU.add)
                        ins.then_inc(S["ev_state"], 1)
                dve.wait_ge(S["ev_scores"], 1)
                for odd_heads in range(2):
                    for c in range(2):
                        half = slice(64 * c, 64 * c + 64)
                        nc.vector.copy_predicated(
                            ev_sc[half, :, :, :].rearrange("p m (a b) t -> p (m a) b t", b=2)[:, :, odd_heads, half],
                            ev_keep[half, :].unsqueeze(1).to_broadcast([64, GLA_HEADS, 64]),
                            acc[half, odd_heads, :].rearrange("p (h t) -> p h t", h=GLA_HEADS)[:, :, half],
                        ).then_inc(S["ev_masked"], 1)
                for gp in range(2):
                    pair_lo(tg + 4 + gp, pair(xT_lo, 4 + 2 * gp), pair(xT_hi, 4 + 2 * gp), gains="each",
                            base=GAIN_AT["pool_scale"] + 2 * gp)
                g = st["gb"]
                dve.wait_ge(S[f"gain_landed{g % 2}"], 16 * (g // 2 + 1))
                for m in range(MT):
                    dve.wait_ge(S["ev_silu"], m + 1)
                    ins = tt(ev_g[:, m, :], ev_g[:, m, :], gB[:, g % 2, 0:GLA_V], ALU.mult)
                link(ins)
                dve.wait_ge(S["ev_rooted"], 1)
                link(nc.vector.reciprocal(ev_ss[:, 2, :], ev_ss[:, 1, :]))
                for m in range(MT):
                    for hd in range(GLA_HEADS):
                        c = slice(hd * P, (hd + 1) * P)
                        n = m * GLA_HEADS + hd
                        stt(ev_o[:, m, c], acc[:, 2 + hd % 2, of_head(m, hd):of_head(m, hd) + P], ev_ss[:, 2, n:n + 1], ev_g[:, m, c], ALU.mult,
                            ALU.mult).then_inc(S["ev_normed"], 1)
                for kp in range(2):
                    pair_lo(tg + 6 + kp, pair(xT_lo, 2 * kp), pair(xT_hi, 2 * kp))
                linear("even_out", add_to_x(1.0), lambda: lo_early(name))

            def rope(dst, src, heads, half, at, t):
                def bc(v):
                    return v.unsqueeze(1).to_broadcast([P, heads, half])
                cos, sin = bc(at[0]), bc(at[1])
                x1, x2 = src[:, :, 0, :], src[:, :, 1, :]
                tt(t[0], x1, cos, ALU.mult)
                tt(t[1], x2, sin, ALU.mult)
                tt(t[2], x2, cos, ALU.mult)
                link(tt(t[3], x1, sin, ALU.mult))
                tt(dst[:, :, 0, :], t[0], t[1], ALU.subtract)
                return tt(dst[:, :, 1, :], t[2], t[3], ALU.add)

            def odd(name):
                st = stage[name]
                tg, nn = st["tg"], st["pre"]
                lo_x(name)
                root(nn)
                b = first["odd_in"][1]

                def rope_index():
                    dve.wait_ge(S["acc_act"], acts[b + 1])
                    dve.wait_ge(S["acc_dve"], dves[b + 1])
                    dve.wait_ge(S["trig_ready"], 2)
                    half = IDX_DIM // 2
                    for m in range(MT):
                        ins = rope(od_ri[:, m, 0:5, :].rearrange("p h (a c) -> p h a c", a=2),
                                   od[:, m, ATT_QI:ATT_WI].rearrange("p (h a c) -> p h a c", a=2, c=half), IDX_HEADS + 1,
                                   half, [trig[:, a, m, HD // 2:96] for a in range(2)],
                                   [od_ti[:, a, :, :] for a in range(4)])
                        link(ins)
                        ins = nc.vector.tensor_copy(od_ri[:, m, 5, :], od_ri[:, m, 4, :])
                    ins.then_inc(S["od_roped"], 1)

                def index_scores(m):
                    n = (m + 1) * P
                    sc = od_is[:, m, 0:n]
                    dve.wait_ge(S["od_relu"], 2 * (m + 1))
                    for hd in range(IDX_HEADS):
                        wi = od[:, m, ATT_WI + hd:ATT_WI + hd + 1]
                        if hd == 0:
                            link(ts(sc, od_rl[:, m, hd, 0:n], wi, None, ALU.mult))
                        else:
                            link(stt(sc, od_rl[:, m, hd, 0:n], wi, sc, ALU.mult, ALU.add))
                    dve.wait_ge(S["od_landed"], 16)
                    dve.wait_ge(S["od_cleared"], 2)
                    link(nc.vector.copy_predicated(sc, od_bar[:, m, 0:n], od_fill[:, 0:n]))

                def pick(m, rounds):
                    sc = od_is[:, m, 0:(m + 1) * P]
                    for r in range(rounds):
                        link(nc.vector.max(od_m8[:, :], sc))
                        link(nc.vector.match_replace(sc, od_m8[:, :], sc, PICKED))

                def mask(m):
                    n = (m + 1) * P
                    sc = od_is[:, m, 0:n]
                    link(ts(sc, sc, (PICKED + BARRED) / 2, NEG, ALU.is_ge, ALU.mult))
                    link(nc.vector.copy_predicated(sc, od_bar[:, m, 0:n], od_neg[:, 0:n]))

                rounds = TOPK // 8

                def indexer(blk, v):
                    if (blk, v) == (0, 3):
                        rope_index()
                    if (blk, v) == (2, 1):
                        index_scores(0)
                    if (blk, v) in ((2, 2), (2, 3), (3, 0)):
                        pick(0, rounds // 4)
                    if (blk, v) == (3, 1):
                        pick(0, rounds - 3 * (rounds // 4))
                        mask(0)
                    if (blk, v) == (3, 2):
                        index_scores(1)

                linear("odd_in", front(od, nn), between=indexer)
                pick(1, rounds)
                mask(1)

                def score(s):
                    m = s % 2
                    n = (m + 1) * P
                    dve.wait_ge(S["od_scores"], s + 1)
                    if s >= 2:
                        dve.wait_ge(S["od_pT_turned"], s - 1)
                    for j in range(2):
                        nc.vector.tensor_tensor_reduce(
                            od_p[:, s % 2, j, 0:n], od_bank(s)[:, j * SEQ:j * SEQ + n], od_is[:, m, 0:n],
                            HD ** -0.5, 2 * NEG, ALU.add, ALU.max, od_mx[:, s, j, 0:1]).then_inc(S["od_scored"], 1)
                    dve.wait_ge(S["od_scored"], 2 * (s + 1))
                    ts(od_mx[:, s, :, 1], od_mx[:, s, :, 0], -1.0, None, ALU.mult).then_inc(S["od_maxed"], 1)

                def normalize(s):
                    n = (s % 2 + 1) * P
                    dve.wait_ge(S["od_exp"], 2 * (s + 1))
                    link(nc.vector.reciprocal(od_mx[:, s, :, 3], od_mx[:, s, :, 2]))
                    for j in range(2):
                        ins = ts(od_p[:, s % 2, j, 0:n], od_p[:, s % 2, j, 0:n], od_mx[:, s, j, 3:4], None, ALU.mult)
                    ins.then_inc(S["od_probs"], 1)

                for s in range(8):
                    score(s)
                    if s:
                        normalize(s - 1)
                    if s >= 3 and s % 2:
                        pair_lo(tg + 4 + (s - 3) // 2, pair(xT_lo, s - 3), pair(xT_hi, s - 3))
                normalize(7)
                pair_lo(tg + 7, pair(xT_lo, 6), pair(xT_hi, 6))
                linear("odd_out", add_to_x(1.0), lambda: lo_early(name))

            def diff(name):
                st = stage[name]
                tg, nn = st["tg"], st["pre"]
                lo_x(name)
                root(nn)
                linear("qkv", front(df, nn))
                for k in range(4):
                    dve.wait_ge(S["df_turned"], 2 * k + 2)
                    nc.vector.tensor_copy(pair(df_kT, 2 * k), acc[:, (2 * k + 1) % 4, :]).then_inc(S["df_k_copied"], 1)

                def score(s):
                    hd, m = s // 2, s % 2
                    n = (m + 1) * P
                    dve.wait_ge(S["df_scores"], s + 1)
                    link(nc.vector.tensor_reduce(df_mx[:, s, 0, :], acc[:, s % 4, :].rearrange("p (j s) -> p j s", j=2)[:, :, 0:n],
                                                 AX.X, ALU.max))
                    ts(df_mx[:, s, 1, :], df_mx[:, s, 0, :], -DIFF_DIM ** -0.5, None, ALU.mult).then_inc(S["df_maxed"], 1)

                def combine(s):
                    n = (s % 2 + 1) * P
                    dve.wait_ge(S["df_exp"], 2 * (s + 1))
                    if s >= 2:
                        dve.wait_ge(S["df_pT_turned"], s - 1)
                    link(nc.vector.reciprocal(df_mx[:, s, 3, :], df_mx[:, s, 2, :]))
                    link(ts(df_mx[:, s, 4, 0:1], df_mx[:, s, 3, 1:2], neg_lam[:, :], None, ALU.mult))
                    link(ts(df_p[:, s % 2, 1, 0:n], df_p[:, s % 2, 1, 0:n], df_mx[:, s, 4, 0:1], None, ALU.mult))
                    stt(df_a[:, s % 2, 0:n], df_p[:, s % 2, 0, 0:n], df_mx[:, s, 3, 0:1], df_p[:, s % 2, 1, 0:n],
                        ALU.mult, ALU.add).then_inc(S["df_probs"], 1)

                def copy_out(hd):
                    dve.wait_ge(S["df_squared"], hd + 1)
                    nc.vector.tensor_copy(df_o[:, :, hd * P:(hd + 1) * P],
                                          ms[:, hd % 2, 0:SEQ].rearrange("p (m c) -> p m c", m=MT)).then_inc(S["df_o_copied"], 1)

                for s in range(16):
                    score(s)
                    if s:
                        combine(s - 1)
                    if s >= 3 and s % 2:
                        copy_out((s - 3) // 2)
                combine(15)
                copy_out(7)
                dve.wait_ge(S["df_rooted"], 1)
                link(nc.vector.reciprocal(df_ss[:, 2, :, :], df_ss[:, 1, :, :]))
                link(ts(df_ss[:, 2, :, :], df_ss[:, 2, :, :], 1.0 - LAMBDA_INIT, None, ALU.mult))
                for kp in range(4):
                    o = df_o[:, :, 2 * kp * HD:2 * (kp + 1) * HD].rearrange("p m (h c) -> p m h c", c=HD)
                    for m in range(MT):
                        r = df_ss[:, 2, m, 2 * kp:2 * kp + 2].unsqueeze(2).to_broadcast([P, 2, HD])
                        ins = tt(o[:, m, :, :], o[:, m, :, :], r, ALU.mult)
                    ins.then_inc(S["df_normed"], 1)
                for kp in range(4):
                    pair_lo(tg + 4 + kp, pair(xT_lo, 2 * kp), pair(xT_hi, 2 * kp), gains="same",
                            base=GAIN_AT["attn_subln_g_2"])
                linear("w_o", gained(name), hold=holds_back(name))

            def ple(name):
                st = stage[name]
                tg, nn, n = st["tg"], st["pre"], name[3]
                lo_x(name)
                root(nn)
                bg, g = first["gate" + n][1], st["gb"]

                def gained_gate(blk):
                    dve.wait_ge(S["acc_act"], acts[bg + blk + 1])
                    dve.wait_ge(S[f"gain_landed{g % 2}"], 16 * (g // 2 + 1))
                    cols = slice(blk * CB, (blk + 1) * CB)
                    for m in range(MT):
                        ins = tt(pl_gg[:, m, cols], pl_g[:, m, cols], gB[:, g % 2, cols], ALU.mult)
                    link(ins)

                linear("gate" + n, lambda blk, b, used: gained_gate(blk - 1) if blk else None,
                       lambda: pair_lo(tg + 4, pair(pl_lo, 0), pair(pl_hi, 0)))

                def evac(blk, b, used):
                    if blk == 0:
                        gained_gate(DB - 1)
                    dve.wait_ge(S["unit_used"], used)
                    cols = slice(blk * CB, (blk + 1) * CB)
                    for m in range(MT):
                        tt(y[:, m, cols], acc[:, 2 * (b % 2) + m, :], pl_g[:, m, cols], ALU.mult).then_inc(S["y_gated"], 1)
                    if blk == DB - 1:
                        for k in range(DB):
                            c = slice(k * CB, (k + 1) * CB)
                            if k:
                                wait_squared(name)
                                variance(name)
                            for m in range(MT):
                                tt(pl_gg[:, m, c], acc[:, 2 * ((b - blk + k) % 2) + m, :], pl_gg[:, m, c],
                                   ALU.mult).then_inc(S["acc_dve"], 1)
                        add_normed(name, pl_gg)

                u, b = first["ple" + n]
                for blk in range(DB):
                    evac(blk, b + blk, u + blk + 1)
                for blk in range(DB):
                    split(u + blk + RING)

            def ssm(name):
                st = stage[name]
                tg, nn = st["tg"], st["pre"]
                wait_x(dve, name)
                nc.vector.tensor_tensor_reduce(y[:, 1, :], x[:, 1, :], x[:, 1, :], 1.0 / D, 0.0, ALU.mult, ALU.add,
                                               ss[:, nn, 1, 0:1]).then_inc(S["sm_squared"], 1)
                root(nn)
                dve.wait_ge(S["rstd_ready"], nn + 1)
                ts(y[:, 1, :], x[:, 1, :], rstd[:, nn, 1:2], None, ALU.mult).then_inc(S["sm_xn"], 1)
                for r in range(2):
                    dve.wait_ge(S["sm_c_turned"], r + 1)
                    for part, sign in [(1, -1.0)] if r else [(0, 1.0), (2, -1.0)]:
                        for hf in range(2):
                            ts(sm_CT[:, part, 16 * hf:16 * hf + 16, :].rearrange("p k s -> p (k s)"), acc[:, 2 + hf, :],
                               sign, None, ALU.mult).then_inc(S["sm_CT_copied"], 1)
                for kp in range(4):
                    dve.wait_ge(S["tp_hi"], tg + kp + 1)
                    k = 2 * kp + 1
                    ts(sm_hT[:, k, :], tp[:, (tg + kp) % 2, SEQ:CB], gT[:, gain_row(name) + k:gain_row(name) + k + 1],
                       None, ALU.mult).then_inc(S["tp_lo"], 1)
                dve.wait_ge(S["sm_trig"], 8)

                def read_out(q):
                    c, hf = q // 2, q % 2
                    dve.wait_ge(S["sm_out"], 8 * (q + 1))
                    if q >= 2:
                        dve.wait_ge(S["sm_g_split"], q - 1)
                    for k in range(4):
                        d = GAIN_AT["ssm_d_2"] + 4 * hf + k
                        ins = stt(sm_y[:, q % 2, k, :], sm_hT[:, 4 * hf + k, c * TC:(c + 1) * TC], gT[:, d:d + 1],
                                  ms[:, hf, k * TC:(k + 1) * TC], ALU.mult, ALU.add)
                    ins.then_inc(S["sm_y_read"], 1)

                def split_gelu(q):
                    c, hf = q // 2, q % 2
                    dve.wait_ge(S["sm_g_hi"], q + 1)
                    ks, cs = slice(4 * hf, 4 * hf + 4), slice(c * TC, (c + 1) * TC)
                    tt(xT_lo[:, ks, cs], sm_y[:, q % 2, :, :], xT_hi[:, ks, cs].bitcast(F32),
                       ALU.subtract).then_inc(S["sm_g_split"], 1)

                half = NJ // 2

                def table(t, s):
                    js = slice(tiles_of(s % half)[0], tiles_of(s % half)[1] + 1, NJ // DK)
                    return t[:, js, :].unsqueeze(2).to_broadcast([P, 2, 2, TC])

                def frame(s):
                    dve.wait_ge(S["sm_bu"], s + 1)
                    if s >= 2:
                        dve.wait_ge(S["sm_states"], s - 1)
                    bu = acc[:, s % 4, :].rearrange("p (j r t) -> p j r t", j=2, r=2)
                    tt(sm_a[:, s % 2, :, :, :], bu, table(sm_cos, s), ALU.mult)
                    tt(sm_z[:, s % 2, :, :, :], bu, table(sm_sin, s), ALU.mult).then_inc(S["sm_read"], 1)

                frame(0)
                for s in range(MT * half):
                    c, jp = divmod(s, half)
                    dve.wait_ge(S["sm_framed"], s + 1)
                    if c:
                        dve.wait_ge(S["sm_carried"], jp + 1)
                    for jj, j in enumerate(tiles_of(jp)):
                        for r in range(2):
                            ins = nc.vector.tensor_tensor_scan(
                                sm_z[:, s % 2, jj, r, :], sm_par[:, 0, j:j + 1].to_broadcast([P, TC]),
                                sm_a[:, s % 2, jj, r, :], sm_carry[:, j, r:r + 1] if c else 0.0, ALU.mult, ALU.add)
                    ins.then_inc(S["sm_scanned"], 1)
                    if s + 1 < MT * half:
                        frame(s + 1)
                    dve.wait_ge(S["sm_scanned"], s + 1)
                    if s >= 2:
                        dve.wait_ge(S["sm_out"], s - 1)
                        dve.wait_ge(S["sm_carried"], min(s - 1, half))
                    z = sm_z[:, s % 2, :, :, :]
                    tt(sm_x[:, s % 2, 0, :, :, :], z, table(sm_cos, s), ALU.mult)
                    tt(sm_x[:, s % 2, 1, :, :, :], z, table(sm_sin, s), ALU.mult).then_inc(S["sm_states"], 1)
                    if s % 8 == 1 and s > 8:
                        if s >= 16:
                            split_gelu(s // 8 - 2)
                        read_out(s // 8 - 1)
                split_gelu(2)
                read_out(3)
                split_gelu(3)
                dve.wait_ge(S["sm_bias"], 16)
                g = st["gb"]
                dve.wait_ge(S[f"gain_landed{g % 2}"], 16 * (g // 2 + 1))
                sm_branch = sm_x[:, :, :, :, :, :].rearrange("p a b c d t -> p (a b c d t)").rearrange("p (m c) -> p m c", m=MT)

                def evac(blk, b, used):
                    dve.wait_ge(S["unit_used"], used)
                    cols = slice(blk % DB * CB, (blk % DB + 1) * CB)
                    bias = sm_bg[:, blk * CB:(blk + 1) * CB]
                    for m in range(MT):
                        dst = y[:, m, cols] if blk < DB else z2(m)
                        tt(dst, acc[:, 2 * (b % 2) + m, :], bias, ALU.add).then_inc(S["acc_dve"], 1)
                    if blk >= DB:
                        for m in range(MT):
                            dve.wait_ge(S["sm_sig"], MT * (blk - DB) + m + 1)
                            tt(y[:, m, cols], y[:, m, cols], z2(m), ALU.mult).then_inc(S["sm_prod"], 1)
                        dve.wait_ge(S["sm_prod"], MT * (blk - DB + 1))
                        for m in range(MT):
                            ins = tt(sm_branch[:, m, cols], y[:, m, cols], gB[:, g % 2, cols], ALU.mult)
                        link(ins)
                    if blk == 2 * DB - 1:
                        wait_squared(name)
                        variance(name)
                        add_normed(name, sm_branch)

                linear("glu", evac, hold=holds_back(name))

            def final(name):
                st = stage[name]
                n, g = st["pre"], st["gb"]
                root(n)
                dve.wait_ge(S["rstd_ready"], n + 1)
                dve.wait_ge(S[f"gain_landed{g % 2}"], 16 * (g // 2 + 1))
                for cb in range(DB):
                    c = slice(cb * CB, (cb + 1) * CB)
                    for m in range(MT):
                        stt(x[:, m, c], x[:, m, c], rstd[:, n, m:m + 1], gB[:, g % 2, c], ALU.mult,
                            ALU.mult).then_inc(S["x_upd"], 1)

            dve.wait_ge(S["gain0_copied"], 1)
            for name in STAGES:
                kind = name.rstrip("0123456789")
                {"ffna": ffn, "ffnb": ffn, "even": even, "odd": odd, "final": final, "diff": diff,
                 "ple": ple, "ssm": ssm}[kind](name)


def kernel(**inputs):
    import numpy as _np
    import concourse.bacc as _bacc
    from concourse import mybir as _mybir
    from concourse.bass_utils import run_bass_kernel_spmd as _run

    nc = _bacc.Bacc("TRN2", target_bir_lowering=False, num_devices=1)
    arrays, aps = {}, {}
    for name, a in [*inputs.items(), *tables().items()]:
        a = _np.ascontiguousarray(a)
        arrays["in_" + name] = a
        aps[name] = nc.dram_tensor("in_" + name, a.shape, _mybir.dt.from_np(a.dtype), kind="ExternalInput").ap()
    out = nc.dram_tensor("out_0", (1, SEQ, D), F32, kind="ExternalOutput").ap()
    scratch = nc.dram_tensor("rel_scratch", (2 * DIFF_HEADS, RELN), F32, kind="Internal").ap()
    build_program(nc, aps, out, scratch)
    r = _run(nc, [arrays], core_ids=[0])
    return r.results[0]["out_0"]
```
